# Optimizing a Trainium2 kernel written in Bass

```python
import math
import jax, jax.numpy as jnp
from jax import lax
import numpy as np

D_MODEL = 1024
BATCH = 1
SEQ = 128
DEPTH = 1
DEC_BATCH = 1
DEC_SEQ = 512
PAST_LEN = 128

GRID_W = 64
RET_HEADS = 4
RET_DK = 128
RET_DV = 128
RET_CHUNK = 128
RET_W = RET_HEADS * RET_DV
ATT_HEADS = 8
ATT_KV_HEADS = 2
ATT_HEAD_DIM = 64
ATT_BLOCK = 128
ATT_W = ATT_HEADS * ATT_HEAD_DIM
ATT_KV_W = ATT_KV_HEADS * ATT_HEAD_DIM
ROPE_THETA = 10000.0
SSM_CH = 512
SSM_GROUP = 16
SSM_GROUPS = SSM_CH // SSM_GROUP
SSM_STATE = 64
N_EXPERTS = 16
N_EXPERT_GROUPS = 4
EXPERTS_PER_GROUP = N_EXPERTS // N_EXPERT_GROUPS
TOP_K = 2
D_FF = 512
N_MOD = 6
EPS = 1e-6

IN_SPLITS = (RET_HEADS * RET_DK, RET_HEADS * RET_DK, RET_W, RET_W,
             ATT_W, ATT_KV_W, ATT_KV_W, SSM_CH, D_MODEL, D_MODEL, D_MODEL)
IN_COLS = sum(IN_SPLITS)
IN_OFFSETS = tuple(sum(IN_SPLITS[:i + 1]) for i in range(len(IN_SPLITS) - 1))

kernel_name = "hybrid_prefix_ctx_diffusion_step"

def _rms(x, g):
    xf = x.astype(jnp.float32)
    y = xf * lax.rsqrt(jnp.mean(xf * xf, axis=-1, keepdims=True) + EPS)
    return (y * g.astype(jnp.float32)).astype(x.dtype)

def _axial_rope_tables(n_tokens):
    rows = n_tokens // GRID_W
    row = jnp.repeat(jnp.arange(rows, dtype=jnp.float32), GRID_W)
    col = jnp.tile(jnp.arange(GRID_W, dtype=jnp.float32), rows)
    n_freq = ATT_HEAD_DIM // 4
    inv = ROPE_THETA ** (-jnp.arange(n_freq, dtype=jnp.float32) / n_freq)
    ang = jnp.concatenate([row[:, None] * inv, col[:, None] * inv], axis=-1)
    return jnp.cos(ang), jnp.sin(ang)

def _apply_rope(x, cos, sin):
    b, n, h, d = x.shape
    xr = x.reshape(b, n, h, d // 2, 2)
    x0, x1 = xr[..., 0], xr[..., 1]
    c = cos[None, :, None, :]
    s = sin[None, :, None, :]
    out = jnp.stack([x0 * c - x1 * s, x0 * s + x1 * c], axis=-1)
    return out.reshape(b, n, h, d).astype(x.dtype)

def _block_attention(q, k, v):
    b, n, h, d = q.shape
    n_blk = n // ATT_BLOCK
    grp = h // ATT_KV_HEADS
    qb = q.reshape(b, n_blk, ATT_BLOCK, ATT_KV_HEADS, grp, d).transpose(1, 0, 2, 3, 4, 5)
    scale = d ** -0.5

    def one_block(q_blk):
        s = jnp.einsum('bqkgd,bskd->bkgqs', q_blk, k).astype(jnp.float32) * scale
        p = jax.nn.softmax(s, axis=-1).astype(v.dtype)
        return jnp.einsum('bkgqs,bskd->bqkgd', p, v)

    out = lax.map(one_block, qb)
    return out.transpose(1, 0, 2, 3, 4, 5).reshape(b, n, h * d)

def _retention_direction(q, k, v, log_gamma, s0):
    b, n_tok, h, dk = q.shape
    dv = v.shape[-1]
    n_chunk = n_tok // RET_CHUNK
    dt = q.dtype
    lg = log_gamma.astype(jnp.float32)
    pos = jnp.arange(RET_CHUNK, dtype=jnp.float32)
    diff = pos[:, None] - pos[None, :]
    decay_mat = jnp.where(diff[None] >= 0, jnp.exp(lg[:, None, None] * jnp.maximum(diff, 0.0)[None]), 0.0).astype(dt)
    zeta = jnp.exp(lg[:, None] * (RET_CHUNK - 1.0 - pos)[None]).astype(dt)
    xi = jnp.exp(lg[:, None] * (pos + 1.0)[None]).astype(dt)
    chunk_decay = jnp.exp(lg * RET_CHUNK).astype(dt)[None, :, None, None]
    qc = q.reshape(b, n_chunk, RET_CHUNK, h, dk)
    kc = k.reshape(b, n_chunk, RET_CHUNK, h, dk)
    vc = v.reshape(b, n_chunk, RET_CHUNK, h, dv)
    scores = jnp.einsum('bnthd,bnshd->bnhts', qc, kc) * decay_mat
    o_inner = jnp.einsum('bnhts,bnshe->bnthe', scores, vc)
    kv = jnp.einsum('bnshd,bnshe,hs->nbhde', kc, vc, zeta)

    def step(state, kv_n):
        return chunk_decay * state + kv_n, state

    s_final, s_before = lax.scan(step, s0.astype(dt), kv)
    o_cross = jnp.einsum('bnthd,nbhde,ht->bnthe', qc, s_before, xi)
    return (o_inner + o_cross).reshape(b, n_tok, h, dv), s_final

def _linear_combine(x, y):
    return (y[0] * x[0], y[0] * x[1] + y[1])

def _s5_direction(u, a_re, a_im, log_dt, b_c, c_c, s0, reverse):
    lam = lax.complex(a_re.astype(jnp.float32), a_im.astype(jnp.float32))
    step = jnp.exp(log_dt.astype(jnp.float32))[:, None]
    a_bar = jnp.exp(lam * step)
    b_bar = ((a_bar - 1.0) / lam)[:, :, None] * b_c
    bu = jnp.einsum('gpi,blgi->blgp', b_bar, u.astype(jnp.float32))
    edge = -1 if reverse else 0
    bu = bu.at[:, edge].add(a_bar[None] * s0)
    a_seq = jnp.broadcast_to(a_bar, bu.shape)
    _, xs = lax.associative_scan(_linear_combine, (a_seq, bu), axis=1, reverse=reverse)
    y = jnp.einsum('gop,blgp->blgo', c_c, xs).real
    final = xs[:, 0] if reverse else xs[:, -1]
    return y, final

def _moe(h, w_router, b_router, w_gate, w_up, w_down):
    b, n, _ = h.shape
    logits = (h @ w_router).astype(jnp.float32) + b_router.astype(jnp.float32)
    probs = jax.nn.softmax(logits, axis=-1)
    grouped = probs.reshape(b, n, N_EXPERT_GROUPS, EXPERTS_PER_GROUP)
    group_score = jnp.sum(lax.top_k(grouped, TOP_K)[0], axis=-1)
    best = jnp.argmax(group_score, axis=-1)
    in_group = jnp.arange(N_EXPERT_GROUPS) == best[..., None]
    masked = jnp.where(in_group[..., None], grouped, -1.0).reshape(b, n, N_EXPERTS)
    top_v, top_i = lax.top_k(masked, TOP_K)
    wts = top_v / jnp.sum(top_v, axis=-1, keepdims=True)
    combine = jnp.sum(jax.nn.one_hot(top_i, N_EXPERTS, dtype=jnp.float32) * wts[..., None], axis=-2).astype(h.dtype)
    hid = jax.nn.silu(jnp.einsum('bld,edf->blef', h, w_gate)) * jnp.einsum('bld,edf->blef', h, w_up)
    return jnp.einsum('blef,efd->bld', hid * combine[..., None], w_down)

def _layer(x, mod, rope, ctx, p):
    b, n, _ = x.shape
    shift1, scale1, gate1, shift2, scale2, gate2 = jnp.split(mod[:, None, :], N_MOD, axis=-1)
    h = _rms(x, p['norm1_g']) * (1.0 + scale1) + shift1
    rq, rk, rv, rg, aq, ak, av, su, g_ret, g_att, g_ssm = jnp.split(h @ p['w_in'], IN_OFFSETS, axis=-1)

    rq = rq.reshape(b, n, RET_HEADS, RET_DK) * (RET_DK ** -0.5)
    rk = rk.reshape(b, n, RET_HEADS, RET_DK)
    rv = rv.reshape(b, n, RET_HEADS, RET_DV)
    if ctx is None:
        ret_s0 = jnp.zeros((b, 2, RET_HEADS, RET_DK, RET_DV), x.dtype)
        ssm_s0 = jnp.zeros((b, 2, SSM_GROUPS, SSM_STATE), jnp.complex64)
    else:
        ret_s0, ssm_s0 = ctx[2], ctx[3]
    o_f, ret_f = _retention_direction(rq, rk, rv, p['ret_lg_f'], ret_s0[:, 0])
    o_b, ret_b = _retention_direction(jnp.flip(rq, 1), jnp.flip(rk, 1), jnp.flip(rv, 1), p['ret_lg_b'], ret_s0[:, 1])
    ro = _rms(o_f + jnp.flip(o_b, 1), p['ret_norm_g'].reshape(RET_HEADS, RET_DV)).reshape(b, n, RET_W)
    ret_branch = (ro * jax.nn.silu(rg)) @ p['w_ret_out']

    aq = _rms(aq.reshape(b, n, ATT_HEADS, ATT_HEAD_DIM), p['att_q_norm_g'])
    ak = _rms(ak.reshape(b, n, ATT_KV_HEADS, ATT_HEAD_DIM), p['att_k_norm_g'])
    av = av.reshape(b, n, ATT_KV_HEADS, ATT_HEAD_DIM)
    if rope is None:
        keys, vals = ak, av
    else:
        cos, sin = rope
        aq = _apply_rope(aq, cos, sin)
        keys = jnp.concatenate([_apply_rope(ak, cos, sin), ctx[0].astype(ak.dtype)], axis=1)
        vals = jnp.concatenate([av, ctx[1].astype(av.dtype)], axis=1)
    att_branch = _block_attention(aq, keys, vals) @ p['w_att_out']

    u = su.reshape(b, n, SSM_GROUPS, SSM_GROUP)
    b_c = lax.complex(p['ssm_b_re'].astype(jnp.float32), p['ssm_b_im'].astype(jnp.float32))
    c_c = lax.complex(p['ssm_c_re'].astype(jnp.float32), p['ssm_c_im'].astype(jnp.float32))
    y_f, ssm_f = _s5_direction(u, p['a_re_f'], p['a_im_f'], p['log_dt_f'], b_c, c_c, ssm_s0[:, 0], False)
    y_b, ssm_b = _s5_direction(u, p['a_re_b'], p['a_im_b'], p['log_dt_b'], b_c, c_c, ssm_s0[:, 1], True)
    y = (y_f + y_b).astype(x.dtype) + p['ssm_d'].reshape(SSM_GROUPS, SSM_GROUP) * u
    y = jax.nn.gelu(y.reshape(b, n, SSM_CH))
    glu_a, glu_b = jnp.split(y @ p['w_glu'], 2, axis=-1)
    ssm_branch = glu_a * jax.nn.sigmoid(glu_b)

    merged = (jax.nn.sigmoid(g_ret) * ret_branch + jax.nn.sigmoid(g_att) * att_branch
              + jax.nn.sigmoid(g_ssm) * ssm_branch)
    x = x + gate1 * (merged @ p['w_out'])

    h2 = _rms(x, p['norm2_g']) * (1.0 + scale2) + shift2
    x = x + gate2 * _moe(h2, p['w_router'], p['b_router'], p['w_gate'], p['w_up'], p['w_down'])

    if ctx is None:
        return x, (ak, av, jnp.stack([ret_f, ret_b], axis=1), jnp.stack([ssm_f, ssm_b], axis=1))
    return x, None

def setup_inputs(seed: int = 0) -> dict:
    key = jax.random.key(seed)
    ks = iter(jax.random.split(key, 48))
    f32 = jnp.float32
    D = D_MODEL
    G, P, I = SSM_GROUPS, SSM_STATE, SSM_GROUP

    def nrm(shape, scale=1.0):
        return jax.random.normal(next(ks), shape, f32) * scale

    ret_base = jnp.log(1.0 - 2.0 ** (-5.0 - jnp.arange(RET_HEADS, dtype=f32)))
    a_im_base = jnp.pi * jnp.arange(P, dtype=f32)
    inp = {}
    inp['x_prompt'] = nrm((BATCH, SEQ, D))
    inp['x_sample'] = nrm((DEC_BATCH, DEC_SEQ, D))
    inp['c'] = nrm((DEC_BATCH, D))
    inp['cache_attn_k'] = nrm((DEC_BATCH, DEPTH, PAST_LEN, ATT_KV_HEADS, ATT_HEAD_DIM))
    inp['cache_attn_v'] = nrm((DEC_BATCH, DEPTH, PAST_LEN, ATT_KV_HEADS, ATT_HEAD_DIM))
    inp['state_ret'] = nrm((DEC_BATCH, DEPTH, 2, RET_HEADS, RET_DK, RET_DV), 4.0)
    inp['state_ssm_re'] = nrm((DEC_BATCH, DEPTH, 2, G, P), 0.1)
    inp['state_ssm_im'] = nrm((DEC_BATCH, DEPTH, 2, G, P), 0.1)
    inp['c_ctx'] = nrm((D,))
    inp['w_ada'] = nrm((DEPTH, D, N_MOD * D), 0.5 * D ** -0.5)
    inp['b_ada'] = nrm((DEPTH, N_MOD * D), 0.02)
    inp['norm1_g'] = 1.0 + nrm((DEPTH, D), 0.02)
    inp['norm2_g'] = 1.0 + nrm((DEPTH, D), 0.02)
    inp['w_in'] = nrm((DEPTH, D, IN_COLS), D ** -0.5)
    inp['ret_lg_f'] = ret_base[None] * jnp.exp(nrm((DEPTH, RET_HEADS), 0.05))
    inp['ret_lg_b'] = ret_base[None] * jnp.exp(nrm((DEPTH, RET_HEADS), 0.05))
    inp['ret_norm_g'] = 1.0 + nrm((DEPTH, RET_W), 0.02)
    inp['w_ret_out'] = nrm((DEPTH, RET_W, D), RET_W ** -0.5)
    inp['att_q_norm_g'] = 1.0 + nrm((DEPTH, ATT_HEAD_DIM), 0.02)
    inp['att_k_norm_g'] = 1.0 + nrm((DEPTH, ATT_HEAD_DIM), 0.02)
    inp['w_att_out'] = nrm((DEPTH, ATT_W, D), ATT_W ** -0.5)
    inp['a_re_f'] = -0.5 * jnp.exp(nrm((DEPTH, G, P), 0.05))
    inp['a_im_f'] = a_im_base + nrm((DEPTH, G, P), 0.01)
    inp['a_re_b'] = -0.5 * jnp.exp(nrm((DEPTH, G, P), 0.05))
    inp['a_im_b'] = a_im_base + nrm((DEPTH, G, P), 0.01)
    inp['log_dt_f'] = jax.random.uniform(next(ks), (DEPTH, G), f32, math.log(0.001), math.log(0.1))
    inp['log_dt_b'] = jax.random.uniform(next(ks), (DEPTH, G), f32, math.log(0.001), math.log(0.1))
    inp['ssm_b_re'] = nrm((DEPTH, G, P, I), (2 * I) ** -0.5)
    inp['ssm_b_im'] = nrm((DEPTH, G, P, I), (2 * I) ** -0.5)
    inp['ssm_c_re'] = nrm((DEPTH, G, I, P), (2 * P) ** -0.5)
    inp['ssm_c_im'] = nrm((DEPTH, G, I, P), (2 * P) ** -0.5)
    inp['ssm_d'] = nrm((DEPTH, SSM_CH))
    inp['w_glu'] = nrm((DEPTH, SSM_CH, 2 * D), SSM_CH ** -0.5)
    inp['w_out'] = nrm((DEPTH, D, D), D ** -0.5)
    inp['w_router'] = nrm((D, N_EXPERTS), D ** -0.5)
    inp['b_router'] = nrm((N_EXPERTS,), 0.01)
    inp['w_gate'] = nrm((DEPTH, N_EXPERTS, D, D_FF), D ** -0.5)
    inp['w_up'] = nrm((DEPTH, N_EXPERTS, D, D_FF), D ** -0.5)
    inp['w_down'] = nrm((DEPTH, N_EXPERTS, D_FF, D), D_FF ** -0.5)
    inp['final_norm_g'] = 1.0 + nrm((D,), 0.02)
    return inp

def reference(x_prompt, x_sample, c, cache_attn_k, cache_attn_v, state_ret, state_ssm_re, state_ssm_im, c_ctx,
              w_ada, b_ada, norm1_g, norm2_g, w_in, ret_lg_f, ret_lg_b, ret_norm_g, w_ret_out,
              att_q_norm_g, att_k_norm_g, w_att_out, a_re_f, a_im_f, a_re_b, a_im_b, log_dt_f, log_dt_b,
              ssm_b_re, ssm_b_im, ssm_c_re, ssm_c_im, ssm_d, w_glu, w_out, w_router, b_router,
              w_gate, w_up, w_down, final_norm_g):
    def layer_params(l):
        return {'norm1_g': norm1_g[l], 'norm2_g': norm2_g[l], 'w_in': w_in[l],
                'ret_lg_f': ret_lg_f[l], 'ret_lg_b': ret_lg_b[l], 'ret_norm_g': ret_norm_g[l],
                'w_ret_out': w_ret_out[l], 'att_q_norm_g': att_q_norm_g[l], 'att_k_norm_g': att_k_norm_g[l],
                'w_att_out': w_att_out[l], 'a_re_f': a_re_f[l], 'a_im_f': a_im_f[l], 'a_re_b': a_re_b[l],
                'a_im_b': a_im_b[l], 'log_dt_f': log_dt_f[l], 'log_dt_b': log_dt_b[l],
                'ssm_b_re': ssm_b_re[l], 'ssm_b_im': ssm_b_im[l], 'ssm_c_re': ssm_c_re[l], 'ssm_c_im': ssm_c_im[l],
                'ssm_d': ssm_d[l], 'w_glu': w_glu[l], 'w_out': w_out[l],
                'w_router': w_router, 'b_router': b_router,
                'w_gate': w_gate[l], 'w_up': w_up[l], 'w_down': w_down[l]}

    xp = x_prompt
    ks_, vs_, rets_, ssms_ = [], [], [], []
    for l in range(DEPTH):
        mod_ctx = jax.nn.silu(c_ctx)[None] @ w_ada[l] + b_ada[l]
        xp, (k_c, v_c, st_r, st_s) = _layer(xp, mod_ctx, None, None, layer_params(l))
        ks_.append(k_c)
        vs_.append(v_c)
        rets_.append(st_r)
        ssms_.append(st_s)
    y_prompt = _rms(xp, final_norm_g)
    new_cache_attn_k = jnp.stack(ks_, axis=1)
    new_cache_attn_v = jnp.stack(vs_, axis=1)
    new_state_ret = jnp.stack(rets_, axis=1)
    ssm_all = jnp.stack(ssms_, axis=1)
    new_state_ssm_re = jnp.real(ssm_all)
    new_state_ssm_im = jnp.imag(ssm_all)

    rope = _axial_rope_tables(x_sample.shape[1])
    xs = x_sample
    for l in range(DEPTH):
        mod_lat = jax.nn.silu(c) @ w_ada[l] + b_ada[l]
        ssm_ctx = lax.complex(state_ssm_re[:, l].astype(jnp.float32), state_ssm_im[:, l].astype(jnp.float32))
        ctx = (cache_attn_k[:, l], cache_attn_v[:, l], state_ret[:, l], ssm_ctx)
        xs, _ = _layer(xs, mod_lat, rope, ctx, layer_params(l))
    y_sample = _rms(xs, final_norm_g)

    return (y_prompt, y_sample, new_cache_attn_k, new_cache_attn_v, new_state_ret, new_state_ssm_re, new_state_ssm_im)


_drawn_inputs = setup_inputs


def setup_inputs(seed=0):
    import zlib

    import numpy as np

    out = dict(_drawn_inputs(seed))
    spreads = {}
    factors = {'cache_attn_k': 18.164,
     'cache_attn_v': 5.356,
     'state_ssm_re': 3.914,
     'state_ssm_im': 5.045,
     'ret_norm_g': 26.039,
     'att_q_norm_g': 8.0,
     'att_k_norm_g': 7.891,
     'a_re_b': 55.886,
     'ssm_c_re': 3.517,
     'ssm_c_im': 3.636,
     'b_router': 3.137,
     'final_norm_g': 20.791,
     'norm2_g': 3.494}
    for name, (base, spread) in spreads.items():
        noise = np.random.default_rng([zlib.crc32(name.encode()), seed]).standard_normal(out[name].shape)
        drawn = base * np.exp(spread * noise) if base else spread * noise
        out[name] = __import__('jax').numpy.asarray(drawn.astype(out[name].dtype))
    for name, factor in factors.items():
        out[name] = (out[name] * factor).astype(out[name].dtype)
    return out
```

```python
import numpy as np
import concourse.bass as bass
from concourse import mybir
from contextlib import ExitStack

F32 = mybir.dt.float32
I32 = mybir.dt.int32
U32 = mybir.dt.uint32
ALU = mybir.AluOpType
ACT = mybir.ActivationFunctionType
AX = mybir.AxisListType

P = 128
D = 1024
KD = D // P
SAMPLE, PROMPT = 512, 128
T = SAMPLE + PROMPT
NT = T // P
NS = SAMPLE // P
RH, RW = 4, 512
AH, KVH, HD = 8, 2, 64
QK_W = (AH + KVH) * HD
KEYS = SAMPLE + PROMPT
G, PS, GI = 32, 64, 16
GP = G // 2
Q = 8
CS, CP_ = SAMPLE // Q, PROMPT // Q
NC = CS + CP_
SC = CS + 1 + CP_ + 1
NE, NG, EG = 16, 4, 4
FF = 512
CAP = 128
PASSES = T // CAP
EPS = 1e-6
COL_RQ, COL_RK, COL_RV, COL_RG, COL_AQ, COL_KV, COL_SU, COL_G = 0, 512, 1024, 1536, 2048, 2560, 2816, 3328
MAGIC = 12582912.0
LN2_HI, LN2_LO = 0.693359375, -2.12194440e-4
TWO_PI_A, TWO_PI_B = 6.28125, 0.0019350051879882812
TWO_PI_C = float(2 * np.pi - 6.28125 - 0.0019350051879882812)
EXP_C = [1 / 5040., 1 / 720., 1 / 120., 1 / 24., 1 / 6., 0.5, 1.0]


def build(nc, a, STOP=99):
    ctx = ExitStack()
    sem = lambda name: ctx.enter_context(nc.semaphore(name))

    used = [0]

    def sb(name, shape, dt=F32):
        return ctx.enter_context(nc.sbuf_tensor(name, shape, dt))

    ident = sb("ident", [P, P])
    upper = sb("upper", [P, P])
    ones = sb("ones", [P, P])
    sel = sb("sel", [2, 2, P])
    small = sb("small", [P, 256])
    cS = sb("cS", [P, KD, 2])
    wring = sb("wring", [P, 2, KD, 512])
    HT = sb("HT", [P, KD, T])
    REG = sb("REG", [P, 38980])

    class Region:
        def __init__(self, at=0):
            self.at = at

        def take(self, *shape, parts=P, dt=F32):
            n = int(np.prod(shape))
            assert self.at + n <= 38980, self.at + n
            v = REG[0:parts, self.at:self.at + n]
            self.at += n
            if dt is not F32:
                v = v.bitcast(dt)
            if len(shape) > 1:
                names = "abcdef"[:len(shape)]
                v = v.rearrange(f"p ({' '.join(names)}) -> p {' '.join(names)}",
                                **{n_: s for n_, s in zip(names, shape)})
            return v

    r = Region()
    X = r.take(NT, D)
    BC = r.take(4, 2, D)
    XN = r.take(2, D)
    SQ = r.take(D)
    cT = r.take(2, KD, 2)
    modrow = r.take(2, 512, parts=2)
    bias_row = r.take(12, 512, parts=2)
    gain_row = r.take(2, D, parts=2)

    r = Region()
    YT = r.take(4, T)
    r = Region()
    FM = r.take(2, 2, GP, P)
    CPW = r.take(2, 2, GP, 9, GI)
    TOE = r.take(G, P)
    U = r.take(G, NC)
    SY_AT = r.at
    S = r.take(Q * 512)
    V_AT = r.at
    V = r.take(2, 2, GP, SC)
    A8_AT = r.at
    A8 = r.take(GP, SC)
    RT_AT = r.at
    RT = r.take(2, GP, CS + 1)
    PAR = r.take(10, 2 * 8)
    SC_ = [r.take(2, GP) for _ in range(18)]
    SCI = r.take(2, GP, dt=I32)
    SF = r.take(2, 2, GP)
    r = Region()
    TMP4 = [r.take(GP * SC) for _ in range(4)]
    Z = [r.take(GP * SC) for _ in range(2)]
    r = Region(V_AT)
    FP = [r.take(GP, Q, GI) for _ in range(2)]
    FPT = r.take(GP, Q, GI)
    CTMP = Region(V_AT).take(GP, 9, GI)
    KP = Region(V_AT).take(G, 2 * Q - 1, GI, parts=GI)
    SU = Region(V_AT).take(NT, 512)
    SRAW = Region(V_AT).take(Q, G, GI, parts=NC)
    SFO = Region(RT_AT).take(4, P, parts=GP)
    RTT = Region(A8_AT).take(GP * 32)
    r = Region()
    NAT = r.take(10, P, parts=GP)
    CNAT = r.take(2, G, PS, parts=GI)
    LD = r.take(2, 2, parts=GP)
    r = Region(SY_AT)
    CT = r.take(2, GP, GI)
    BN = r.take(2, GP, GI)
    BB = r.take(2, 2, GP, GI)
    PW = r.take(2, 2, 9, GP)
    BBT = r.take(GP, GI)
    PWT = r.take(2 * 4 * GP)
    DT_ = r.take(G, parts=GI)
    DG = r.take(G, GI, parts=GI)
    assert r.at <= V_AT

    r = Region(4 * T)
    RQT = r.take(RH, T)
    RKT = r.take(RH, T)
    RK = r.take(NT, RW)
    RV = r.take(NT, RW)
    RG = r.take(NT, RW)
    AQK = r.take(NT, QK_W)
    AV = r.take(NT, KVH * HD)
    ROT = r.take(4, T)
    ATT = r.take(4, T)
    E4 = r.at
    RQ = r.take(NT, RW)
    r = Region(E4)
    ST = r.take(2, NS, RW)
    DEC = r.take(RH, P)
    XI = r.take(2, RH, P)
    ZETA = r.take(2, RH)
    CD = r.take(2, RH)
    LG = r.take(2, RH)
    DIST = r.take(4, P)
    MASK = r.take(2, P)
    ZPOS = r.take(2)
    RNG = r.take(RW)
    SS = r.take(2, RW)
    QX = r.take(2, 2, RH, P)
    VZ = r.take(2, RW)
    KVO = r.take(2, RW)
    RSS = r.take(3, NT * RH)
    KVT = r.take(RW)
    OALL = RK
    r = Region(E4)
    QTT = r.take(4, T)
    KTT = r.take(KEYS)
    KTP = r.take(P)
    CK = r.take(KVH * HD)
    CV = r.take(KVH * HD)
    PR = r.take(2, KEYS)
    PT = r.take(2, 5 * P)
    AO = r.take(2, RW)
    ROPE = r.take(2, NS, HD)
    QGL = r.take(2, HD)
    QG = r.take(AH + KVH, HD)
    QT1 = r.take(QK_W)
    QT2 = r.take(QK_W)
    QSS = r.take(3, NT * (AH + KVH))
    ASUM = r.take(NT, AH)
    AMAX = r.take(4)

    r = Region(4 * T)
    MER = r.take(NT, D)
    MERT_AT = r.at
    MERT = r.take(KD, T)
    TG = r.take(NT, 512)
    MT1 = r.take(2, 512)
    MT2 = r.take(2, 512)
    assert r.at <= 4 * T + RH * T * 2 + 3 * NT * RW + NT * QK_W + NT * P, "ROT and ATT stay"
    X2 = Region().take(NT, D)
    r = Region(5120 + 4 * 4096)
    BC2 = r.take(4, 2, D)
    modrow2 = r.take(2, 512, parts=2)
    bias2 = r.take(8, 512, parts=2)
    gain2 = r.take(D, parts=2)
    SQ2 = r.take(D)
    assert MERT_AT + KD * T <= 5120 + 4 * 4096
    slots = [wring[:, j] for j in range(2)] + [REG[:, 5120 + 4096 * j:5120 + 4096 * (j + 1)].rearrange("p (k c) -> p k c", k=KD) for j in range(4)]
    WG = [slots[0], slots[3]]
    WU = [slots[1], slots[4]]
    WD = [x.rearrange("p k c -> p (k c)").rearrange("p (k c) -> p k c", k=4) for x in (slots[2], slots[5])]
    HTF = HT[:].rearrange("p k t -> p (k t)")
    ROWS2 = HTF[:, 0:2048].rearrange("p (b c) -> p b c", b=2)
    COLS2 = HTF[:, 2048:4096].rearrange("p (b k t) -> p b k t", b=2, k=KD)
    TH = HTF[:, 4096:4608]
    r = Region(5120 + 4 * 4096 + 8192)
    HID = r.take(2, 512)
    HIDT = r.take(2, 512)
    OUT = r.take(2, D)
    YR = r.take(2, 2, D)
    WR = r.take(KD, NE)
    BR = r.take(NE)
    IOTA = r.take(NE)
    TOK = r.take(NT, dt=I32)
    WP = r.take(2, NT)
    PACE = r.take(2)
    ROUTE = r.take(14, NT)
    CIDX = r.take(NT, 2, dt=I32)
    IDX = r.take(NE, dt=I32)
    TOP_COUNT = r.take(1, dt=I32)
    r = Region(5120 + 4 * 4096 + 8192)
    LOGIT, PROB, TMPR, EQ, M1, M2, MB, RANK = [r.take(NT, NE) for _ in range(8)]
    GH = [r.take(NT, NG) for _ in range(8)]
    ZERO = r.take(NE * T // P, dt=I32)
    COMB_STEPS = 2 * 9 + 4 * NT
    SQ2F = ROWS2[:, 0, :]
    FG = COLS2[:, 0].rearrange("p k t -> p (k t)")

    banks = ctx.enter_context(nc.psum_tensor("banks", [P, 8, 512], F32))

    phase = sem("phase_joined")
    consts_in = sem("consts_in")
    c_in = sem("c_in")
    x_in = sem("x_in")
    rows_in = sem("rows_in")
    w_in0, w_in1 = sem("w_slot0_loaded"), sem("w_slot1_loaded")
    w_used = sem("w_blocks_used")
    full_d, free_d = sem("psum_full_for_vector"), sem("psum_emptied_by_vector")
    full_a, free_a = sem("psum_full_for_scalar"), sem("psum_emptied_by_scalar")
    dve_step, act_step, pool_step = sem("dve_step"), sem("act_step"), sem("pool_step")
    tanh_c, silu_c = sem("tanh_c_ready"), sem("silu_c_ready")
    sq_ready = sem("squares_summed")
    mod_ready = sem("mod_row_ready")
    xn_ready, xn_used = sem("xn_tile_ready"), sem("xn_tile_transposed")
    par_in = sem("s5_parameters_in")
    nat_ready = sem("s5_natural_ready")
    a2d = sem("scalar_result_for_vector")
    d2a = sem("vector_result_for_scalar")
    d2p = sem("vector_result_for_tensor")
    scr = sem("scratch_written")
    scr_in = sem("scratch_read")
    toe_in = sem("toeplitz_copied")
    out_done = sem("outputs_written")
    ret_in = sem("retention_inputs_in")
    ret_exp = sem("decays_ready")
    vz_ready, kv_done = sem("decayed_values_ready"), sem("new_states_ready")
    kvo_ready = sem("context_states_ready")
    sd_ready = sem("decayed_scores_ready")
    ro_gate, ro_ready = sem("retention_gate_tanh"), sem("retention_rows_ready")
    att_in = sem("attention_inputs_in")
    qk_ready = sem("queries_keys_ready")
    kv_out = sem("context_keys_ready")
    s_full, s_max, p_ready = sem("scores_full"), sem("maximum_ready"), sem("probabilities_ready")
    pt_full, pt_ready = sem("probabilities_transposed"), sem("transposed_probabilities_ready")
    o_full, ao_ready, aot_full, aot_ready = sem("attention_out_full"), sem("attention_rows_ready"), sem("attention_rows_transposed"), sem("attention_columns_ready")
    mer_step = sem("gated_tiles_added")
    tg_ready = sem("gate_tanh_ready")
    mer_ready = sem("merged_ready")
    tb_ready, tb_used = sem("glu_tanh_ready"), sem("glu_tanh_used")
    route_in, h2_ready, h2_out, h2t_ready = sem("router_inputs_in"), sem("normed_row_ready"), sem("normed_row_stored"), sem("normed_columns_ready")
    exp_ready, masks_ready, pos_ready, pos_out, zero_ready, zero_out = (sem(n) for n in (
        "router_exponentials", "choice_masks_ready", "positions_ready", "tokens_listed", "zero_ready", "lists_zeroed"))
    idx_in = sem("token_lists_in")
    g_in = [sem("rows_gathered0"), sem("rows_gathered1")]
    wg_in = [sem("gate_weights_in0"), sem("gate_weights_in1")]
    wu_in = [sem("up_weights_in0"), sem("up_weights_in1")]
    wd_in = [sem("down_weights_in0"), sem("down_weights_in1")]
    g_t, gt_d, gt_a = sem("rows_transposed"), sem("columns_by_vector"), sem("columns_by_scalar")
    gate_full, up_full, th_ready, hid_ready = sem("gate_full"), sem("up_full"), sem("gate_tanh"), sem("hidden_ready")
    ht_full, ht_ready, dn0, dn1 = sem("hidden_transposed"), sem("hidden_columns_ready"), sem("down_half0_full"), sem("down_half1_full")
    out_d, out_a = sem("expert_out_by_vector"), sem("expert_out_by_scalar")
    out_wr = [sem("expert_rows_stored0"), sem("expert_rows_stored1")]
    hid_step, comb_step = sem("hidden_step"), sem("combine_step")
    cidx_ready, y_in, combined = sem("row_places_ready"), [sem("expert_rows_in0"), sem("expert_rows_in1")], sem("tiles_combined")
    fin_in, fin_sq, fin_ready = sem("final_gain_in"), sem("final_squares"), sem("final_rows_ready")
    x2_in, x2_ready = sem("residual_in"), sem("residual_ready")

    def engine_tools(eng, step):
        count = [0]

        def done(ins):
            count[0] += 1
            ins.then_inc(step, 1)
            eng.wait_ge(step, count[0])
        return done

    def phase_end(eng, n):
        eng.sem_inc(phase, 1)
        eng.wait_ge(phase, 5 * (n + 1))

    def at_least(eng, s, n):
        if not isinstance(n, int) or n > 0:
            eng.wait_ge(s, n)

    def expert_pipeline(eng, r, begin, end):
        def turn(e):
            last = None if isinstance(e, int) and e == 0 else lambda: end(16 * r + e - 1, 8 * r + i - 1, e - 1, 1)
            begin(16 * r + e, 8 * r + i, e, 0, last)
            begin(16 * r + e + 1, 8 * r + i, e + 1, 1, lambda: end(16 * r + e, 8 * r + i, e, 0))

        for i in range(2):
            turn(2 * i)
        with eng.Fori(2, NE // 2) as i:
            turn(2 * i)
        end(16 * r + 15, 8 * r + 7, 15, 1)

    def all_passes(eng, one_pass):
        one_pass(0)
        most = eng.value_load(TOP_COUNT[0:1, 0:1], min_val=0, max_val=T)
        with eng.If(most > CAP):
            with eng.Fori(1, PASSES) as r:
                one_pass(r)

    class Bank:

        def __init__(self, first, full, free):
            self.first, self.full, self.free, self.k = first, full, free, 0

        def bank(self):
            return banks[:, self.first + self.k % 4, :]

        def open(self, pe):
            if self.k >= 4:
                pe.wait_ge(self.free, self.k - 3)
            return self.bank()

        def close(self, last):
            last.then_inc(self.full, 1)
            self.k += 1

        def take(self, eng):
            eng.wait_ge(self.full, self.k + 1)
            return self.bank()

        def give(self, last):
            last.then_inc(self.free, 1)
            self.k += 1

        def all_emptied(self, pe):
            if self.k:
                pe.wait_ge(self.free, self.k)

    w_ada, w_in = a["w_ada"][0], a["w_in"][0]
    blocks = [(w_ada, D, 512 * n, 512) for n in range(4)]
    blocks += [(w_in, D, COL_SU, 512)]
    blocks += [(w_in, D, c, 512) for c in (COL_RQ, COL_RK, COL_RV, COL_RG, COL_AQ)] + [(w_in, D, COL_KV, 256)]
    for n in range(2):
        blocks += [(w_in, D, COL_G + 512 * n, 512), (a["w_ret_out"][0], 512, 512 * n, 512)]
        blocks += [(w_in, D, COL_G + D + 512 * n, 512), (a["w_att_out"][0], 512, 512 * n, 512)]
        blocks += [(w_in, D, COL_G + 2 * D + 512 * n, 512)]
        blocks += [(a["w_glu"][0], 512, 512 * n, 512), (a["w_glu"][0], 512, D + 512 * n, 512)]
    blocks += [(w_ada, D, 512 * n, 512) for n in range(4, 12)]
    blocks += [(a["w_out"][0], D, 512 * n, 512) for n in range(2)]

    scratch_h2 = nc.dram_tensor("scratch_h2", (T, D), F32).ap()
    scratch_out = nc.dram_tensor("scratch_out", (NE * CAP, D), F32).ap()
    lists = nc.dram_tensor("token_lists", (NE * T, 1), I32).ap()
    scratch_su = nc.dram_tensor("scratch_su", (T, 512), F32).ap()

    KV_ORDER = ((0, 0), (1, 3), (0, 1), (1, 2), (0, 2), (1, 1), (0, 4), (1, 4))
    FA5 = 8 + (16 + NT + 6 + 8 + 8) + (15 + NT) + NT + NT + 2 * 4 * NT + NT

    block = ctx.enter_context(nc.Block())

    @block.sync
    def _(sp):
        n_out = 0
        for t, src in ((ident, "k_ident"), (upper, "k_upper"), (sel, "k_sel")):
            sp.dma_start(t[:], a[src]).then_inc(consts_in, 16)
        sp.dma_start(cT[:, 0, :, 0], a["c"].rearrange("o (k p) -> p (o k)", p=P), allow_slow_non_contiguous=True).then_inc(c_in, 16)
        sp.dma_start(cT[:, 0, :, 1], a["c_ctx"].rearrange("(k p) -> p k", p=P), allow_slow_non_contiguous=True).then_inc(c_in, 16)
        for t in range(NT):
            src = a["x_sample"][0, P * t:P * (t + 1), :] if t < NS else a["x_prompt"][0]
            sp.dma_start(X[:, t, :], src).then_inc(x_in, 16)
        for s in range(2):
            sp.dma_start(bias_row[s:s + 1], a["b_ada"].rearrange("o (n c) -> o n c", n=12)).then_inc(rows_in, 16)
            sp.dma_start(gain_row[s:s + 1, 0, :], a["norm1_g"]).then_inc(rows_in, 16)
            sp.dma_start(gain_row[s:s + 1, 1, :], a["norm2_g"]).then_inc(rows_in, 16)

        for n, (w, rows, c0, cols) in enumerate(blocks):
            if n >= 2:
                sp.wait_ge(w_used, n - 1)
            sp.dma_start(wring[:, n % 2, 0:rows // P, 0:cols],
                         w[0:rows, c0:c0 + cols].rearrange("(k p) c -> p k c", p=P)).then_inc((w_in0, w_in1)[n % 2], 16)
            if n == 4:
                pass
            if n == 3:
                phase_end(sp, 0)
                if STOP <= 0:
                    return
                pair = lambda x: x.rearrange("(g h) p -> g (h p)", h=2)
                for d, (re, im, ld) in enumerate((("a_re_f", "a_im_f", "log_dt_f"), ("a_re_b", "a_im_b", "log_dt_b"))):
                    sp.dma_start(NAT[:, d, :], pair(a[re][0])).then_inc(par_in, 16)
                    sp.dma_start(NAT[:, 2 + d, :], pair(a[im][0])).then_inc(par_in, 16)
                    sp.dma_start(LD[:, d, :], a[ld][0].rearrange("(g h) -> g h", h=2)).then_inc(par_in, 16)
                    sp.dma_start(NAT[:, 6 + d, :], pair(a["state_ssm_re"][0, 0, d])).then_inc(par_in, 16)
                    sp.dma_start(NAT[:, 8 + d, :], pair(a["state_ssm_im"][0, 0, d])).then_inc(par_in, 16)
                for j, (b, c) in enumerate((("ssm_b_re", "ssm_c_re"), ("ssm_b_im", "ssm_c_im"))):
                    for h in range(2):
                        sp.dma_start(BN[64 * h:64 * h + 64, j], a[b][0].rearrange("(g h) p i -> h p g i", h=2)[h]).then_inc(par_in, 16)
                    sp.dma_start(CNAT[:, j], a[c][0].rearrange("g o p -> o g p")).then_inc(par_in, 16)
                sp.dma_start(DT_, a["ssm_d"].rearrange("o (g i) -> i (o g)", i=GI), allow_slow_non_contiguous=True).then_inc(par_in, 16)
            if n == 4:
                sp.wait_ge(d2p, 2)
                for s in range(Q):
                    sp.dma_start(TOE[16 * s:16 * s + 16, :, :],
                                 KP[:, :, 7 - s:15 - s, :].rearrange("i g t o -> i g (t o)")).then_inc(toe_in, 16)
                sp.wait_ge(toe_in, 16 * Q)
                sp.sem_inc(scr_in, 1)
                for t in range(NT):
                    sp.wait_ge(scr, t + 1)
                    sp.dma_start(scratch_su[P * t:P * (t + 1), :], SU[:, t, :]).then_inc(out_done, 16)
                n_out += NT
                sp.wait_ge(out_done, 16 * n_out)
                sp.dma_start(SRAW.rearrange("c s g i -> c (s g i)"), scratch_su.rearrange("(c s) f -> c (s f)", s=Q)).then_inc(scr, 16)
                sp.wait_ge(d2a, 3)
                for j, name in enumerate(("new_re", "new_im")):
                    for d in range(2):
                        sp.dma_start(a[name][0, 0, d].rearrange("(g h) p -> g (h p)", h=2), SFO[:, 2 * j + d, :]).then_inc(out_done, 16)
                n_out += 4
                sp.wait_ge(out_done, 16 * n_out)
                phase_end(sp, 1)
                if STOP <= 1:
                    return
            if n == 10:
                phase_end(sp, 2)
                if STOP <= 2:
                    return
                for d, name in enumerate(("ret_lg_f", "ret_lg_b")):
                    sp.dma_start(LG[:, d, :], a[name].broadcast_to([P, RH])).then_inc(ret_in, 16)
                    sp.dma_start(ST[:, d, 3 * d, :].rearrange("p (h e) -> p h e", h=RH),
                                 a["state_ret"][0, 0, d].rearrange("h p e -> p h e")).then_inc(ret_in, 16)
                sp.dma_start(RNG, a["ret_norm_g"].broadcast_to([P, RW])).then_inc(ret_in, 16)
                sp.dma_start(DIST, a["k_dist"]).then_inc(ret_in, 16)
                sp.dma_start(MASK, a["k_mask"]).then_inc(ret_in, 16)
                sp.dma_start(ZPOS, a["k_zpos"]).then_inc(ret_in, 16)
                for d in range(2):
                    sp.wait_ge(kvo_ready, d + 1)
                    sp.dma_start(a["new_ret"][0, 0, d].rearrange("h p e -> p h e"),
                                 KVO[:, d, :].rearrange("p (h e) -> p h e", h=RH)).then_inc(out_done, 16)
                n_out += 2
                sp.wait_ge(out_done, 16 * n_out)
                phase_end(sp, 3)
                if STOP <= 3:
                    return
                sp.dma_start(CK, a["cache_attn_k"][0, 0].rearrange("t h d -> t (h d)")).then_inc(att_in, 16)
                sp.dma_start(CV, a["cache_attn_v"][0, 0].rearrange("t h d -> t (h d)")).then_inc(att_in, 16)
                sp.dma_start(ROPE, a["k_rope"]).then_inc(att_in, 16)
                sp.dma_start(QGL[:, 0, :], a["att_q_norm_g"].broadcast_to([P, HD])).then_inc(att_in, 16)
                sp.dma_start(QGL[:, 1, :], a["att_k_norm_g"].broadcast_to([P, HD])).then_inc(att_in, 16)
                sp.wait_ge(kv_out, 1)
                sp.dma_start(a["new_k"][0, 0].rearrange("t h d -> t (h d)"), AQK[:, NS, AH * HD:]).then_inc(out_done, 16)
                sp.dma_start(a["new_v"][0, 0].rearrange("t h d -> t (h d)"), AV[:, NS, :]).then_inc(out_done, 16)
                n_out += 2
                sp.wait_ge(out_done, 16 * n_out)
                phase_end(sp, 4)
                if STOP <= 4:
                    return
            if n == 24:
                phase_end(sp, 5)
                if STOP <= 5:
                    return
                for t in range(NT):
                    src = a["x_sample"][0, P * t:P * (t + 1), :] if t < NS else a["x_prompt"][0]
                    sp.dma_start(X2[:, t, :], src).then_inc(x2_in, 16)
                for s in range(2):
                    sp.dma_start(bias2[s:s + 1], a["b_ada"].rearrange("o (n c) -> o n c", n=12)[:, 4:12, :]).then_inc(x2_in, 16)
                    sp.dma_start(gain2[s:s + 1, :], a["norm2_g"]).then_inc(x2_in, 16)
        phase_end(sp, 6)
        if STOP <= 6:
            return

        sp.dma_start(WR, a["w_router"].rearrange("(k p) e -> p k e", p=P)).then_inc(route_in, 16)
        sp.dma_start(BR, a["b_router"].rearrange("(o e) -> o e", o=1).broadcast_to([P, NE])).then_inc(route_in, 16)
        sp.dma_start(IOTA, a["k_iota"]).then_inc(route_in, 16)
        sp.dma_start(TOK, a["k_tok"]).then_inc(route_in, 16)
        sp.wait_ge(zero_ready, 1)
        sp.dma_start(lists.rearrange("(p c) o -> p (c o)", p=P), ZERO).then_inc(zero_out, 16)
        for t in range(NT):
            sp.wait_ge(h2_ready, t + 1)
            sp.dma_start(scratch_h2[P * t:P * t + P, :], ROWS2[:, t % 2, :]).then_inc(h2_out, 16)
            sp.wait_ge(h2_out, 16 * (t + 1))
        phase_end(sp, 7)
        if STOP <= 7:
            return

        def weights_in(n, m, e, b):
            at_least(sp, up_full, n - 1)
            sp.dma_start(WG[b], a["w_gate"][0][e].rearrange("(k p) c -> p k c", p=P)).then_inc(wg_in[b], 16)
            sp.dma_start(WU[b], a["w_up"][0][e].rearrange("(k p) c -> p k c", p=P)).then_inc(wu_in[b], 16)
            at_least(sp, dn1, n - 1)
            sp.dma_start(WD[b], a["w_down"][0][e].rearrange("(k p) c -> p k c", p=P)).then_inc(wd_in[b], 16)

        def sp_pass(r):
            if not isinstance(r, int):
                sp.wait_ge(combined, NT * r)
            for k in range(2):
                sp.dma_start(IDX[:, 8 * k:8 * k + 8], lists.rearrange("(e r) o -> r (e o)", r=T)[bass.ds(CAP * r, CAP), 8 * k:8 * k + 8],
                             allow_slow_non_contiguous=True).then_inc(idx_in, 16)
            for e in range(2):
                weights_in(16 * r + e, 8 * r, e, e)
            with sp.Fori(1, NE // 2) as i:
                for b in range(2):
                    weights_in(16 * r + 2 * i + b, 8 * r + i, 2 * i + b, b)

        all_passes(sp, sp_pass)
        phase_end(sp, 8)
        if STOP <= 8:
            return
        sp.dma_start(FG, a["final_norm_g"].rearrange("(o e) -> o e", o=1).broadcast_to([P, D])).then_inc(fin_in, 16)
        for t in range(NT):
            sp.wait_ge(fin_ready, t + 1)
            dst = a["y_sample"][0, P * t:P * (t + 1), :] if t < NS else a["y_prompt"][0]
            sp.dma_start(dst, X2[:, t, :]).then_inc(out_done, 16)
        n_out += NT
        sp.wait_ge(out_done, 16 * n_out)

    @block.tensor
    def _(pe):
        vec, sca = Bank(0, full_d, free_d), Bank(4, full_a, free_a)
        wcount = [0]
        mm = nc.tensor.matmul

        def all_emptied():
            vec.all_emptied(pe)
            sca.all_emptied(pe)

        def weights():
            n = wcount[0]
            wcount[0] += 1
            pe.wait_ge((w_in0, w_in1)[n % 2], 16 * (n // 2 + 1))
            return wring[:, n % 2]

        def weights_used(bank):
            pe.wait_ge(bank.full, bank.k)
            pe.sem_inc(w_used, 1)

        def ada_block(n, stage_kind):
            w = weights()
            out = vec.open(pe)
            for k in range(KD):
                last = mm(out[0:2, :], cS[:, k, :], w[:, k, :], start=k == 0, stop=k == KD - 1)
            vec.close(last)
            weights_used(vec)
            pe.wait_ge(mod_ready, n + 1)
            for s in range(2):
                out = sca.open(pe)
                row = modrow if n < 4 else modrow2
                sca.close(mm(out, sel[:, s, :], row[:, n % 2, :], start=True, stop=True))

        pe.wait_ge(consts_in, 48)
        pe.wait_ge(silu_c, 1)
        for n in range(4):
            ada_block(n, n)
        for t in range(NT):
            pe.wait_ge(xn_ready, t + 1)
            for half in range(2):
                out = vec.open(pe)
                for j in range(4):
                    k = 4 * half + j
                    last = nc.tensor.transpose(out[:, P * j:P * j + P], XN[:, t % 2, P * k:P * k + P], ident[:])
                vec.close(last)
        phase_end(pe, 0)
        if STOP <= 0:
            return

        pe.wait_ge(par_in, 16 * 17)
        pe.wait_ge(nat_ready, 1)
        out = vec.open(pe)
        for j in range(10):
            last = nc.tensor.transpose(out[:, 16 * j:16 * j + 16], NAT[:, j, :], ident[0:16, 0:16])
        vec.close(last)
        for j in range(2):
            out = vec.open(pe)
            for p in range(GP):
                last = nc.tensor.transpose(out[:, 16 * p:16 * p + 16],
                                           CNAT[:, j, 2 * p:2 * p + 2, :].rearrange("o g p -> o (g p)"), ident[0:16, 0:16])
            vec.close(last)
        for d in range(2):
            pe.wait_ge(d2a, d + 1)
            for j in range(2):
                for q in range(4):
                    out = sca.open(pe)
                    for p in range(4):
                        last = nc.tensor.transpose(out[:, P * p:P * p + P],
                                                   FP[j][:, 4 * q + p].rearrange("p s i -> p (s i)"), ident[:])
                    sca.close(last)
        pe.wait_ge(d2p, 1)
        for d in range(2):
            for q in range(G // 4):
                out = vec.open(pe)
                for j in range(4):
                    h, p = q % 2, 4 * (q // 2) + j
                    hs = slice(64 * h, 64 * h + 64)
                    for c in range(2):
                        last = mm(out[0:GI, P * j:P * j + P], BB[hs, d, c, p, :],
                                  CPW[hs, d, c, p, 0:Q, :].rearrange("p k o -> p (k o)"), start=c == 0, stop=c == 1)
                vec.close(last)
        w = weights()
        for t in range(NT):
            out = sca.open(pe)
            for k in range(KD):
                last = mm(out, HT[:, k, P * t:P * t + P], w[:, k, :], start=k == 0, stop=k == KD - 1)
            sca.close(last)
        weights_used(sca)
        pe.wait_ge(d2p, 3)
        for q in range(6):
            gs = range(6 * q, min(6 * q + 6, G))
            out = sca.open(pe)
            for j, g in enumerate(gs):
                last = nc.tensor.transpose(out[:, NC * j:NC * j + NC], S[0:NC, P * g:P * g + P], ident[0:NC, 0:NC])
            sca.close(last)
        sca.all_emptied(pe)
        for d in range(2):
            for c in range(2):
                for q in range(3):
                    ps = range(6 * q, min(6 * q + 6, GP))
                    out = vec.open(pe)
                    for j, p in enumerate(ps):
                        for h in range(2):
                            last = mm(out[64 * h:64 * h + 64, NC * j:NC * j + NC], FM[:, d, c, p, 64 * h:64 * h + 64],
                                      U[:, 2 * p + h, :], start=True, stop=True)
                    vec.close(last)
        pe.wait_ge(toe_in, 16 * Q)
        pe.wait_ge(d2p, 4)
        for q in range(G // 4):
            out = sca.open(pe)
            for j in range(4):
                h, p = q % 2, 4 * (q // 2) + j
                g = 2 * p + h
                hs = slice(64 * h, 64 * h + 64)
                o = out[0:NC, P * j:P * j + P]
                mm(o, U[:, g, :], TOE[:, g, :], start=True, stop=False)
                for d in range(2):
                    for c in range(2):
                        xin = V[hs, d, c, :, :].rearrange("p a b -> p (a b)")[:, NC * p:NC * p + NC]
                        pw = CPW[hs, d, c, p, 1:Q + 1, :]
                        if d:
                            pw = pw[:, ::-1, :]
                        last = mm(o, xin, pw, start=False, stop=d + c == 2)
            sca.close(last)
        out = vec.open(pe)
        for j in range(4):
            last = mm(out[0:GP, P * j:P * j + P], SF[:, j // 2, j % 2, :], ident[:], start=True, stop=True)
        vec.close(last)
        sca.all_emptied(pe)
        Y = S[0:NC, :].rearrange("c (t f) -> c t f", t=Q)
        for kb in range(4):
            for th in range(2):
                out = sca.open(pe)
                for j in range(4):
                    last = nc.tensor.transpose(out[:, NC * j:NC * j + NC], Y[:, 4 * th + j, P * kb:P * kb + P], ident[0:NC, 0:NC])
                sca.close(last)
        phase_end(pe, 1)
        if STOP <= 1:
            return


        turn = [0]

        def project(lhs, w, kd, cols=512):
            out = (vec, sca)[turn[0] % 2].open(pe)
            for k in range(kd):
                last = mm(out[:, 0:cols], lhs(k), w[:, k, 0:cols], start=k == 0, stop=k == kd - 1)
            (vec, sca)[turn[0] % 2].close(last)
            turn[0] += 1

        def transposes(chan, blocks):
            out = chan.open(pe)
            for j, src in enumerate(blocks):
                last = nc.tensor.transpose(out[:, P * j:P * j + P], src, ident[:])
            chan.close(last)

        for b in range(6):
            w = weights()
            for t in range(NT):
                project(lambda k: HT[:, k, P * t:P * t + P], w, KD, 512 if b < 5 else 256)
            weights_used((vec, sca)[(turn[0] - 1) % 2])
        all_emptied()
        for t in range(NT):
            transposes(sca, [RQ[:, t, P * h:P * h + P] for h in range(RH)])
            transposes(vec, [RK[:, t, P * h:P * h + P] for h in range(RH)])
        phase_end(pe, 2)
        if STOP <= 2:
            return

        for i, (d, t) in enumerate(KV_ORDER):
            pe.wait_ge(vz_ready, i + 1)
            out = vec.open(pe)
            for h in range(RH):
                hs = slice(P * h, P * h + P)
                last = mm(out[:, hs], RK[:, t, hs], VZ[:, i % 2, hs], start=True, stop=True)
            vec.close(last)
        pe.wait_ge(kv_done, len(KV_ORDER))
        for t in range(NT):
            ts_ = slice(P * t, P * t + P)
            out = vec.open(pe)
            for h in range(RH):
                last = mm(out[:, P * h:P * h + P], RKT[:, h, ts_], RQT[:, h, ts_], start=True, stop=True)
            vec.close(last)
            pe.wait_ge(sd_ready, t + 1)
            out = vec.open(pe)
            for h in range(RH):
                hs = slice(P * h, P * h + P)
                last = mm(out[:, hs], SS[:, t % 2, hs], RV[:, t, hs], start=True, stop=t == NS)
                if t < NS:
                    for d in range(2):
                        last = mm(out[:, hs], QX[:, t % 2, d, h, :], ST[:, d, t, hs], start=False, stop=d == 1)
            vec.close(last)
        for t in range(NT):
            pe.wait_ge(ro_ready, t + 1)
            transposes(sca, [OALL[:, t, P * h:P * h + P] for h in range(RH)])
        phase_end(pe, 3)
        if STOP <= 3:
            return

        pe.wait_ge(qk_ready, 1)
        for t in range(NT):
            transposes(sca, [AQK[:, t, P * b:P * b + P] for b in range(4)])
        transposes(vec, [AQK[:, t, 512:640] for t in range(NS)])
        transposes(vec, [CK, AQK[:, NS, 512:640]])
        all_emptied()
        flat = banks[:].rearrange("p b c -> p (b c)")
        units = [(t, b, half) for t in range(NT) for b in range(4) for half in range(2)]

        def keys_of(t):
            return KEYS if t < NS else P

        def scores(i):
            t, b, half = units[i]
            if i >= 2:
                pe.wait_ge(p_ready, i - 1)
            hs = slice(64 * half, 64 * half + 64)
            q = QTT[hs, b, P * t:P * t + P]
            at = 1024 * half
            if t < NS:
                mm(flat[:, at:at + 512], q, KTT[hs, 0:512], start=True, stop=True)
                last = mm(flat[:, at + 512:at + 640], q, KTT[hs, 512:640], start=True, stop=True)
            else:
                last = mm(flat[:, at:at + P], q, KTP[hs, :], start=True, stop=True)
            last.then_inc(s_full, 1)

        def turn_probabilities(i):
            t = units[i][0]
            pe.wait_ge(p_ready, i + 1)
            if i >= 1:
                pe.wait_ge(pt_ready, i)
            for c in range(keys_of(t) // P):
                last = nc.tensor.transpose(flat[:, 2048 + P * c:2048 + P * c + P], PR[:, i % 2, P * c:P * c + P], ident[:])
            last.then_inc(pt_full, 1)

        def values(i):
            t, b, half = units[i]
            pe.wait_ge(pt_ready, i + 1)
            if b == half == 0 and t >= 1:
                pe.wait_ge(ao_ready, t)
            head = b + 4 * half
            n = keys_of(t) // P
            for c in range(n):
                if t < NS:
                    v = AV[:, c, :] if c < NS else CV
                else:
                    v = AV[:, NS, :]
                last = mm(banks[:, 6, 64 * head:64 * head + 64], PT[:, i % 2, P * c:P * c + P],
                          v[:, 64 * half:64 * half + 64], start=c == 0, stop=c == n - 1)
            last.then_inc(o_full, 1)

        def turn_outputs(t):
            pe.wait_ge(ao_ready, t + 1)
            if t >= 1:
                pe.wait_ge(aot_ready, t)
            for b in range(4):
                last = nc.tensor.transpose(banks[:, 7, P * b:P * b + P], AO[:, t % 2, P * b:P * b + P], ident[:])
            last.then_inc(aot_full, 1)

        scores(0)
        for i in range(len(units)):
            if i + 1 < len(units):
                scores(i + 1)
            turn_probabilities(i)
            if i >= 1:
                values(i - 1)
            if i % 8 == 2 and i > 8:
                turn_outputs(i // 8 - 1)
        values(len(units) - 1)
        turn_outputs(NT - 1)
        phase_end(pe, 4)
        if STOP <= 4:
            return

        for n in range(2):
            for branch, x in enumerate((ROT, ATT, YT)):
                w = weights()
                for t in range(NT):
                    out = sca.open(pe)
                    for k in range(KD):
                        last = mm(out, HT[:, k, P * t:P * t + P], w[:, k, :], start=k == 0, stop=k == KD - 1)
                    sca.close(last)
                weights_used(sca)
                chans = (vec,) if branch < 2 else (sca, vec)
                ws = [weights() for _ in chans]
                for t in range(NT):
                    for chan, w in zip(chans, ws[::-1]):
                        out = chan.open(pe)
                        for k in range(4):
                            last = mm(out, x[:, k, P * t:P * t + P], w[:, k, :], start=k == 0, stop=k == 3)
                        chan.close(last)
                for _ in chans:
                    weights_used(vec)
        for t in range(NT):
            pe.wait_ge(mer_ready, t + 1)
            for half in range(2):
                transposes((vec, sca)[half], [MER[:, t, P * k:P * k + P] for k in range(4 * half, 4 * half + 4)])
        phase_end(pe, 5)
        if STOP <= 5:
            return

        for n in range(4, 12):
            ada_block(n, n)
        for n in range(2):
            w = weights()
            for t in range(NT):
                out = vec.open(pe)
                for k in range(KD):
                    last = mm(out, MERT[:, k, P * t:P * t + P], w[:, k, :], start=k == 0, stop=k == KD - 1)
                vec.close(last)
            weights_used(vec)
        phase_end(pe, 6)
        if STOP <= 6:
            return

        pe.wait_ge(route_in, 64)
        for t in range(NT):
            pe.wait_ge(h2_ready, t + 1)
            for half in range(2):
                transposes((vec, sca)[half], [ROWS2[:, t % 2, P * k:P * k + P] for k in range(4 * half, 4 * half + 4)])
            all_emptied()
            out = vec.open(pe)
            for k in range(KD):
                last = mm(out[:, 0:NE], COLS2[:, t % 2, k, :], WR[:, k, :], start=k == 0, stop=k == KD - 1)
            vec.close(last)
        pe.wait_ge(masks_ready, 1)
        out = vec.open(pe)
        for t in range(NT):
            for j in range(t + 1):
                mm(out[:, NE * t:NE * t + NE], upper[:] if j == t else ones[:], MB[:, j, :], start=j == 0, stop=j == t)
        for j in range(NT):
            last = mm(out[:, NE * NT:NE * NT + NE], ones[:], MB[:, j, :], start=j == 0, stop=j == NT - 1)
        vec.close(last)
        phase_end(pe, 7)
        if STOP <= 7:
            return

        def down(n, m, e, b):
            pe.wait_ge(hid_ready, n + 1)
            at_least(pe, ht_ready, n)
            for k in range(4):
                last = nc.tensor.transpose(banks[:, 4, P * k:P * k + P], HID[:, b, P * k:P * k + P], ident[:])
            last.then_inc(ht_full, 1)
            pe.wait_ge(ht_ready, n + 1)
            pe.wait_ge(wd_in[b], 16 * m + 16)
            for half, (full, emptied) in enumerate(((dn0, out_d), (dn1, out_a))):
                at_least(pe, emptied, n)
                for k in range(4):
                    last = mm(banks[:, 5 + half, :], HIDT[:, b, P * k:P * k + P], WD[b][:, k, 512 * half:512 * half + 512],
                              start=k == 0, stop=k == 3)
                last.then_inc(full, 1)

        def gate_up(n, m, e, b, before):
            pe.wait_ge(g_in[b], 16 * m + 16)
            at_least(pe, gt_d, n)
            at_least(pe, gt_a, n)
            for k in range(KD):
                last = nc.tensor.transpose(banks[:, k // 4, P * (k % 4):P * (k % 4) + P], ROWS2[:, b, P * k:P * k + P], ident[:])
            last.then_inc(g_t, 1)
            if before:
                before()
            pe.wait_ge(gt_d, n + 1)
            pe.wait_ge(gt_a, n + 1)
            at_least(pe, hid_ready, n)
            for bank, w, w_in_, full in ((2, WG, wg_in, gate_full), (3, WU, wu_in, up_full)):
                pe.wait_ge(w_in_[b], 16 * m + 16)
                for k in range(KD):
                    last = mm(banks[:, bank, :], COLS2[:, b, k, :], w[b][:, k, :], start=k == 0, stop=k == KD - 1)
                last.then_inc(full, 1)

        all_passes(pe, lambda r: expert_pipeline(pe, r, gate_up, down))
        phase_end(pe, 8)

    @block.scalar
    def _(act):
        sca = Bank(4, full_a, free_a)
        act_done = engine_tools(act, act_step)
        A = nc.scalar.activation

        def copy_out(dst, cols=512):
            src = sca.take(act)
            sca.give(A(dst, src[0:dst.shape[0], 0:cols], ACT.Copy))

        act.wait_ge(c_in, 32)
        A(cT[:, 1], cT[:, 0], ACT.Tanh, scale=0.5).then_inc(tanh_c, 1)
        for t in range(NT):
            act.wait_ge(x_in, 16 * NT)
            act_done(A(SQ, X[:, t, :], ACT.Square, accum_out=small[:, t:t + 1]))
        act.sem_inc(sq_ready, 1)
        for n in range(4):
            for s in range(2):
                copy_out(BC[:, n // 2, s, 512 * (n % 2):512 * (n % 2) + 512])
        act.wait_ge(free_a, 8)
        act.sem_inc(a2d, 1)
        phase_end(act, 0)
        if STOP <= 0:
            return

        act.wait_ge(x_in, 16 * NT + 1)
        act_done(A(SC_[4], SC_[3], ACT.Sin))
        A(SC_[5], SC_[3], ACT.Sin, scale=0.5).then_inc(a2d, 1)
        for d in range(2):
            for j in range(2):
                for q in range(4):
                    src = sca.take(act)
                    sca.give(A(FM[:, d, j, 4 * q:4 * q + 4, :], src.rearrange("p (a b) -> p a b", a=4), ACT.Copy))
        act.wait_ge(free_a, 8 + 16)
        act.sem_inc(a2d, 1)
        act.wait_ge(scr_in, 1)
        for t in range(NT):
            src = sca.take(act)
            sca.give(A(SU[:, t, :], src, ACT.Copy))
            act.wait_ge(free_a, sca.k)
            act.sem_inc(scr, 1)
        for q in range(6):
            n = min(6, G - 6 * q)
            src = sca.take(act)
            sca.give(A(U[:, 6 * q:6 * q + n, :], src[:, 0:NC * n].rearrange("p (a b) -> p a b", a=n), ACT.Copy))
        Y = S[0:NC, :].rearrange("c (t g o) -> c g t o", t=Q, g=G)
        for q in range(G // 4):
            src = sca.take(act)
            sca.give(A(Y[:, 8 * (q // 2) + q % 2:8 * (q // 2) + 8:2], src[0:NC].rearrange("c (g t o) -> c g t o", g=4, t=Q), ACT.Gelu_apprx_tanh))
        for kb in range(4):
            for th in range(2):
                src = sca.take(act)
                dst = YT[:, kb, :].rearrange("p (c t) -> p t c", t=Q)[:, 4 * th:4 * th + 4, :]
                sca.give(A(dst, src[:, 0:4 * NC].rearrange("p (t c) -> p t c", t=4), ACT.Copy))
        act.wait_ge(free_a, sca.k)
        phase_end(act, 1)
        if STOP <= 1:
            return


        for b in range(6):
            for t in range(NT):
                if (NT * b + t) % 2:
                    src = sca.take(act)
                    if b < 5:
                        sca.give(A((RQ, RK, RV, RG, AQK[:, :, 0:512])[b][:, t, :], src, ACT.Copy))
                    else:
                        act_done(A(AQK[:, t, 512:640], src[:, 0:128], ACT.Copy))
                        sca.give(A(AV[:, t, :], src[:, 128:256], ACT.Copy))
        for t in range(NT):
            src = sca.take(act)
            sca.give(A(RQT[:, :, P * t:P * t + P], src.rearrange("p (a b) -> p a b", a=4), ACT.Copy, scale=float(P) ** -0.5))
        act.wait_ge(free_a, sca.k)
        phase_end(act, 2)
        if STOP <= 2:
            return

        act.wait_ge(ret_in, 16 * 8)
        for d in range(2):
            for h in range(RH):
                lg = LG[:, d, h:h + 1]
                A(QX[:, 0, d, h, :], DIST[:, d, :], ACT.Exp, scale=lg)
                A(XI[:, d, h, :], DIST[:, 2 + d, :], ACT.Exp, scale=lg)
                A(ZETA[:, d, h:h + 1], ZPOS[:, d:d + 1], ACT.Exp, scale=lg)
        act_done(A(CD, LG, ACT.Exp, scale=float(P)))
        act.sem_inc(ret_exp, 1)
        for t in range(NT):
            if t == 0:
                act.wait_ge(kv_done, len(KV_ORDER))
            if t >= 2:
                act.wait_ge(ro_ready, t - 1)
            A(VZ[:, t % 2, :], RG[:, t, :], ACT.Tanh, scale=0.5).then_inc(ro_gate, 1)
            if t >= 1:
                src = sca.take(act)
                sca.give(A(ROT[:, :, P * (t - 1):P * t], src.rearrange("p (a b) -> p a b", a=4), ACT.Copy, scale=0.5))
        src = sca.take(act)
        sca.give(A(ROT[:, :, P * (NT - 1):P * NT], src.rearrange("p (a b) -> p a b", a=4), ACT.Copy, scale=0.5))
        act.wait_ge(free_a, sca.k)
        phase_end(act, 3)
        if STOP <= 3:
            return

        for t in range(NT):
            src = sca.take(act)
            sca.give(A(QTT[:, :, P * t:P * t + P], src.rearrange("p (a b) -> p a b", a=4), ACT.Copy, scale=float(HD) ** -0.5))
        flat = banks[:].rearrange("p b c -> p (b c)")
        for i in range(8 * NT):
            t, b, half = i // 8, i % 8 // 2, i % 2
            n = KEYS if t < NS else P
            act.wait_ge(s_max, i + 1)
            if i >= 2:
                act.wait_ge(pt_full, i - 1)
            head = b + 4 * half
            A(PR[:, i % 2, 0:n], flat[:, 1024 * half:1024 * half + n], ACT.Exp, bias=AMAX[:, i % 4:i % 4 + 1],
              accum_out=ASUM[:, t, head:head + 1]).then_inc(p_ready, 1)
        phase_end(act, 4)
        if STOP <= 4:
            return

        for n in range(2):
            for branch in range(3):
                for t in range(NT):
                    src = sca.take(act)
                    if n + branch:
                        act.wait_ge(mer_step, NT * (3 * n + branch - 1) + t + 1)
                    act_done(A(TG[:, t, :], src, ACT.Tanh, scale=0.5))
                    act.sem_inc(free_a, 1); sca.k += 1
                    act.sem_inc(tg_ready, 1)
                if branch == 2:
                    for t in range(NT):
                        src = sca.take(act)
                        i = NT * n + t
                        if i >= 2:
                            act.wait_ge(tb_used, i - 1)
                        act_done(A(MT1[:, i % 2, :], src, ACT.Tanh, scale=0.5))
                        act.sem_inc(free_a, 1); sca.k += 1
                        act.sem_inc(tb_ready, 1)
        for t in range(NT):
            src = sca.take(act)
            sca.give(A(MERT[:, 4:8, P * t:P * t + P], src.rearrange("p (a b) -> p a b", a=4), ACT.Copy, scale=0.5))
        act.wait_ge(free_a, sca.k)
        phase_end(act, 5)
        if STOP <= 5:
            return

        for n in range(8):
            for s in range(2):
                copy_out(BC2[:, n // 2, s, 512 * (n % 2):512 * (n % 2) + 512])
        act.wait_ge(free_a, sca.k)
        act.sem_inc(a2d, 1)
        phase_end(act, 6)
        if STOP <= 6:
            return

        for t in range(NT):
            act_done(A(SQ2, X2[:, t, :], ACT.Square, accum_out=small[:, t:t + 1]))
        act.sem_inc(sq_ready, 1)
        for t in range(NT):
            src = sca.take(act)
            act_done(A(COLS2[:, t % 2, 4:8, :], src.rearrange("p (a b) -> p a b", a=4), ACT.Copy))
            act.sem_inc(free_a, 1); sca.k += 1
        act.wait_ge(exp_ready, 1)
        act_done(A(PROB, LOGIT, ACT.Exp))
        act.sem_inc(exp_ready, 1)
        phase_end(act, 7)
        if STOP <= 7:
            return

        def act_end(n, m, e, b):
            act.wait_ge(ht_full, n + 1)
            at_least(act, dn1, n - 1)
            A(HIDT[:, b, :], banks[:, 4, :], ACT.Copy).then_inc(ht_ready, 1)
            act.wait_ge(dn1, n + 1)
            at_least(act, out_wr[b], 16 * m)
            A(OUT[:, b, 512:1024], banks[:, 6, :], ACT.Copy).then_inc(out_a, 1)
            act.wait_ge(out_a, n + 1)
            act.wait_ge(out_d, n + 1)
            act.dma_start(scratch_out.rearrange("(e p) c -> e p c", p=CAP)[e], OUT[:, b, :]).then_inc(out_wr[b], 16)

        def act_begin(n, m, e, b, before):
            act.wait_ge(g_t, n + 1)
            at_least(act, up_full, n - 1)
            A(COLS2[:, b, 4:8, :], banks[:, 1, :].rearrange("p (a b) -> p a b", a=4), ACT.Copy).then_inc(gt_a, 1)
            if before:
                before()
            act.wait_ge(gate_full, n + 1)
            at_least(act, hid_ready, n)
            A(TH, banks[:, 2, :], ACT.Tanh, scale=0.5).then_inc(th_ready, 1)

        all_passes(act, lambda r: expert_pipeline(act, r, act_begin, act_end))
        phase_end(act, 8)
        if STOP <= 8:
            return
        for t in range(NT):
            act_done(A(SQ2F, X2[:, t, :], ACT.Square, accum_out=small[:, t:t + 1]))
        act.sem_inc(fin_sq, 1)

    @block.vector
    def _(dve):
        vec = Bank(0, full_d, free_d)
        done = engine_tools(dve, dve_step)
        V_ = nc.vector
        tt, ts, stt, cp = V_.tensor_tensor, V_.tensor_scalar, V_.scalar_tensor_tensor, V_.tensor_copy

        def rsqrt(out, x, t):
            done(ts(out.bitcast(I32), x.bitcast(I32), -0.5, float(0x5f3759df), ALU.mult, ALU.add))
            for _ in range(4):
                done(tt(t, out, out, ALU.mult))
                done(tt(t, t, x, ALU.mult))
                done(ts(t, t, -0.5, 1.5, ALU.mult, ALU.add))
                done(tt(out, out, t, ALU.mult))

        def exact_exp(out, x, t, r, k):
            done(ts(r, x, -87.0, 88.0, ALU.max, ALU.min))
            done(ts(t, r, 1.4426950408889634, MAGIC, ALU.mult, ALU.add))
            done(ts(t, t, -MAGIC, None, ALU.add))
            done(ts(k, t, 127.0, 8388608.0, ALU.add, ALU.mult))
            done(stt(r, t, -LN2_HI, r, ALU.mult, ALU.add))
            done(stt(r, t, -LN2_LO, r, ALU.mult, ALU.add))
            done(ts(out, r, EXP_C[0], None, ALU.mult))
            for c in EXP_C[1:]:
                done(stt(out, out, c, r, ALU.add, ALU.mult))
            done(ts(out, out, 1.0, None, ALU.add))
            done(tt(out, out, k.bitcast(F32), ALU.mult))

        def cmul(ore, oim, ar, ai, br, bi, t):
            done(tt(t, ar, br, ALU.mult))
            done(tt(ore, ai, bi, ALU.mult))
            done(tt(ore, t, ore, ALU.subtract))
            done(tt(t, ar, bi, ALU.mult))
            done(tt(oim, ai, br, ALU.mult))
            done(tt(oim, t, oim, ALU.add))

        done(V_.memset(ones[:], 1.0))
        dve.wait_ge(tanh_c, 1)
        done(stt(cT[:, 1], cT[:, 1], 1.0, cT[:, 0], ALU.add, ALU.mult))
        ts(cS[:], cT[:, 1], 0.5, None, ALU.mult).then_inc(silu_c, 1)
        dve.wait_ge(sq_ready, 1)
        done(ts(small[:, 8:8 + NT], small[:, 0:NT], 1.0 / D, EPS, ALU.mult, ALU.add))
        rsqrt(small[:, 16:16 + NT], small[:, 8:8 + NT], small[:, 24:24 + NT])
        dve.wait_ge(rows_in, 96)

        def mod_row(n, row, gain):
            src = vec.take(dve)
            done(tt(row, src[0:2, :], bias_row[:, n, :], ALU.add))
            vec.k += 1
            dve.sem_inc(free_d, 1)
            if gain is not None:
                done(stt(row, row, 1.0, gain[:, 512 * (n % 2):512 * (n % 2) + 512], ALU.add, ALU.mult))
            dve.sem_inc(mod_ready, 1)

        for n in range(4):
            if n >= 2:
                dve.wait_ge(full_a, 2 * (n - 1))
            mod_row(n, modrow[:, n % 2, :], gain_row[:, 0] if n >= 2 else None)
        dve.wait_ge(a2d, 1)
        for t in range(NT):
            s = 0 if t < NS else 1
            if t >= 2:
                dve.wait_ge(full_d, 4 + 2 * (t - 1))
            xn = XN[:, t % 2, :]
            done(stt(xn, X[:, t, :], small[:, 16 + t:17 + t], BC[:, 1, s, :], ALU.mult, ALU.mult))
            tt(xn, xn, BC[:, 0, s, :], ALU.add).then_inc(xn_ready, 1)
            for half in range(2):
                src = vec.take(dve)
                vec.give(cp(HT[:, 4 * half:4 * half + 4, P * t:P * t + P], src.rearrange("p (a b) -> p a b", a=4)))
        dve.wait_ge(free_d, vec.k)
        dve.wait_ge(dve_step, 1)
        phase_end(dve, 0)
        if STOP <= 0:
            return

        dve.wait_ge(par_in, 16 * 17)
        for d in range(2):
            done(cp(NAT[:, 4 + d, :].rearrange("g (h p) -> g h p", h=2),
                    LD[:, d, :].unsqueeze(2).broadcast_to([GP, 2, PS])))
        dve.sem_inc(nat_ready, 1)
        src = vec.take(dve)
        done(cp(PAR.rearrange("p a b -> p (a b)"), src[:, 0:160]))
        dve.sem_inc(free_d, 1); vec.k += 1
        for j in range(2):
            src = vec.take(dve)
            vec.give(cp(CT[:, j], src[:, 0:256].rearrange("p (a b) -> p a b", a=GP)))
        dve.wait_ge(free_d, vec.k)
        par = lambda n: PAR[:, n:n + 2, :]
        are, aim, ldt = par(0), par(2), par(4)
        step_, re, im, mag, t1, t2 = SC_[0], SC_[1], SC_[2], SC_[6], SC_[7], SC_[8]
        exact_exp(step_, ldt, t1, t2, SCI)
        done(tt(re, are, step_, ALU.mult))
        done(tt(im, aim, step_, ALU.mult))
        exact_exp(mag, re, t1, t2, SCI)
        ang = SC_[3]
        done(ts(t1, im, float(1 / (2 * np.pi)), MAGIC, ALU.mult, ALU.add))
        done(ts(t1, t1, -MAGIC, None, ALU.add))
        done(stt(ang, t1, -TWO_PI_A, im, ALU.mult, ALU.add))
        done(stt(ang, t1, -TWO_PI_B, ang, ALU.mult, ALU.add))
        done(stt(ang, t1, -TWO_PI_C, ang, ALU.mult, ALU.add))
        ts(ang, ang, 3.1415925, -3.1415925, ALU.min, ALU.max).then_inc(x_in, 1)
        dve.wait_ge(a2d, 2)
        sin, cos, half_sin = SC_[4], SC_[9], SC_[5]
        done(tt(cos, half_sin, half_sin, ALU.mult))
        done(ts(cos, cos, -2.0, 1.0, ALU.mult, ALU.add))
        done(V_.memset(PW[:, 0, :, 0, :], 1.0))
        done(V_.memset(PW[:, 1, :, 0, :], 0.0))
        done(tt(PW[:, 0, :, 1, :], mag, cos, ALU.mult))
        done(tt(PW[:, 1, :, 1, :], mag, sin, ALU.mult))
        for m in (1, 2, 4):
            b = [PW[:, j, :, m, :].unsqueeze(2).broadcast_to([P, 2, m, GP]) for j in range(2)]
            t = PWT[:, 0:2 * m * GP].rearrange("p (a b c) -> p a b c", a=2, b=m)
            cmul(PW[:, 0, :, m + 1:2 * m + 1, :], PW[:, 1, :, m + 1:2 * m + 1, :],
                 PW[:, 0, :, 1:m + 1, :], PW[:, 1, :, 1:m + 1, :], b[0], b[1], t)
        nre, den, qre, qim = SC_[10], SC_[11], SC_[12], SC_[13]
        done(ts(nre, PW[:, 0, :, 1, :], -1.0, None, ALU.add))
        done(tt(den, are, are, ALU.mult))
        done(tt(t1, aim, aim, ALU.mult))
        done(tt(den, den, t1, ALU.add))
        done(V_.reciprocal(den, den))
        nim = PW[:, 1, :, 1, :]
        done(tt(qre, nre, are, ALU.mult))
        done(tt(t1, nim, aim, ALU.mult))
        done(tt(qre, qre, t1, ALU.add))
        done(tt(qre, qre, den, ALU.mult))
        done(tt(qim, nim, are, ALU.mult))
        done(tt(t1, nre, aim, ALU.mult))
        done(tt(qim, qim, t1, ALU.subtract))
        done(tt(qim, qim, den, ALU.mult))
        for d in range(2):
            bc = lambda x: x[:, d, :].unsqueeze(2).broadcast_to([P, GP, GI])
            cmul(BB[:, d, 0], BB[:, d, 1], bc(qre), bc(qim), BN[:, 0], BN[:, 1], BBT)
        ure, uim, vre, vim, m8 = SC_[10], SC_[11], SC_[12], SC_[13], SC_[14]
        cmul(ure, uim, cos, sin, cos, sin, t1)
        cmul(vre, vim, ure, uim, ure, uim, t1)
        cmul(SC_[15], SC_[16], vre, vim, vre, vim, t1)
        done(tt(m8, mag, mag, ALU.mult))
        done(tt(m8, m8, m8, ALU.mult))
        done(tt(m8, m8, m8, ALU.mult))
        for d in range(2):
            pw = [PW[:, j, d, 0:Q, :].rearrange("p k g -> p g k") for j in range(2)]
            if d == 0:
                pw = [x[:, :, ::-1] for x in pw]
            pw = [x.unsqueeze(3).broadcast_to([P, GP, Q, GI]) for x in pw]
            bb = [BB[:, d, j].unsqueeze(2).broadcast_to([P, GP, Q, GI]) for j in range(2)]
            if d == 1:
                dve.wait_ge(free_a, 8 + 8)
            cmul(FP[0], FP[1], pw[0], pw[1], bb[0], bb[1], FPT)
            dve.sem_inc(d2a, 1)
        dve.wait_ge(free_a, 8 + 16)
        for d in range(2):
            pw = [PW[:, j, d].rearrange("p k g -> p g k").unsqueeze(3).broadcast_to([P, GP, 9, GI]) for j in range(2)]
            ct = [CT[:, j].unsqueeze(2).broadcast_to([P, GP, 9, GI]) for j in range(2)]
            done(tt(CTMP, ct[1], pw[1], ALU.mult))
            done(tt(CPW[:, d, 0], ct[0], pw[0], ALU.mult))
            done(tt(CPW[:, d, 0], CPW[:, d, 0], CTMP, ALU.subtract))
            done(tt(CTMP, ct[0], pw[1], ALU.mult))
            done(tt(CPW[:, d, 1], ct[1], pw[0], ALU.mult))
            fl = lambda x: x.rearrange("p a b c -> p (a b c)")
            done(stt(fl(CPW[:, d, 1]), fl(CPW[:, d, 1]), -1.0, fl(CTMP), ALU.mult, ALU.subtract))
        dve.sem_inc(d2p, 1)
        for d in range(2):
            for q in range(G // 4):
                src = vec.take(dve)[0:GI].rearrange("i (g k o) -> i g k o", g=4, k=Q)
                gs = slice(8 * (q // 2) + q % 2, 8 * (q // 2) + 8, 2)
                if d == 0:
                    vec.give(cp(KP[:, gs, 7:15, :], src))
                else:
                    if q == 0:
                        dve.wait_ge(free_d, vec.k)
                    done(cp(KP[:, gs, 0:7, :], src[:, :, 7:0:-1, :]))
                    vec.give(tt(KP[:, gs, 7, :], KP[:, gs, 7, :], src[:, :, 0, :], ALU.add))
        dve.wait_ge(free_d, vec.k)
        done(tt(DG, DT_.unsqueeze(2).broadcast_to([GI, G, GI]),
                ident[0:GI, 0:GI].unsqueeze(1).broadcast_to([GI, G, GI]), ALU.mult))
        tt(KP[:, :, 7, :], KP[:, :, 7, :], DG, ALU.add).then_inc(d2p, 1)
        dve.wait_ge(scr, NT + 16)
        cp(S[0:NC, :].rearrange("c (g s i) -> c s g i", g=G, s=Q), SRAW).then_inc(d2p, 1)
        dve.wait_ge(d2p, 3)
        done(V_.memset(V[:, :, :, :, CS + 1].rearrange("p a b c -> p (a b) c"), 0.0))
        for d in range(2):
            for c in range(2):
                done(cp(V[:, d, c, :, 0], PAR[:, 6 + 2 * c + d, :]))
        for d in range(2):
            for c in range(2):
                for q in range(3):
                    n = min(6, GP - 6 * q)
                    src = vec.take(dve)[:, 0:NC * n].rearrange("p (a b) -> p a b", a=n)
                    lat, con = src[:, :, 0:CS], src[:, :, CS:NC]
                    if d:
                        lat, con = lat[:, :, ::-1], con[:, :, ::-1]
                    done(cp(V[:, d, c, 6 * q:6 * q + n, 1:CS + 1], lat))
                    vec.give(cp(V[:, d, c, 6 * q:6 * q + n, CS + 2:SC], con))
        dve.wait_ge(free_d, vec.k)
        v3 = lambda x: x.rearrange("p (a b) -> p a b", b=SC)
        parts = ((slice(0, CS + 1), slice(0, CS + 1)), (slice(CS + 1, SC), slice(0, CP_ + 1)))
        for d in range(2):
            rot = [RT[:, j] for j in range(2)]
            for j in range(2):
                done(V_.memset(rot[j][:, :, 0], 1.0 - j))
                done(cp(rot[j][:, :, 1], SC_[15 + j][:, d, :]))
            for m in (1, 2, 4, 8, 16, 32):
                b = [x[:, :, m:m + 1].broadcast_to([P, GP, m]) for x in rot]
                cmul(rot[0][:, :, m + 1:2 * m + 1], rot[1][:, :, m + 1:2 * m + 1],
                     rot[0][:, :, 1:m + 1], rot[1][:, :, 1:m + 1], b[0], b[1],
                     RTT[:, 0:m * GP].rearrange("p (a b) -> p a b", b=m))
            done(cp(A8, m8[:, d, :].unsqueeze(2).broadcast_to([P, GP, SC])))
            done(V_.memset(A8[:, :, 0], 0.0))
            done(V_.memset(A8[:, :, CS + 1], 0.0))
            vr, vi = V[:, d, 0], V[:, d, 1]
            for cols, k in parts:
                for dst, r_, x in ((0, 0, vr), (1, 1, vi), (2, 0, vi), (3, 1, vr)):
                    done(tt(v3(TMP4[dst])[:, :, cols], rot[r_][:, :, k], x[:, :, cols], ALU.mult))
            fl = lambda x: x.rearrange("p a b -> p (a b)")
            done(tt(fl(vr), TMP4[0], TMP4[1], ALU.add))
            done(tt(fl(vi), TMP4[2], TMP4[3], ALU.subtract))
            for j, x in enumerate((vr, vi)):
                done(V_.tensor_tensor_scan(Z[j], fl(A8), fl(x), 0.0, ALU.mult, ALU.add))
            for cols, k in parts:
                for dst, r_, x in ((0, 0, 0), (1, 1, 1), (2, 0, 1), (3, 1, 0)):
                    done(tt(v3(TMP4[dst])[:, :, cols], rot[r_][:, :, k], v3(Z[x])[:, :, cols], ALU.mult))
            for j, (x, y, op) in enumerate(((0, 1, ALU.subtract), (2, 3, ALU.add))):
                xin = fl(V[:, d, j])[:, 0:GP * NC].rearrange("p (a b) -> p a b", b=NC)
                for out, cols in ((xin[:, :, 0:CS], slice(0, CS)), (xin[:, :, CS:NC], slice(CS + 1, CS + 1 + CP_))):
                    if d:
                        out = out[:, :, ::-1]
                    done(tt(out, v3(TMP4[x])[:, :, cols], v3(TMP4[y])[:, :, cols], op))
                done(tt(SF[:, j, d, :], v3(TMP4[x])[:, :, SC - 1], v3(TMP4[y])[:, :, SC - 1], op))
        dve.sem_inc(d2p, 1)
        src = vec.take(dve)
        vec.give(cp(SFO.rearrange("p a b -> p (a b)"), src[0:GP, :]))
        dve.wait_ge(free_d, vec.k)
        dve.sem_inc(d2a, 1)
        phase_end(dve, 1)
        if STOP <= 1:
            return


        for b in range(6):
            for t in range(NT):
                if (NT * b + t) % 2 == 0:
                    src = vec.take(dve)
                    if b < 5:
                        vec.give(cp((RQ, RK, RV, RG, AQK[:, :, 0:512])[b][:, t, :], src))
                    else:
                        done(cp(AQK[:, t, 512:640], src[:, 0:128]))
                        vec.give(cp(AV[:, t, :], src[:, 128:256]))
        for t in range(NT):
            src = vec.take(dve)
            vec.give(cp(RKT[:, :, P * t:P * t + P], src.rearrange("p (a b) -> p a b", a=4)))
        dve.wait_ge(free_d, vec.k)
        phase_end(dve, 2)
        if STOP <= 2:
            return

        dve.wait_ge(ret_in, 16 * 8)
        dve.wait_ge(ret_exp, 1)
        for d in range(2):
            done(tt(QX[:, 0, d], QX[:, 0, d], MASK[:, d, :].unsqueeze(1).broadcast_to([P, RH, P]), ALU.mult))
        done(tt(DEC, QX[:, 0, 0], QX[:, 0, 1], ALU.add))
        r3 = lambda x: x.rearrange("p (h e) -> p h e", h=RH)
        for i in range(len(KV_ORDER) + 1):
            if i < len(KV_ORDER):
                d, t = KV_ORDER[i]
                if i >= 2:
                    dve.wait_ge(full_d, vec.k + 1 - 0)
                tt(r3(VZ[:, i % 2, :]), r3(RV[:, t, :]), ZETA[:, d, :].unsqueeze(2).broadcast_to([P, RH, P]),
                   ALU.mult).then_inc(vz_ready, 1)
            if i >= 1:
                d, t = KV_ORDER[i - 1]
                src = vec.take(dve)
                if t == NS:
                    done(cp(KVO[:, d, :], src))
                    dve.sem_inc(kvo_ready, 1)
                else:
                    nxt = t + 1 if d == 0 else t - 1
                    for h in range(RH):
                        hs = slice(P * h, P * h + P)
                        done(stt(ST[:, d, nxt, hs], ST[:, d, t, hs], CD[:, d, h:h + 1], src[:, hs], ALU.mult, ALU.add))
                dve.sem_inc(free_d, 1); vec.k += 1
                dve.sem_inc(kv_done, 1)
        for t in range(NT):
            if t < NS:
                for d in range(2):
                    done(tt(QX[:, t % 2, d], RQT[:, :, P * t:P * t + P], XI[:, d], ALU.mult))
            src = vec.take(dve)
            done(tt(r3(SS[:, t % 2, :]), r3(src), DEC, ALU.mult))
            dve.sem_inc(free_d, 1); vec.k += 1
            dve.sem_inc(sd_ready, 1)
            src = vec.take(dve)
            done(cp(OALL[:, t, :], src))
            dve.sem_inc(free_d, 1); vec.k += 1
            done(tt(KVT, OALL[:, t, :], OALL[:, t, :], ALU.mult))
            done(V_.tensor_reduce(RSS[:, 0, RH * t:RH * t + RH], r3(KVT), AX.X, ALU.add))
        done(ts(RSS[:, 0, :], RSS[:, 0, :], 1.0 / P, EPS, ALU.mult, ALU.add))
        rsqrt(RSS[:, 1, :], RSS[:, 0, :], RSS[:, 2, :])
        for t in range(NT):
            o = OALL[:, t, :]
            done(tt(r3(o), r3(o), RSS[:, 1, RH * t:RH * t + RH].unsqueeze(2).broadcast_to([P, RH, P]), ALU.mult))
            done(tt(o, o, RNG, ALU.mult))
            dve.wait_ge(ro_gate, t + 1)
            done(stt(VZ[:, t % 2, :], VZ[:, t % 2, :], 1.0, RG[:, t, :], ALU.add, ALU.mult))
            tt(o, o, VZ[:, t % 2, :], ALU.mult).then_inc(ro_ready, 1)
        dve.wait_ge(ro_ready, NT)
        phase_end(dve, 3)
        if STOP <= 3:
            return

        NH = AH + KVH
        dve.wait_ge(att_in, 16 * 5)
        done(cp(QG[:, 0:AH, :], QGL[:, 0:1, :].broadcast_to([P, AH, HD])))
        done(cp(QG[:, AH:NH, :], QGL[:, 1:2, :].broadcast_to([P, KVH, HD])))
        h3 = lambda x: x.rearrange("p (h e) -> p h e", e=HD)
        for t in range(NT):
            done(tt(QT1, AQK[:, t, :], AQK[:, t, :], ALU.mult))
            done(V_.tensor_reduce(QSS[:, 0, NH * t:NH * t + NH], h3(QT1), AX.X, ALU.add))
        done(ts(QSS[:, 0, :], QSS[:, 0, :], 1.0 / HD, EPS, ALU.mult, ALU.add))
        rsqrt(QSS[:, 1, :], QSS[:, 0, :], QSS[:, 2, :])
        for t in range(NT):
            x, rs = AQK[:, t, :], QSS[:, 1, NH * t:NH * t + NH]
            swap = lambda v: v.rearrange("p (h b) -> p h b", h=2)
            done(tt(QT1[:, 0:512].rearrange("p (b h e) -> p h b e", b=4, h=2), x[:, 0:512].rearrange("p (h b e) -> p h b e", h=2, b=4),
                    swap(rs[:, 0:AH]).unsqueeze(3).broadcast_to([P, 2, 4, HD]), ALU.mult))
            done(tt(h3(QT1[:, 512:640]), h3(x[:, 512:640]), rs[:, AH:NH].unsqueeze(2).broadcast_to([P, KVH, HD]), ALU.mult))
            if t == NS:
                done(tt(h3(x), h3(QT1), QG, ALU.mult))
                break
            done(tt(h3(QT1), h3(QT1), QG, ALU.mult))
            pairs = lambda v: v.rearrange("p (h e two) -> p h e two", two=2, e=HD // 2)
            cos, sn = (ROPE[:, j, t, :] for j in range(2))
            done(tt(h3(x), h3(QT1), cos.unsqueeze(1).broadcast_to([P, NH, HD]), ALU.mult))
            for j in range(2):
                s_ = sn.rearrange("p (e two) -> p e two", two=2)[:, :, j].unsqueeze(1).broadcast_to([P, NH, HD // 2])
                done(tt(pairs(QT2)[:, :, :, j], pairs(QT1)[:, :, :, 1 - j], s_, ALU.mult))
            done(tt(x, x, QT2, ALU.add))
        dve.sem_inc(qk_ready, 1)
        dve.sem_inc(kv_out, 1)
        src = vec.take(dve)
        vec.give(cp(KTT[:, 0:512], src))
        src = vec.take(dve)
        done(cp(KTT[:, 512:640], src[:, 0:P]))
        vec.give(cp(KTP, src[:, P:2 * P]))
        dve.wait_ge(free_d, vec.k)
        flat = banks[:].rearrange("p b c -> p (b c)")
        NU = 8 * NT

        def top(i):
            t, half = i // 8, i % 2
            n = KEYS if t < NS else P
            dve.wait_ge(s_full, i + 1)
            if i >= 4:
                dve.wait_ge(p_ready, i - 3)
            V_.tensor_reduce(AMAX[:, i % 4:i % 4 + 1], flat[:, 1024 * half:1024 * half + n], AX.X, ALU.max,
                             negate=True).then_inc(s_max, 1)

        def copy_turned(i):
            n = KEYS if i // 8 < NS else P
            dve.wait_ge(pt_full, i + 1)
            if i >= 2:
                dve.wait_ge(o_full, i - 1)
            cp(PT[:, i % 2, 0:n], flat[:, 2048:2048 + n]).then_inc(pt_ready, 1)

        def rows_out(t):
            dve.wait_ge(o_full, 8 * t + 8)
            done(V_.reciprocal(ASUM[:, t, :], ASUM[:, t, :]))
            if t >= 2:
                dve.wait_ge(aot_full, t - 1)
            tt(h3(AO[:, t % 2, :]), h3(banks[:, 6, :]), ASUM[:, t, :].unsqueeze(2).broadcast_to([P, AH, HD]),
               ALU.mult).then_inc(ao_ready, 1)

        def columns_out(t):
            dve.wait_ge(aot_full, t + 1)
            cp(ATT[:, :, P * t:P * t + P], banks[:, 7, :].rearrange("p (a b) -> p a b", a=4)).then_inc(aot_ready, 1)

        top(0)
        for i in range(NU):
            if i + 1 < NU:
                top(i + 1)
            copy_turned(i)
            if i % 8 == 0 and i:
                rows_out(i // 8 - 1)
            if i % 8 == 2 and i > 8:
                columns_out(i // 8 - 1)
        rows_out(NT - 1)
        columns_out(NT - 1)
        dve.wait_ge(aot_ready, NT)
        phase_end(dve, 4)
        if STOP <= 4:
            return

        for n in range(2):
            ns = slice(512 * n, 512 * n + 512)
            for branch in range(3):
                for t in range(NT):
                    dve.wait_ge(tg_ready, NT * (3 * n + branch) + t + 1)
                    dst = MER[:, t, ns]
                    src = vec.take(dve)
                    if branch == 0:
                        done(stt(dst, TG[:, t, :], 1.0, src, ALU.add, ALU.mult))
                        dve.sem_inc(free_d, 1); vec.k += 1
                    else:
                        i = NT * n + t
                        if branch == 1:
                            done(stt(MT2[:, t % 2, :], TG[:, t, :], 1.0, src, ALU.add, ALU.mult))
                            dve.sem_inc(free_d, 1); vec.k += 1
                        else:
                            dve.wait_ge(tb_ready, i + 1)
                            done(stt(MT2[:, t % 2, :], MT1[:, i % 2, :], 1.0, src, ALU.add, ALU.mult))
                            dve.sem_inc(free_d, 1); vec.k += 1
                            dve.sem_inc(tb_used, 1)
                            done(ts(TG[:, t, :], TG[:, t, :], 0.5, 0.5, ALU.mult, ALU.add))
                            done(tt(MT2[:, t % 2, :], MT2[:, t % 2, :], TG[:, t, :], ALU.mult))
                        done(tt(dst, dst, MT2[:, t % 2, :], ALU.add))
                    dve.sem_inc(mer_step, 1)
                    if n == 1 and branch == 2:
                        dve.sem_inc(mer_ready, 1)
        for t in range(NT):
            src = vec.take(dve)
            vec.give(ts(MERT[:, 0:4, P * t:P * t + P], src.rearrange("p (a b) -> p a b", a=4), 0.5, None, ALU.mult))
        dve.wait_ge(free_d, vec.k)
        phase_end(dve, 5)
        if STOP <= 5:
            return

        dve.wait_ge(x2_in, 16 * (NT + 4))
        fa = FA5
        for n in range(4, 12):
            if n >= 6:
                dve.wait_ge(full_a, fa + 2 * (n - 5))
            src = vec.take(dve)
            row = modrow2[:, n % 2, :]
            done(tt(row, src[0:2, :], bias2[:, n - 4, :], ALU.add))
            vec.k += 1
            dve.sem_inc(free_d, 1)
            if n in (8, 9):
                done(stt(row, row, 1.0, gain2[:, 512 * (n % 2):512 * (n % 2) + 512], ALU.add, ALU.mult))
            dve.sem_inc(mod_ready, 1)
        dve.wait_ge(a2d, 4)
        for n in range(2):
            ns = slice(512 * n, 512 * n + 512)
            for t in range(NT):
                s = 0 if t < NS else 1
                src = vec.take(dve)
                done(tt(SQ2[:, 0:512], src, BC2[:, 0, s, ns], ALU.mult))
                done(tt(X2[:, t, ns], X2[:, t, ns], SQ2[:, 0:512], ALU.add))
                dve.sem_inc(free_d, 1); vec.k += 1
        phase_end(dve, 6)
        if STOP <= 6:
            return

        done(V_.memset(ZERO, 0))
        dve.sem_inc(zero_ready, 1)
        dve.wait_ge(sq_ready, 2)
        done(ts(small[:, 8:8 + NT], small[:, 0:NT], 1.0 / D, EPS, ALU.mult, ALU.add))
        rsqrt(small[:, 16:16 + NT], small[:, 8:8 + NT], small[:, 24:24 + NT])
        dve.wait_ge(route_in, 64)
        for t in range(NT):
            s = 0 if t < NS else 1
            if t >= 2:
                dve.wait_ge(h2_out, 16 * (t - 1))
            h = ROWS2[:, t % 2, :]
            done(stt(h, X2[:, t, :], small[:, 16 + t:17 + t], BC2[:, 2, s, :], ALU.mult, ALU.mult))
            done(tt(h, h, BC2[:, 1, s, :], ALU.add))
            dve.sem_inc(h2_ready, 1)
            src = vec.take(dve)
            done(cp(COLS2[:, t % 2, 0:4, :], src.rearrange("p (a b) -> p a b", a=4)))
            dve.sem_inc(free_d, 1); vec.k += 1
            src = vec.take(dve)
            done(tt(LOGIT[:, t, :], src[:, 0:NE], BR, ALU.add))
            dve.sem_inc(free_d, 1); vec.k += 1
        c = lambda j: ROUTE[:, j, :]
        over = lambda x, n: x.unsqueeze(2).broadcast_to([P, NT, n])
        red = lambda out, x, op: done(V_.tensor_reduce(out, x, AX.X, op))
        red(c(0), LOGIT, ALU.max)
        done(tt(LOGIT, LOGIT, over(c(0), NE), ALU.subtract))
        dve.sem_inc(exp_ready, 1)
        dve.wait_ge(exp_ready, 2)
        red(c(0), PROB, ALU.add)
        done(V_.reciprocal(c(0), c(0)))
        done(tt(PROB, PROB, over(c(0), NE), ALU.mult))
        p4 = PROB.rearrange("p t (g e) -> p t g e", e=EG)
        for j, (x, y, op) in enumerate(((0, 1, ALU.max), (0, 1, ALU.min), (2, 3, ALU.max), (2, 3, ALU.min))):
            done(tt(GH[j], p4[:, :, :, x], p4[:, :, :, y], op))
        done(tt(GH[4], GH[0], GH[2], ALU.max))
        done(tt(GH[5], GH[0], GH[2], ALU.min))
        done(tt(GH[6], GH[1], GH[3], ALU.max))
        done(tt(GH[5], GH[5], GH[6], ALU.max))
        done(tt(GH[4], GH[4], GH[5], ALU.add))

        def first_largest(onehot, index, value, x, n, tmp):
            it = IOTA[:, 0:n].unsqueeze(1).broadcast_to([P, NT, n])
            red(value, x, ALU.max)
            done(tt(tmp, x, over(value, n), ALU.is_equal))
            done(ts(tmp, tmp, -99.0, 99.0, ALU.mult, ALU.add))
            done(tt(tmp, tmp, it, ALU.add))
            red(index, tmp, ALU.min)
            done(tt(onehot, it, over(index, n), ALU.is_equal))

        first_largest(GH[7], c(0), c(1), GH[4], NG, GH[0])
        g16 = GH[7].unsqueeze(3).broadcast_to([P, NT, NG, EG])
        t4 = lambda x: x.rearrange("p t (g e) -> p t g e", e=EG)
        done(tt(t4(PROB), t4(PROB), g16, ALU.mult))
        done(tt(t4(PROB), t4(PROB), g16, ALU.add))
        done(ts(PROB, PROB, -1.0, None, ALU.add))
        E1, E2, V1, V2, R1, R2, W1, W2 = (c(j) for j in range(2, 10))
        first_largest(M1, E1, V1, PROB, NE, EQ)
        done(stt(PROB.rearrange("p t e -> p (t e)"), M1.rearrange("p t e -> p (t e)"), -3.0, PROB.rearrange("p t e -> p (t e)"), ALU.mult, ALU.add))
        first_largest(M2, E2, V2, PROB, NE, EQ)
        done(tt(MB, M1, M2, ALU.add))
        dve.sem_inc(masks_ready, 1)
        done(tt(c(0), V1, V2, ALU.add))
        done(V_.reciprocal(c(0), c(0)))
        for w_, v in ((W1, V1), (W2, V2)):
            done(tt(w_, v, c(0), ALU.mult))
            done(ts(w_, w_, 0.5, None, ALU.mult))
        src = vec.take(dve)
        done(cp(RANK, src[:, 0:NT * NE].rearrange("p (t e) -> p t e", t=NT)))
        red(c(0)[:, 0:1], src[:, NT * NE:NT * NE + NE], ALU.max)
        done(cp(TOP_COUNT, c(0)[:, 0:1]))
        dve.sem_inc(free_d, 1); vec.k += 1
        for k, (m_, rk, e_) in enumerate(((M1, R1, E1), (M2, R2, E2))):
            done(tt(EQ, m_, RANK, ALU.mult))
            red(rk, EQ, ALU.add)
            done(stt(CIDX[:, :, k], e_, float(T), rk, ALU.mult, ALU.add))
        dve.sem_inc(pos_ready, 1)
        phase_end(dve, 7)
        if STOP <= 7:
            return

        def dve_end(n, m, e, b):
            dve.wait_ge(dn0, n + 1)
            at_least(dve, out_wr[b], 16 * m)
            cp(OUT[:, b, 0:512], banks[:, 5, :]).then_inc(out_d, 1)

        def dve_begin(n, m, e, b, before):
            dve.wait_ge(g_t, n + 1)
            at_least(dve, up_full, n - 1)
            cp(COLS2[:, b, 0:4, :], banks[:, 0, :].rearrange("p (a b) -> p a b", a=4)).then_inc(gt_d, 1)
            if before:
                before()
            dve.wait_ge(th_ready, n + 1)
            at_least(dve, ht_full, n - 1)
            stt(HID[:, b, :], TH, 1.0, banks[:, 2, :], ALU.add, ALU.mult).then_inc(hid_step, 1)
            dve.wait_ge(hid_step, n + 1)
            dve.wait_ge(up_full, n + 1)
            tt(HID[:, b, :], HID[:, b, :], banks[:, 3, :], ALU.mult).then_inc(hid_ready, 1)

        def dve_pass(r):
            if not isinstance(r, int):
                dve.wait_ge(combined, NT * r)
            expert_pipeline(dve, r, dve_begin, dve_end)
            k = [0]

            def step(ins):
                k[0] += 1
                ins.then_inc(comb_step, 1)
                dve.wait_ge(comb_step, COMB_STEPS * r + k[0])

            lo = ROUTE[:, 10, :]
            for j, (rk, e_, w_) in enumerate(((R1, E1, W1), (R2, E2, W2))):
                if isinstance(r, int):
                    step(ts(lo, rk, 0.0, None, ALU.add))
                else:
                    step(ts(rk, rk, -float(CAP), None, ALU.add))
                    step(ts(lo, rk, 0.0, None, ALU.add))
                step(ts(ROUTE[:, 11, :], lo, 0.0, None, ALU.is_ge))
                step(ts(ROUTE[:, 12, :], lo, CAP - 0.5, None, ALU.is_lt))
                step(tt(ROUTE[:, 11, :], ROUTE[:, 11, :], ROUTE[:, 12, :], ALU.mult))
                step(tt(ROUTE[:, 11, :], ROUTE[:, 11, :], w_, ALU.mult))
                step(cp(WP[:, j, :], ROUTE[:, 11, :]))
                step(ts(lo, lo, 0.0, CAP - 1.0, ALU.max, ALU.min))
                step(stt(CIDX[:, :, j], e_, float(CAP), lo, ALU.mult, ALU.add))
                if isinstance(r, int):
                    step(cp(ROUTE[:, 12, :], lo))
            dve.sem_inc(cidx_ready, 1)
            for t in range(NT):
                s = 0 if t < NS else 1
                dve.wait_ge(y_in[t % 2], 32 * ((3, 2)[t % 2] * r + t // 2 + 1))
                y = [YR[:, t % 2, j, :] for j in range(2)]
                step(ts(y[0], y[0], WP[:, 0, t:t + 1], None, ALU.mult))
                step(stt(y[0], y[1], WP[:, 1, t:t + 1], y[0], ALU.mult, ALU.add))
                step(tt(y[0], y[0], BC2[:, 3, s, :], ALU.mult))
                step(tt(X2[:, t, :], X2[:, t, :], y[0], ALU.add))
                dve.sem_inc(combined, 1)
            assert k[0] == COMB_STEPS

        all_passes(dve, dve_pass)
        phase_end(dve, 8)
        if STOP <= 8:
            return
        dve.wait_ge(fin_sq, 1)
        dve.wait_ge(fin_in, 16)
        done(ts(small[:, 8:8 + NT], small[:, 0:NT], 1.0 / D, EPS, ALU.mult, ALU.add))
        rsqrt(small[:, 16:16 + NT], small[:, 8:8 + NT], small[:, 24:24 + NT])
        for t in range(NT):
            stt(X2[:, t, :], X2[:, t, :], small[:, 16 + t:17 + t], FG, ALU.mult, ALU.mult).then_inc(fin_ready, 1)

    @block.gpsimd
    def _(pool):
        phase_end(pool, 0)
        if STOP <= 0:
            return
        for n in range(1, 7):
            phase_end(pool, n)
            if STOP <= n:
                return
        nc.gpsimd.memset(PACE, 0.0).then_inc(pool_step, 1)
        pool.wait_ge(pool_step, 1)
        pool.wait_ge(zero_out, 16)
        pool.wait_ge(pos_ready, 1)
        pool.wait_ge(route_in, 64)
        for t in range(NT):
            for k in range(2):
                pool.indirect_dma_start(lists, bass.IndirectOffsetOnAxis(ap=CIDX[:, t, k:k + 1].bitcast(U32), axis=0),
                                        TOK[:, t:t + 1], None).then_inc(pos_out, 16)
        pool.wait_ge(pos_out, 16 * 2 * NT)
        phase_end(pool, 7)
        if STOP <= 7:
            return

        def pool_wait(s_, n):
            at_least(pool, s_, n)
            if not isinstance(n, int):
                nc.gpsimd.tensor_tensor(PACE[:, 1:2], PACE[:, 0:1], PACE[:, 0:1], ALU.add)

        def pool_pass(r):
            pool_wait(idx_in, 32 * r + 32)
            for e in range(NE):
                pool_wait(g_t, 16 * r + e - 1)
                pool.indirect_dma_start(ROWS2[:, e % 2, :], None, scratch_h2,
                                        bass.IndirectOffsetOnAxis(ap=IDX[:, e:e + 1].bitcast(U32), axis=0)).then_inc(g_in[e % 2], 16)
            for b in range(2):
                pool_wait(out_wr[b], 16 * 8 * r + 16 * 8)
            pool_wait(cidx_ready, r + 1)
            for t in range(NT):
                if t >= 2:
                    pool_wait(combined, NT * r + t - 1)
                for k in range(2):
                    pool.indirect_dma_start(YR[:, t % 2, k, :], None, scratch_out,
                                            bass.IndirectOffsetOnAxis(ap=CIDX[:, t, k:k + 1].bitcast(U32), axis=0)).then_inc(y_in[t % 2], 16)
            pool_wait(combined, NT * r + NT)

        all_passes(pool, pool_pass)
        phase_end(pool, 8)

    ctx.close()




def constants():
    k = {}
    k["k_ident"] = np.eye(P, dtype=np.float32)
    k["k_upper"] = np.triu(np.ones((P, P), np.float32), 1)
    s = np.zeros((2, 2, P), np.float32)
    s[0, 0] = 1
    s[1, 1] = 1
    k["k_sel"] = s
    k["k_iota"] = np.tile(np.arange(NE, dtype=np.float32), (P, 1))
    k["k_tok"] = np.ascontiguousarray(np.arange(T, dtype=np.int32).reshape(NT, P).T)
    pos = np.arange(P, dtype=np.float32)
    s_, t_ = pos[:, None], pos[None, :]
    k["k_dist"] = np.stack([np.maximum(t_ - s_, 0), np.maximum(s_ - t_, 0), t_ + 1 + 0 * s_, P - t_ + 0 * s_], 1).astype(np.float32)
    k["k_mask"] = np.stack([t_ >= s_, s_ >= t_], 1).astype(np.float32)
    k["k_zpos"] = np.stack([P - 1 - pos, pos], 1).astype(np.float32)
    tok = np.arange(SAMPLE)
    inv = np.float32(10000.0) ** (-np.arange(HD // 4, dtype=np.float32) / np.float32(HD // 4))
    ang = np.concatenate([(tok // 64).astype(np.float32)[:, None] * inv, (tok % 64).astype(np.float32)[:, None] * inv], 1)
    c, s = np.repeat(np.cos(ang), 2, 1), np.repeat(np.sin(ang), 2, 1)
    s[:, 0::2] *= -1
    k["k_rope"] = np.ascontiguousarray(np.stack([c, s]).reshape(2, NS, P, HD).transpose(2, 0, 1, 3)).astype(np.float32)
    return k


_INS = ["x_prompt", "x_sample", "c", "cache_attn_k", "cache_attn_v", "state_ret", "state_ssm_re", "state_ssm_im", "c_ctx",
        "w_ada", "b_ada", "norm1_g", "norm2_g", "w_in", "ret_lg_f", "ret_lg_b", "ret_norm_g", "w_ret_out",
        "att_q_norm_g", "att_k_norm_g", "w_att_out", "a_re_f", "a_im_f", "a_re_b", "a_im_b", "log_dt_f", "log_dt_b",
        "ssm_b_re", "ssm_b_im", "ssm_c_re", "ssm_c_im", "ssm_d", "w_glu", "w_out", "w_router", "b_router",
        "w_gate", "w_up", "w_down", "final_norm_g"]
_OUTS = {"y_prompt": (1, PROMPT, D), "y_sample": (1, SAMPLE, D), "new_k": (1, 1, PROMPT, KVH, HD),
         "new_v": (1, 1, PROMPT, KVH, HD), "new_ret": (1, 1, 2, RH, P, P), "new_re": (1, 1, 2, G, PS), "new_im": (1, 1, 2, G, PS)}


def kernel(**inputs):
    import concourse.bacc as bacc
    from concourse.bass_utils import run_bass_kernel_spmd

    nc = bacc.Bacc("TRN2", target_bir_lowering=False, num_devices=1)
    arrays = {name: np.ascontiguousarray(inputs[name]) for name in _INS}
    arrays.update(constants())
    aps = {name: nc.dram_tensor(name, x.shape, mybir.dt.from_np(x.dtype), kind="ExternalInput").ap() for name, x in arrays.items()}
    for name, shape in _OUTS.items():
        aps[name] = nc.dram_tensor(name, shape, F32, kind="ExternalOutput").ap()
    build(nc, aps)
    got = run_bass_kernel_spmd(nc, [arrays], core_ids=[0]).results[0]
    return tuple(got[name] for name in _OUTS)
```

```python
import numpy as np
import concourse.bass as bass
from concourse import mybir
from contextlib import ExitStack

F32 = mybir.dt.float32
I32 = mybir.dt.int32
U32 = mybir.dt.uint32
ALU = mybir.AluOpType
ACT = mybir.ActivationFunctionType
AX = mybir.AxisListType

P = 128
D = 1024
KD = D // P
SAMPLE, PROMPT = 512, 128
T = SAMPLE + PROMPT
NT = T // P
NS = SAMPLE // P
RH, RW = 4, 512
AH, KVH, HD = 8, 2, 64
QK_W = (AH + KVH) * HD
KEYS = SAMPLE + PROMPT
G, PS, GI = 32, 64, 16
GH_, GPH = G // 2, G // 4
GP = G // 2
Q = 8
CS, CP_ = SAMPLE // Q, PROMPT // Q
NC = CS + CP_
SC = CS + 1 + CP_ + 1
NE, NG, EG = 16, 4, 4
FF = 512
CAP = 128
PASSES = T // CAP
EPS = 1e-6
COL_RQ, COL_RK, COL_RV, COL_RG, COL_AQ, COL_KV, COL_SU, COL_G = 0, 512, 1024, 1536, 2048, 2560, 2816, 3328
MAGIC = 12582912.0
LN2_HI, LN2_LO = 0.693359375, -2.12194440e-4
TWO_PI_A, TWO_PI_B = 6.28125, 0.0019350051879882812
TWO_PI_C = float(2 * np.pi - 6.28125 - 0.0019350051879882812)
EXP_C = [1 / 5040., 1 / 720., 1 / 120., 1 / 24., 1 / 6., 0.5, 1.0]


def build(nc, a, STOP=99):
    ctx = ExitStack()
    sem = lambda name: ctx.enter_context(nc.semaphore(name))

    used = [0]

    def sb(name, shape, dt=F32):
        return ctx.enter_context(nc.sbuf_tensor(name, shape, dt))

    ident = sb("ident", [P, P])
    upper = sb("upper", [P, P])
    ones = sb("ones", [P, P])
    sel = sb("sel", [P, 2, P])
    small = sb("small", [P, 256])
    cS = sb("cS", [P, KD, 32])
    wring = sb("wring", [P, 2, KD, 512])
    HT = sb("HT", [P, KD, T])
    REG = sb("REG", [P, 38740])

    class Region:
        def __init__(self, at=0):
            self.at = at

        def take(self, *shape, parts=P, dt=F32):
            n = int(np.prod(shape))
            assert self.at + n <= 38740, self.at + n
            v = REG[0:parts, self.at:self.at + n]
            self.at += n
            if dt is not F32:
                v = v.bitcast(dt)
            if len(shape) > 1:
                names = "abcdef"[:len(shape)]
                v = v.rearrange(f"p ({' '.join(names)}) -> p {' '.join(names)}",
                                **{n_: s for n_, s in zip(names, shape)})
            return v

    YT = Region().take(4, T)
    r = Region(4 * T)
    RQT = r.take(RH, T)
    RKT = r.take(RH, T)
    RK = r.take(NT, RW)
    RV = r.take(NT, RW)
    RG = r.take(NT, RW)
    AQK_AT = r.at
    AQK = r.take(NT, QK_W)
    AV = r.take(NT, KVH * HD)
    OWN = r.at

    r = Region()
    X = r.take(NT, D)
    BC = r.take(2, 2, D)
    XN = r.take(2, D)
    SQ = r.take(D)
    cT = r.take(2, KD, 2)
    modrow = r.take(2, 512)
    bias_row = r.take(4, 512, parts=2)
    gain_row = r.take(D)
    assert r.at <= OWN

    r = Region(OWN)
    FM = r.take(2, 2, GPH, P)
    CPW = r.take(2, 2, GPH, 9, GI)
    TOE_AT = r.at
    TOE = r.take(GH_, P)
    U = r.take(GH_, NC)
    SY_AT = r.at
    S = r.take(Q * GH_ * GI)
    V_AT = r.at
    V = r.take(2, 2, GPH, SC)
    A8_AT = r.at
    A8 = r.take(GPH, SC)
    RT_AT = r.at
    RT = r.take(2, GPH, CS + 1)
    PAR = r.take(10, GPH)
    SC_ = [r.take(2, GPH) for _ in range(17)]
    SCI = r.take(2, GPH, dt=I32)
    SF = r.take(2, 2, GPH)
    r = Region(OWN)
    TMP4 = [r.take(GPH * SC) for _ in range(4)]
    Z = [r.take(GPH * SC) for _ in range(2)]
    assert r.at <= OWN + 4 * GPH * P
    r = Region(V_AT)
    FP = [r.take(GPH, Q, GI) for _ in range(2)]
    FPT = r.take(GPH, Q, GI)
    assert r.at <= RT_AT
    CTMP = Region(V_AT).take(GPH, 9, GI)
    KP = Region(V_AT).take(GH_, 2 * Q - 1, GI, parts=GI)
    SU = Region(TOE_AT).take(NT, 512)
    SRAW = Region(V_AT).take(Q, GH_, GI, parts=NC)
    SFO = Region(RT_AT).take(4, P, parts=GPH)
    RTT = Region(A8_AT).take(GPH * 32)
    r = Region(OWN)
    NAT = r.take(10, P, parts=GPH)
    CNAT = r.take(2, GH_, PS, parts=GI)
    LD = r.take(2, 2, parts=GPH)
    r = Region(SY_AT)
    CT = r.take(2, GPH, GI)
    BN = r.take(2, GPH, GI)
    BB = r.take(2, 2, GPH, GI)
    PW = r.take(2, 2, 9, GPH)
    BBT = r.take(GPH, GI)
    PWT = r.take(2 * 4 * GPH)
    DT_ = r.take(GH_, parts=GI)
    DG = r.take(GH_, GI, parts=GI)
    assert r.at <= V_AT

    r = Region(OWN)
    ROT = r.take(4, T)
    ATT = r.take(4, T)
    E4 = r.at
    ST = r.take(2, NS, RW)
    DEC = r.take(RH, P)
    XI = r.take(2, RH, P)
    ZETA = r.take(2, RH)
    CD = r.take(2, RH)
    LG = r.take(2, RH)
    DIST = r.take(4, P)
    MASK = r.take(2, P)
    ZPOS = r.take(2)
    RNG = r.take(RW)
    SS = r.take(2, RW)
    QX = r.take(2, 2, RH, P)
    VZ = r.take(2, RW)
    KVO = r.take(2, RW)
    RSS = r.take(3, NT * RH)
    KVT = r.take(RW)
    OALL = RK
    r = Region(E4)
    QTT = r.take(4, T)
    KTT = r.take(KEYS)
    KTP = r.take(P)
    CK = r.take(KVH * HD)
    CV = r.take(KVH * HD)
    PR = r.take(2, KEYS)
    PT = r.take(2, 5 * P)
    AO = r.take(2, RW)
    ROPE = r.take(2, NS, HD)
    QGL = r.take(2, HD)
    QG = r.take(AH + KVH, HD)
    QT1 = r.take(QK_W)
    QT2 = r.take(QK_W)
    QSS = r.take(3, NT * (AH + KVH))
    ASUM = r.take(NT, AH)
    AMAX = r.take(4)
    TG5_AT = r.at
    TG5 = r.take(NT, 512)
    TG = [REG[:, 4 * T + 2560 * j:4 * T + 2560 * (j + 1)].rearrange("p (t c) -> p t c", t=NT) for j in range(5)] + [TG5]

    r = Region(E4)
    MER = r.take(NT, D)
    MERT_AT = r.at
    MERT = r.take(KD, T)
    assert MERT_AT + KD * T <= TG5_AT + 2560
    r = Region(AQK_AT)
    MT1 = r.take(2, 512)
    MT2 = r.take(2, 512)
    r = Region(4 * T)
    X2 = r.take(NT, D)
    BC2 = r.take(4, 2, D)
    SLOT_AT = r.at
    modrow2 = r.take(2, 512)
    bias2 = r.take(8, 512, parts=2)
    gain2 = r.take(D)
    SQ2 = r.take(D)
    assert r.at <= MERT_AT
    r = Region(SLOT_AT)
    slots = [wring[:, j] for j in range(2)] + [r.take(KD, 512) for j in range(4)]
    WG = [slots[0], slots[3]]
    WU = [slots[1], slots[4]]
    WD = [x.rearrange("p k c -> p (k c)").rearrange("p (k c) -> p k c", k=4) for x in (slots[2], slots[5])]
    HTF = HT[:].rearrange("p k t -> p (k t)")
    ROWS2 = HTF[:, 0:2048].rearrange("p (b c) -> p b c", b=2)
    COLS2 = HTF[:, 2048:4096].rearrange("p (b k t) -> p b k t", b=2, k=KD)
    TH = HTF[:, 4096:4608]
    r0 = Region(0)
    HID = r0.take(2, 512)
    HIDT = r0.take(2, 512)
    MISC_AT = r.at
    OUT = r.take(2, D)
    YR = r.take(2, 2, D)
    WR = r.take(KD, NE)
    BR = r.take(NE)
    IOTA = r.take(NE)
    TOK = r.take(NT, dt=I32)
    WP = r.take(2, NT)
    PACE = r.take(27)
    ROUTE = r.take(14, NT)
    CIDX = r.take(NT, 2, dt=I32)
    IDX = r.take(NE, dt=I32)
    TOP_COUNT = r.take(1, dt=I32)
    r = Region(0)
    LOGIT, PROB, TMPR, EQ, M1, M2, MB, RANK = [r.take(NT, NE) for _ in range(8)]
    GH = [r.take(NT, NG) for _ in range(8)]
    ZERO = r.take(NE * T // P, dt=I32)
    COMB_STEPS = 2 * 9 + 4 * NT
    SQ2F = ROWS2[:, 0, :]
    FG = COLS2[:, 0].rearrange("p k t -> p (k t)")

    banks = ctx.enter_context(nc.psum_tensor("banks", [P, 8, 512], F32))

    phase = sem("phase_joined")
    consts_in = sem("consts_in")
    c_in = sem("c_in")
    x_in = sem("x_in")
    rows_in = sem("rows_in")
    w_in0, w_in1 = sem("w_slot0_loaded"), sem("w_slot1_loaded")
    w_used = sem("w_blocks_used")
    full_d, free_d = sem("psum_full_for_vector"), sem("psum_emptied_by_vector")
    full_a, free_a = sem("psum_full_for_scalar"), sem("psum_emptied_by_scalar")
    full_p, free_p = sem("projection_full"), sem("projection_emptied")
    full_g, free_g = sem("gate_block_full"), sem("gate_block_emptied")
    f_ready, f_done = sem("s5_input_matrices_ready"), sem("s5_input_matrices_turned")
    cpw_ready, kp_ready, s_chunks = sem("s5_output_powers_ready"), sem("s5_lag_kernels_ready"), sem("s5_chunks_ready")
    ang_ready, sin_ready = sem("s5_angles_ready"), sem("s5_sines_ready")
    sraw_in, xi_ready, sf_ready = sem("s5_chunks_in"), sem("s5_states_ready"), sem("s5_final_states_ready")
    bn_in, su_out, state_out = sem("s5_b_in"), sem("s5_channels_stored"), sem("states_stored")
    s5_done = sem("s5_half_done")
    bc_ready = sem("modulation_spread")
    dve_step, act_step, pool_step = sem("dve_step"), sem("act_step"), sem("pool_step")
    tanh_c, silu_c = sem("tanh_c_ready"), sem("silu_c_ready")
    sq_ready = sem("squares_summed")
    mod_ready = sem("mod_row_ready")
    xn_ready, xn_used = sem("xn_tile_ready"), sem("xn_tile_transposed")
    par_in = sem("s5_parameters_in")
    nat_ready = sem("s5_natural_ready")
    a2d = sem("scalar_result_for_vector")
    d2a = sem("vector_result_for_scalar")
    d2p = sem("vector_result_for_tensor")
    scr = sem("scratch_written")
    scr_in = sem("scratch_read")
    toe_in = sem("toeplitz_copied")
    out_done = sem("outputs_written")
    ret_in = sem("retention_inputs_in")
    ret_exp = sem("decays_ready")
    vz_ready, kv_done = sem("decayed_values_ready"), sem("new_states_ready")
    kvo_ready = sem("context_states_ready")
    sd_ready = sem("decayed_scores_ready")
    ro_gate, ro_ready = sem("retention_gate_tanh"), sem("retention_rows_ready")
    att_in = sem("attention_inputs_in")
    qk_ready = sem("queries_keys_ready")
    kv_out = sem("context_keys_ready")
    s_full, s_max, p_ready = sem("scores_full"), sem("maximum_ready"), sem("probabilities_ready")
    pt_full, pt_ready = sem("probabilities_transposed"), sem("transposed_probabilities_ready")
    o_full, ao_ready, aot_full, aot_ready = sem("attention_out_full"), sem("attention_rows_ready"), sem("attention_rows_transposed"), sem("attention_columns_ready")
    mer_step = sem("gated_tiles_added")
    tg_ready = sem("gate_tanh_ready")
    mer_ready = sem("merged_ready")
    tb_ready, tb_used = sem("glu_tanh_ready"), sem("glu_tanh_used")
    route_in, h2_ready, h2_out, h2t_ready = sem("router_inputs_in"), sem("normed_row_ready"), sem("normed_row_stored"), sem("normed_columns_ready")
    exp_ready, masks_ready, pos_ready, pos_out, zero_ready, zero_out = (sem(n) for n in (
        "router_exponentials", "choice_masks_ready", "positions_ready", "tokens_listed", "zero_ready", "lists_zeroed"))
    idx_in = sem("token_lists_in")
    g_in = [sem("rows_gathered0"), sem("rows_gathered1")]
    wg_in = [sem("gate_weights_in0"), sem("gate_weights_in1")]
    wu_in = [sem("up_weights_in0"), sem("up_weights_in1")]
    wd_in = [sem("down_weights_in0"), sem("down_weights_in1")]
    g_t, gt_d, gt_a = sem("rows_transposed"), sem("columns_by_vector"), sem("columns_by_scalar")
    gate_full, up_full, th_ready, hid_ready = sem("gate_full"), sem("up_full"), sem("gate_tanh"), sem("hidden_ready")
    ht_full, ht_ready, dn0, dn1 = sem("hidden_transposed"), sem("hidden_columns_ready"), sem("down_half0_full"), sem("down_half1_full")
    out_d, out_a = sem("expert_out_by_vector"), sem("expert_out_by_scalar")
    out_wr = [sem("expert_rows_stored0"), sem("expert_rows_stored1")]
    hid_step, comb_step = sem("hidden_step"), sem("combine_step")
    cidx_ready, y_in, combined = sem("row_places_ready"), [sem("expert_rows_in0"), sem("expert_rows_in1")], sem("tiles_combined")
    fin_in, fin_sq, fin_ready = sem("final_gain_in"), sem("final_squares"), sem("final_rows_ready")
    x2_in, x2_ready = sem("residual_in"), sem("residual_ready")

    def engine_tools(eng, step):
        count = [0]

        def done(ins):
            count[0] += 1
            ins.then_inc(step, 1)
            eng.wait_ge(step, count[0])
        return done

    def phase_end(eng, n):
        eng.sem_inc(phase, 1)
        eng.wait_ge(phase, 5 * (n + 1))

    def at_least(eng, s, n):
        if not isinstance(n, int) or n > 0:
            eng.wait_ge(s, n)

    def expert_pipeline(eng, r, begin, end):
        def turn(e):
            last = None if isinstance(e, int) and e == 0 else lambda: end(16 * r + e - 1, 8 * r + i - 1, e - 1, 1)
            begin(16 * r + e, 8 * r + i, e, 0, last)
            begin(16 * r + e + 1, 8 * r + i, e + 1, 1, lambda: end(16 * r + e, 8 * r + i, e, 0))

        for i in range(2):
            turn(2 * i)
        with eng.Fori(2, NE // 2) as i:
            turn(2 * i)
        end(16 * r + 15, 8 * r + 7, 15, 1)

    def all_passes(eng, one_pass):
        one_pass(0)
        most = eng.value_load(TOP_COUNT[0:1, 0:1], min_val=0, max_val=T)
        with eng.If(most > CAP):
            with eng.Fori(1, PASSES) as r:
                one_pass(r)

    class Bank:

        def __init__(self, first, depth, full, free):
            self.first, self.depth, self.full, self.free, self.k = first, depth, full, free, 0

        def bank(self):
            return banks[:, self.first + self.k % self.depth, :]

        def open(self, pe):
            if self.k >= self.depth:
                pe.wait_ge(self.free, self.k - self.depth + 1)
            return self.bank()

        def close(self, last):
            last.then_inc(self.full, 1)
            self.k += 1

        def take(self, eng):
            eng.wait_ge(self.full, self.k + 1)
            return self.bank()

        def give(self, last):
            last.then_inc(self.free, 1)
            self.k += 1

        def all_emptied(self, pe):
            if self.k:
                pe.wait_ge(self.free, self.k)

    w_ada, w_in = a["w_ada"][0], a["w_in"][0]
    blocks = [(w_ada, D, 512 * n, 512) for n in range(4)]
    blocks += [(w_in, D, c, 512) for c in (COL_SU, COL_RQ, COL_RK, COL_RV, COL_RG, COL_AQ)] + [(w_in, D, COL_KV, 256)]
    blocks += [(w_in, D, COL_G + D * branch + 512 * n, 512) for n in range(2) for branch in range(3)]
    FIRST_MERGE_BLOCK = len(blocks)
    for n in range(2):
        blocks += [(a["w_ret_out"][0], 512, 512 * n, 512), (a["w_att_out"][0], 512, 512 * n, 512)]
        blocks += [(a["w_glu"][0], 512, 512 * n, 512), (a["w_glu"][0], 512, D + 512 * n, 512)]
    ada = lambda n: (w_ada, D, 512 * n, 512)
    w_out = a["w_out"][0]
    FIRST_LAST_BLOCK = len(blocks)
    blocks += [ada(4), ada(5), (w_out, D, 0, 512), ada(6), ada(7), (w_out, D, 512, 512), ada(8), ada(9), ada(10), ada(11)]

    scratch_h2 = nc.dram_tensor("scratch_h2", (T, D), F32).ap()
    scratch_out = nc.dram_tensor("scratch_out", (NE * CAP, D), F32).ap()
    lists = nc.dram_tensor("token_lists", (NE * T, 1), I32).ap()
    scratch_su = nc.dram_tensor("scratch_su", (T, 512), F32).ap()

    LAST_ORDER = (4, 5, None, 6, 7, None, 8, 9, 10, 11)
    ORDER = (("params", 0), ("modulate", 0), ("su", 0), ("F", 0), 3, ("K", 0), 3, ("U", 0), ("V", 0), 10, ("Y", 0), 1, ("out", 0),
             ("params", 1), 4, ("F", 1), 4, ("K", 1), 1, ("U", 1), ("V", 1), 7, ("Y", 1), ("out", 1))
    PROJ_TILES = 8 + 5 * NT
    assert sum(x for x in ORDER if isinstance(x, int)) == PROJ_TILES

    KV_ORDER = ((0, 0), (1, 3), (0, 1), (1, 2), (0, 2), (1, 1), (0, 4), (1, 4))
    FULL_A_BEFORE_LAST = 8 + 2 * (8 + 3 + 4 + 4) + NT + NT + 2 * NT + NT

    block = ctx.enter_context(nc.Block())

    @block.sync
    def _(sp):
        for t, src in ((ident, "k_ident"), (upper, "k_upper"), (sel, "k_sel")):
            sp.dma_start(t[:], a[src]).then_inc(consts_in, 16)
        sp.dma_start(cT[:, 0, :, 0], a["c"].rearrange("o (k p) -> p (o k)", p=P), allow_slow_non_contiguous=True).then_inc(c_in, 16)
        sp.dma_start(cT[:, 0, :, 1], a["c_ctx"].rearrange("(k p) -> p k", p=P), allow_slow_non_contiguous=True).then_inc(c_in, 16)
        n_loaded = [0]

        def load_block():
            n = n_loaded[0]
            n_loaded[0] += 1
            w, rows, c0, cols = blocks[n]
            if n >= 2:
                sp.wait_ge(w_used, n - 1)
            sp.dma_start(wring[:, n % 2, 0:rows // P, 0:cols],
                         w[0:rows, c0:c0 + cols].rearrange("(k p) c -> p k c", p=P)).then_inc((w_in0, w_in1)[n % 2], 16)

        load_block()
        load_block()
        for t in range(NT):
            src = a["x_sample"][0, P * t:P * (t + 1), :] if t < NS else a["x_prompt"][0]
            sp.dma_start(X[:, t, :], src).then_inc(x_in, 16)
        for s in range(2):
            sp.dma_start(bias_row[s:s + 1], a["b_ada"].rearrange("o (n c) -> o n c", n=12)[:, 0:4, :]).then_inc(rows_in, 16)
        sp.dma_start(gain_row, a["norm1_g"].broadcast_to([P, D])).then_inc(rows_in, 16)
        while n_loaded[0] < 11:
            load_block()
        phase_end(sp, 0)
        phase_end(sp, 1)
        while n_loaded[0] < FIRST_MERGE_BLOCK:
            load_block()
        phase_end(sp, 2)
        while n_loaded[0] < FIRST_LAST_BLOCK:
            load_block()
        phase_end(sp, 3)
        for t in range(NT):
            src = a["x_sample"][0, P * t:P * (t + 1), :] if t < NS else a["x_prompt"][0]
            sp.dma_start(X2[:, t, :], src).then_inc(x2_in, 16)
        for s in range(2):
            sp.dma_start(bias2[s:s + 1], a["b_ada"].rearrange("o (n c) -> o n c", n=12)[:, 4:12, :]).then_inc(x2_in, 16)
        sp.dma_start(gain2, a["norm2_g"].broadcast_to([P, D])).then_inc(x2_in, 16)
        while n_loaded[0] < len(blocks):
            load_block()
        phase_end(sp, 4)
        if STOP <= 4:
            return
        n_out = 0
        sp.dma_start(WR, a["w_router"].rearrange("(k p) e -> p k e", p=P)).then_inc(route_in, 16)
        sp.dma_start(BR, a["b_router"].rearrange("(o e) -> o e", o=1).broadcast_to([P, NE])).then_inc(route_in, 16)
        sp.dma_start(IOTA, a["k_iota"]).then_inc(route_in, 16)
        sp.dma_start(TOK, a["k_tok"]).then_inc(route_in, 16)
        sp.wait_ge(zero_ready, 1)
        sp.dma_start(lists.rearrange("(p c) o -> p (c o)", p=P), ZERO).then_inc(zero_out, 16)
        for t in range(NT):
            sp.wait_ge(h2_ready, t + 1)
            sp.dma_start(scratch_h2[P * t:P * t + P, :], ROWS2[:, t % 2, :]).then_inc(h2_out, 16)
            sp.wait_ge(h2_out, 16 * (t + 1))
        phase_end(sp, 5)
        if STOP <= 5:
            return

        def weights_in(n, m, e, b):
            at_least(sp, up_full, n - 1)
            sp.dma_start(WG[b], a["w_gate"][0][e].rearrange("(k p) c -> p k c", p=P)).then_inc(wg_in[b], 16)
            sp.dma_start(WU[b], a["w_up"][0][e].rearrange("(k p) c -> p k c", p=P)).then_inc(wu_in[b], 16)
            at_least(sp, dn1, n - 1)
            sp.dma_start(WD[b], a["w_down"][0][e].rearrange("(k p) c -> p k c", p=P)).then_inc(wd_in[b], 16)

        def sp_pass(r):
            if not isinstance(r, int):
                sp.wait_ge(combined, NT * r)
            for k in range(2):
                sp.dma_start(IDX[:, 8 * k:8 * k + 8], lists.rearrange("(e r) o -> r (e o)", r=T)[bass.ds(CAP * r, CAP), 8 * k:8 * k + 8],
                             allow_slow_non_contiguous=True).then_inc(idx_in, 16)
            for e in range(2):
                weights_in(16 * r + e, 8 * r, e, e)
            with sp.Fori(1, NE // 2) as i:
                for b in range(2):
                    weights_in(16 * r + 2 * i + b, 8 * r + i, 2 * i + b, b)

        all_passes(sp, sp_pass)
        phase_end(sp, 6)
        if STOP <= 6:
            return
        sp.dma_start(FG, a["final_norm_g"].rearrange("(o e) -> o e", o=1).broadcast_to([P, D])).then_inc(fin_in, 16)
        for t in range(NT):
            sp.wait_ge(fin_ready, t + 1)
            dst = a["y_sample"][0, P * t:P * (t + 1), :] if t < NS else a["y_prompt"][0]
            sp.dma_start(dst, X2[:, t, :]).then_inc(out_done, 16)
        n_out += NT
        sp.wait_ge(out_done, 16 * n_out)

    @block.tensor
    def _(pe):
        vec, sca = Bank(0, 4, full_d, free_d), Bank(4, 2, full_a, free_a)
        pro, gat = Bank(6, 2, full_p, free_p), Bank(7, 1, full_g, free_g)
        wcount = [0]
        mm = nc.tensor.matmul

        def all_emptied():
            vec.all_emptied(pe)
            sca.all_emptied(pe)

        def weights():
            n = wcount[0]
            wcount[0] += 1
            pe.wait_ge((w_in0, w_in1)[n % 2], 16 * (n // 2 + 1))
            return wring[:, n % 2]

        def weights_used(bank):
            pe.wait_ge(bank.full, bank.k)
            pe.sem_inc(w_used, 1)

        def transposes(chan, blocks_):
            out = chan.open(pe)
            for j, src in enumerate(blocks_):
                last = nc.tensor.transpose(out[:, P * j:P * j + P], src, ident[:])
            chan.close(last)

        def ada_block(n):
            w = weights()
            out = vec.open(pe)
            for k in range(KD):
                j = k % 4
                last = mm(out[32 * j:32 * j + 32, :], cS[:, k, :], w[:, k, :], start=k < 4, stop=k >= 4)
            vec.close(last)
            weights_used(vec)
            pe.wait_ge(mod_ready, n + 1)
            for s in range(2):
                out = sca.open(pe)
                row = modrow if n < 4 else modrow2
                sca.close(mm(out, sel[:, s, :], row[:, n % 2, :], start=True, stop=True))

        def project(out, w, t, cols=512):
            for k in range(KD):
                last = mm(out[:, 0:cols], HT[:, k, P * t:P * t + P], w[:, k, 0:cols], start=k == 0, stop=k == KD - 1)
            return last

        proj = [0, None]

        def tiles(count):
            for _ in range(count):
                i = proj[0]
                proj[0] += 1
                if i == 0 or i >= 8 and (i - 8) % NT == 0:
                    proj[1] = weights()
                out = pro.open(pe)
                if i < 8:
                    h, context = i // 2, i % 2
                    cols = slice(SAMPLE, T) if context else slice(0, SAMPLE)
                    for k in range(KD):
                        last = mm(out[:, 0:PROMPT if context else SAMPLE], proj[1][:, k, P * h:P * h + P], HT[:, k, cols],
                                  start=k == 0, stop=k == KD - 1)
                else:
                    last = project(out, proj[1], (i - 8) % NT, 512 if i < 8 + 4 * NT else 256)
                pro.close(last)
                if i == 7 or i > 8 and (i - 8) % NT == NT - 1:
                    weights_used(pro)

        def modulate(_):
            pe.wait_ge(silu_c, 1)
            for n in range(4):
                ada_block(n)
            for t in range(NT):
                pe.wait_ge(xn_ready, t + 1)
                for half in range(2):
                    transposes(vec, [XN[:, t % 2, P * k:P * k + P] for k in range(4 * half, 4 * half + 4)])
            vec.all_emptied(pe)

        def params(hf):
            pe.wait_ge(par_in, 16 * 15 * (hf + 1))
            pe.wait_ge(nat_ready, hf + 1)
            out = vec.open(pe)
            for j in range(10):
                last = nc.tensor.transpose(out[:, GPH * j:GPH * j + GPH], NAT[:, j, :], ident[0:GPH, 0:GPH])
            vec.close(last)
            for j in range(2):
                out = vec.open(pe)
                for p in range(GPH):
                    last = nc.tensor.transpose(out[:, 16 * p:16 * p + 16],
                                               CNAT[:, j, 2 * p:2 * p + 2, :].rearrange("o g p -> o (g p)"), ident[0:16, 0:16])
                vec.close(last)

        def turn_F(hf):
            for d in range(2):
                pe.wait_ge(f_ready, 2 * hf + d + 1)
                for j in range(2):
                    for q in range(2):
                        transposes(sca, [FP[j][:, 4 * q + p].rearrange("p s i -> p (s i)") for p in range(4)])

        def lag_kernels(hf):
            pe.wait_ge(cpw_ready, hf + 1)
            for d in range(2):
                for q in range(4):
                    out = vec.open(pe)
                    for j in range(4):
                        h, p = q % 2, 4 * (q // 2) + j
                        hs = slice(64 * h, 64 * h + 64)
                        for c in range(2):
                            last = mm(out[0:GI, P * j:P * j + P], BB[hs, d, c, p, :],
                                      CPW[hs, d, c, p, 0:Q, :].rearrange("p k o -> p (k o)"), start=c == 0, stop=c == 1)
                    vec.close(last)

        def su_rows(_):
            w = weights()
            for t in range(NT):
                pro.close(project(pro.open(pe), w, t))
            weights_used(pro)

        def turn_U(hf):
            pe.wait_ge(s_chunks, hf + 1)
            for q in range(3):
                gs = range(6 * q, min(6 * q + 6, GH_))
                out = sca.open(pe)
                for j, g in enumerate(gs):
                    last = nc.tensor.transpose(out[:, NC * j:NC * j + NC], S[0:NC, P * g:P * g + P], ident[0:NC, 0:NC])
                sca.close(last)
            sca.all_emptied(pe)

        def chunk_inputs(hf):
            for d in range(2):
                for c in range(2):
                    for q in range(2):
                        ps = range(6 * q, min(6 * q + 6, GPH))
                        out = vec.open(pe)
                        for j, p in enumerate(ps):
                            for h in range(2):
                                last = mm(out[64 * h:64 * h + 64, NC * j:NC * j + NC], FM[:, d, c, p, 64 * h:64 * h + 64],
                                          U[:, 2 * p + h, :], start=True, stop=True)
                        vec.close(last)

        def chunk_outputs(hf):
            pe.wait_ge(toe_in, 16 * Q * (hf + 1))
            pe.wait_ge(xi_ready, hf + 1)
            for q in range(4):
                out = sca.open(pe)
                for j in range(4):
                    h, p = q % 2, 4 * (q // 2) + j
                    g = 2 * p + h
                    hs = slice(64 * h, 64 * h + 64)
                    o = out[0:NC, P * j:P * j + P]
                    mm(o, U[:, g, :], TOE[:, g, :], start=True, stop=False)
                    for d in range(2):
                        for c in range(2):
                            xin = V[hs, d, c, :, :].rearrange("p a b -> p (a b)")[:, NC * p:NC * p + NC]
                            pw = CPW[hs, d, c, p, 1:Q + 1, :]
                            if d:
                                pw = pw[:, ::-1, :]
                            last = mm(o, xin, pw, start=False, stop=d + c == 2)
                sca.close(last)
            out = vec.open(pe)
            for j in range(4):
                last = mm(out[0:GPH, P * j:P * j + P], SF[:, j // 2, j % 2, :], ident[:], start=True, stop=True)
            vec.close(last)

        def turn_outputs_s5(hf):
            sca.all_emptied(pe)
            Y = S[0:NC, :].rearrange("c (t f) -> c t f", t=Q)
            for kb in range(2):
                for th in range(2):
                    out = sca.open(pe)
                    for j in range(4):
                        last = nc.tensor.transpose(out[:, NC * j:NC * j + NC], Y[:, 4 * th + j, P * kb:P * kb + P], ident[0:NC, 0:NC])
                    sca.close(last)

        pe.wait_ge(consts_in, 48)
        steps = dict(params=params, modulate=modulate, su=su_rows, F=turn_F, K=lag_kernels, U=turn_U, V=chunk_inputs, Y=chunk_outputs,
                     out=turn_outputs_s5)
        for step in ORDER:
            if isinstance(step, int):
                tiles(step)
            else:
                steps[step[0]](step[1])
        phase_end(pe, 0)
        if STOP <= 0:
            return

        for t in range(NT):
            transposes(vec, [RK[:, t, P * h:P * h + P] for h in range(RH)])
        for i, (d, t) in enumerate(KV_ORDER):
            pe.wait_ge(vz_ready, i + 1)
            out = vec.open(pe)
            for h in range(RH):
                hs = slice(P * h, P * h + P)
                last = mm(out[:, hs], RK[:, t, hs], VZ[:, i % 2, hs], start=True, stop=True)
            vec.close(last)
        pe.wait_ge(kv_done, len(KV_ORDER))
        for t in range(NT):
            ts_ = slice(P * t, P * t + P)
            out = vec.open(pe)
            for h in range(RH):
                last = mm(out[:, P * h:P * h + P], RKT[:, h, ts_], RQT[:, h, ts_], start=True, stop=True)
            vec.close(last)
            pe.wait_ge(sd_ready, t + 1)
            out = vec.open(pe)
            for h in range(RH):
                hs = slice(P * h, P * h + P)
                last = mm(out[:, hs], SS[:, t % 2, hs], RV[:, t, hs], start=True, stop=t == NS)
                if t < NS:
                    for d in range(2):
                        last = mm(out[:, hs], QX[:, t % 2, d, h, :], ST[:, d, t, hs], start=False, stop=d == 1)
            vec.close(last)
        for t in range(NT):
            pe.wait_ge(ro_ready, t + 1)
            transposes(sca, [OALL[:, t, P * h:P * h + P] for h in range(RH)])
        phase_end(pe, 1)
        if STOP <= 1:
            return

        pe.wait_ge(qk_ready, 1)
        for t in range(NT):
            transposes(sca, [AQK[:, t, P * b:P * b + P] for b in range(4)])
        transposes(vec, [AQK[:, t, 512:640] for t in range(NS)])
        transposes(vec, [CK, AQK[:, NS, 512:640]])
        all_emptied()
        flat = banks[:].rearrange("p b c -> p (b c)")
        units = [(t, b, half) for t in range(NT) for b in range(4) for half in range(2)]

        def keys_of(t):
            return KEYS if t < NS else P

        gate = [0, None]

        def gate_tile():
            i = gate[0]
            gate[0] += 1
            if i % NT == 0:
                gate[1] = weights()
            gat.close(project(gat.open(pe), gate[1], i % NT))
            if i % NT == NT - 1:
                weights_used(gat)

        def scores(i):
            t, b, half = units[i]
            if i >= 2:
                pe.wait_ge(p_ready, i - 1)
            hs = slice(64 * half, 64 * half + 64)
            q = QTT[hs, b, P * t:P * t + P]
            at = 1024 * half
            if t < NS:
                mm(flat[:, at:at + 512], q, KTT[hs, 0:512], start=True, stop=True)
                last = mm(flat[:, at + 512:at + 640], q, KTT[hs, 512:640], start=True, stop=True)
            else:
                last = mm(flat[:, at:at + P], q, KTP[hs, :], start=True, stop=True)
            last.then_inc(s_full, 1)

        def turn_probabilities(i):
            t = units[i][0]
            pe.wait_ge(p_ready, i + 1)
            if i >= 1:
                pe.wait_ge(pt_ready, i)
            if turned[0]:
                pe.wait_ge(aot_ready, turned[0])
            for c in range(keys_of(t) // P):
                last = nc.tensor.transpose(flat[:, 2048 + P * c:2048 + P * c + P], PR[:, i % 2, P * c:P * c + P], ident[:])
            last.then_inc(pt_full, 1)

        def values(i):
            t, b, half = units[i]
            pe.wait_ge(pt_ready, i + 1)
            if b == half == 0 and t >= 1:
                pe.wait_ge(ao_ready, t)
            head = b + 4 * half
            n = keys_of(t) // P
            for c in range(n):
                if t < NS:
                    v = AV[:, c, :] if c < NS else CV
                else:
                    v = AV[:, NS, :]
                last = mm(banks[:, 6, 64 * head:64 * head + 64], PT[:, i % 2, P * c:P * c + P],
                          v[:, 64 * half:64 * half + 64], start=c == 0, stop=c == n - 1)
            last.then_inc(o_full, 1)

        def turn_outputs(t):
            pe.wait_ge(ao_ready, t + 1)
            pe.wait_ge(pt_ready, 8 * t + (8 if t == NT - 1 else 11))
            turned[0] = t + 1
            for b in range(4):
                last = nc.tensor.transpose(banks[:, 4, P * b:P * b + P], AO[:, t % 2, P * b:P * b + P], ident[:])
            last.then_inc(aot_full, 1)

        turned = [0]
        scores(0)
        for i in range(len(units)):
            if i + 1 < len(units):
                scores(i + 1)
            if i % 4 != 3:
                gate_tile()
            turn_probabilities(i)
            if i >= 1:
                values(i - 1)
            if i % 8 == 2 and i > 8:
                turn_outputs(i // 8 - 1)
        values(len(units) - 1)
        turn_outputs(NT - 1)
        phase_end(pe, 2)
        if STOP <= 2:
            return

        for n in range(2):
            for branch, x in enumerate((ROT, ATT, YT)):
                chans = (vec,) if branch < 2 else (vec, sca)
                ws = [weights() for _ in chans]
                for t in range(NT):
                    for chan, w in list(zip(chans, ws))[::-1]:
                        out = chan.open(pe)
                        for k in range(4):
                            last = mm(out, x[:, k, P * t:P * t + P], w[:, k, :], start=k == 0, stop=k == 3)
                        chan.close(last)
                for _ in chans:
                    weights_used(vec)
        for t in range(NT):
            pe.wait_ge(mer_ready, t + 1)
            for half in range(2):
                transposes((vec, sca)[half], [MER[:, t, P * k:P * k + P] for k in range(4 * half, 4 * half + 4)])
        phase_end(pe, 3)
        if STOP <= 3:
            return

        def project_out():
            w = weights()
            for t in range(NT):
                out = vec.open(pe)
                for k in range(KD):
                    last = mm(out, MERT[:, k, P * t:P * t + P], w[:, k, :], start=k == 0, stop=k == KD - 1)
                vec.close(last)
            weights_used(vec)

        for step in LAST_ORDER:
            project_out() if step is None else ada_block(step)
        phase_end(pe, 4)
        if STOP <= 4:
            return

        pe.wait_ge(route_in, 64)
        for t in range(NT):
            pe.wait_ge(h2_ready, t + 1)
            for half in range(2):
                transposes((vec, sca)[half], [ROWS2[:, t % 2, P * k:P * k + P] for k in range(4 * half, 4 * half + 4)])
            all_emptied()
            out = vec.open(pe)
            for k in range(KD):
                last = mm(out[:, 0:NE], COLS2[:, t % 2, k, :], WR[:, k, :], start=k == 0, stop=k == KD - 1)
            vec.close(last)
        pe.wait_ge(masks_ready, 1)
        out = vec.open(pe)
        for t in range(NT):
            for j in range(t + 1):
                mm(out[:, NE * t:NE * t + NE], upper[:] if j == t else ones[:], MB[:, j, :], start=j == 0, stop=j == t)
        for j in range(NT):
            last = mm(out[:, NE * NT:NE * NT + NE], ones[:], MB[:, j, :], start=j == 0, stop=j == NT - 1)
        vec.close(last)
        phase_end(pe, 5)
        if STOP <= 5:
            return

        def down(n, m, e, b):
            pe.wait_ge(hid_ready, n + 1)
            at_least(pe, ht_ready, n)
            for k in range(4):
                last = nc.tensor.transpose(banks[:, 4, P * k:P * k + P], HID[:, b, P * k:P * k + P], ident[:])
            last.then_inc(ht_full, 1)
            pe.wait_ge(ht_ready, n + 1)
            pe.wait_ge(wd_in[b], 16 * m + 16)
            for half, (full, emptied) in enumerate(((dn0, out_d), (dn1, out_a))):
                at_least(pe, emptied, n)
                for k in range(4):
                    last = mm(banks[:, 5 + half, :], HIDT[:, b, P * k:P * k + P], WD[b][:, k, 512 * half:512 * half + 512],
                              start=k == 0, stop=k == 3)
                last.then_inc(full, 1)

        def gate_up(n, m, e, b, before):
            pe.wait_ge(g_in[b], 16 * m + 16)
            at_least(pe, gt_d, n)
            at_least(pe, gt_a, n)
            for k in range(KD):
                last = nc.tensor.transpose(banks[:, k // 4, P * (k % 4):P * (k % 4) + P], ROWS2[:, b, P * k:P * k + P], ident[:])
            last.then_inc(g_t, 1)
            if before:
                before()
            pe.wait_ge(gt_d, n + 1)
            pe.wait_ge(gt_a, n + 1)
            at_least(pe, hid_ready, n)
            for bank, w, w_in_, full in ((2, WG, wg_in, gate_full), (3, WU, wu_in, up_full)):
                pe.wait_ge(w_in_[b], 16 * m + 16)
                for k in range(KD):
                    last = mm(banks[:, bank, :], COLS2[:, b, k, :], w[b][:, k, :], start=k == 0, stop=k == KD - 1)
                last.then_inc(full, 1)

        all_passes(pe, lambda r: expert_pipeline(pe, r, gate_up, down))
        phase_end(pe, 6)

    @block.scalar
    def _(act):
        sca = Bank(4, 2, full_a, free_a)
        pro, gat = Bank(6, 2, full_p, free_p), Bank(7, 1, full_g, free_g)
        act_done = engine_tools(act, act_step)
        A = nc.scalar.activation
        four = lambda x: x.rearrange("p (a b) -> p a b", a=4)

        def copy_out(dst):
            src = sca.take(act)
            sca.give(A(dst, src, ACT.Copy))

        act.wait_ge(c_in, 32)
        A(cT[:, 1], cT[:, 0], ACT.Tanh, scale=0.5).then_inc(tanh_c, 1)

        def params(hf):
            act.wait_ge(ang_ready, hf + 1)
            act_done(A(SC_[4], SC_[3], ACT.Sin))
            A(SC_[5], SC_[3], ACT.Sin, scale=0.5).then_inc(sin_ready, 1)

        def modulate(_):
            for t in range(NT):
                act.wait_ge(x_in, 16 * NT)
                act_done(A(SQ, X[:, t, :], ACT.Square, accum_out=small[:, t:t + 1]))
            act.sem_inc(sq_ready, 1)
            for n in range(4):
                for s in range(2):
                    copy_out(BC[:, n // 2, s, 512 * (n % 2):512 * (n % 2) + 512])
            act.wait_ge(free_a, sca.k)
            act.sem_inc(bc_ready, 1)

        def turn_F(hf):
            for d in range(2):
                for j in range(2):
                    for q in range(2):
                        src = sca.take(act)
                        sca.give(A(FM[:, d, j, 4 * q:4 * q + 4, :], four(src), ACT.Copy))
                act.wait_ge(free_a, sca.k)
                act.sem_inc(f_done, 1)

        def su_rows(_):
            for t in range(NT):
                src = pro.take(act)
                pro.give(A(SU[:, t, :], src, ACT.Copy))
                act.wait_ge(free_p, pro.k)
                act.sem_inc(scr, 1)

        def turn_U(hf):
            for q in range(3):
                n = min(6, GH_ - 6 * q)
                src = sca.take(act)
                sca.give(A(U[:, 6 * q:6 * q + n, :], src[:, 0:NC * n].rearrange("p (a b) -> p a b", a=n), ACT.Copy))

        def chunk_outputs(hf):
            Y = S[0:NC, :].rearrange("c (t g o) -> c g t o", t=Q, g=GH_)
            for q in range(4):
                src = sca.take(act)
                sca.give(A(Y[:, 8 * (q // 2) + q % 2:8 * (q // 2) + 8:2], src[0:NC].rearrange("c (g t o) -> c g t o", g=4, t=Q),
                           ACT.Gelu_apprx_tanh))

        def turn_outputs_s5(hf):
            for kb in range(2):
                for th in range(2):
                    src = sca.take(act)
                    dst = YT[:, 2 * hf + kb, :].rearrange("p (c t) -> p t c", t=Q)[:, 4 * th:4 * th + 4, :]
                    sca.give(A(dst, src[:, 0:4 * NC].rearrange("p (t c) -> p t c", t=4), ACT.Copy))
            act.wait_ge(free_a, sca.k)
            act.sem_inc(s5_done, 1)

        proj = [0]

        def tiles(count):
            for _ in range(count):
                i = proj[0]
                proj[0] += 1
                src = pro.take(act)
                if i < 8:
                    h, context = i // 2, i % 2
                    cols = slice(SAMPLE, T) if context else slice(0, SAMPLE)
                    pro.give(A(RQT[:, h, cols], src[:, 0:PROMPT if context else SAMPLE], ACT.Copy, scale=float(P) ** -0.5))
                    continue
                b, t = (i - 8) // NT, (i - 8) % NT
                if b < 4:
                    pro.give(A((RK, RV, RG, AQK[:, :, 0:512])[b][:, t, :], src, ACT.Copy))
                else:
                    act_done(A(AQK[:, t, 512:640], src[:, 0:128], ACT.Copy))
                    pro.give(A(AV[:, t, :], src[:, 128:256], ACT.Copy))

        none = lambda hf: None
        steps = dict(params=params, modulate=modulate, su=su_rows, F=turn_F, K=none, U=turn_U, V=none, Y=chunk_outputs,
                     out=turn_outputs_s5)
        for step in ORDER:
            if isinstance(step, int):
                tiles(step)
            else:
                steps[step[0]](step[1])
        act.wait_ge(free_p, pro.k)
        phase_end(act, 0)
        if STOP <= 0:
            return

        act.wait_ge(ret_in, 16 * 8)
        for d in range(2):
            for h in range(RH):
                lg = LG[:, d, h:h + 1]
                A(QX[:, 0, d, h, :], DIST[:, d, :], ACT.Exp, scale=lg)
                A(XI[:, d, h, :], DIST[:, 2 + d, :], ACT.Exp, scale=lg)
                A(ZETA[:, d, h:h + 1], ZPOS[:, d:d + 1], ACT.Exp, scale=lg)
        act_done(A(CD, LG, ACT.Exp, scale=float(P)))
        act.sem_inc(ret_exp, 1)
        for t in range(NT):
            if t == 0:
                act.wait_ge(kv_done, len(KV_ORDER))
            if t >= 2:
                act.wait_ge(ro_ready, t - 1)
            A(VZ[:, t % 2, :], RG[:, t, :], ACT.Tanh, scale=0.5).then_inc(ro_gate, 1)
            if t >= 1:
                src = sca.take(act)
                sca.give(A(ROT[:, :, P * (t - 1):P * t], src.rearrange("p (a b) -> p a b", a=4), ACT.Copy, scale=0.5))
        src = sca.take(act)
        sca.give(A(ROT[:, :, P * (NT - 1):P * NT], src.rearrange("p (a b) -> p a b", a=4), ACT.Copy, scale=0.5))
        act.wait_ge(free_a, sca.k)
        phase_end(act, 1)
        if STOP <= 1:
            return

        for t in range(NT):
            src = sca.take(act)
            sca.give(A(QTT[:, :, P * t:P * t + P], src.rearrange("p (a b) -> p a b", a=4), ACT.Copy, scale=float(HD) ** -0.5))
        flat = banks[:].rearrange("p b c -> p (b c)")
        for i in range(8 * NT):
            t, b, half = i // 8, i % 8 // 2, i % 2
            n = KEYS if t < NS else P
            act.wait_ge(s_max, i + 1)
            if i >= 2:
                act.wait_ge(pt_full, i - 1)
            head = b + 4 * half
            if i % 4 != 3:
                j = gat.k
                src = gat.take(act)
                gat.give(A(TG[j // NT][:, j % NT, :], src, ACT.Tanh, scale=0.5))
            A(PR[:, i % 2, 0:n], flat[:, 1024 * half:1024 * half + n], ACT.Exp, bias=AMAX[:, i % 4:i % 4 + 1],
              accum_out=ASUM[:, t, head:head + 1]).then_inc(p_ready, 1)
        phase_end(act, 2)
        if STOP <= 2:
            return

        for i in range(2 * NT):
            src = sca.take(act)
            if i >= 2:
                act.wait_ge(tb_used, i - 1)
            act_done(A(MT1[:, i % 2, :], src, ACT.Tanh, scale=0.5))
            act.sem_inc(free_a, 1); sca.k += 1
            act.sem_inc(tb_ready, 1)
        for t in range(NT):
            src = sca.take(act)
            sca.give(A(MERT[:, 4:8, P * t:P * t + P], src.rearrange("p (a b) -> p a b", a=4), ACT.Copy, scale=0.5))
        act.wait_ge(free_a, sca.k)
        phase_end(act, 3)
        if STOP <= 3:
            return

        for n in range(8):
            for s in range(2):
                copy_out(BC2[:, n // 2, s, 512 * (n % 2):512 * (n % 2) + 512])
            act.wait_ge(free_a, sca.k)
            act.sem_inc(bc_ready, 1)
        phase_end(act, 4)
        if STOP <= 4:
            return

        for t in range(NT):
            act_done(A(SQ2, X2[:, t, :], ACT.Square, accum_out=small[:, t:t + 1]))
        act.sem_inc(sq_ready, 1)
        for t in range(NT):
            src = sca.take(act)
            act_done(A(COLS2[:, t % 2, 4:8, :], src.rearrange("p (a b) -> p a b", a=4), ACT.Copy))
            act.sem_inc(free_a, 1); sca.k += 1
        act.wait_ge(exp_ready, 1)
        act_done(A(PROB, LOGIT, ACT.Exp))
        act.sem_inc(exp_ready, 1)
        phase_end(act, 5)
        if STOP <= 5:
            return

        def act_end(n, m, e, b):
            act.wait_ge(ht_full, n + 1)
            at_least(act, dn1, n - 1)
            A(HIDT[:, b, :], banks[:, 4, :], ACT.Copy).then_inc(ht_ready, 1)
            act.wait_ge(dn1, n + 1)
            at_least(act, out_wr[b], 16 * m)
            A(OUT[:, b, 512:1024], banks[:, 6, :], ACT.Copy).then_inc(out_a, 1)
            act.wait_ge(out_a, n + 1)
            act.wait_ge(out_d, n + 1)
            act.dma_start(scratch_out.rearrange("(e p) c -> e p c", p=CAP)[e], OUT[:, b, :]).then_inc(out_wr[b], 16)

        def act_begin(n, m, e, b, before):
            act.wait_ge(g_t, n + 1)
            at_least(act, up_full, n - 1)
            A(COLS2[:, b, 4:8, :], banks[:, 1, :].rearrange("p (a b) -> p a b", a=4), ACT.Copy).then_inc(gt_a, 1)
            if before:
                before()
            act.wait_ge(gate_full, n + 1)
            at_least(act, hid_ready, n)
            A(TH, banks[:, 2, :], ACT.Tanh, scale=0.5).then_inc(th_ready, 1)

        all_passes(act, lambda r: expert_pipeline(act, r, act_begin, act_end))
        phase_end(act, 6)
        if STOP <= 6:
            return
        for t in range(NT):
            act_done(A(SQ2F, X2[:, t, :], ACT.Square, accum_out=small[:, t:t + 1]))
        act.sem_inc(fin_sq, 1)

    @block.vector
    def _(dve):
        vec = Bank(0, 4, full_d, free_d)
        done = engine_tools(dve, dve_step)
        V_ = nc.vector
        tt, ts, stt, cp = V_.tensor_tensor, V_.tensor_scalar, V_.scalar_tensor_tensor, V_.tensor_copy

        def rsqrt(out, x, t):
            done(ts(out.bitcast(I32), x.bitcast(I32), -0.5, float(0x5f3759df), ALU.mult, ALU.add))
            for _ in range(4):
                done(tt(t, out, out, ALU.mult))
                done(tt(t, t, x, ALU.mult))
                done(ts(t, t, -0.5, 1.5, ALU.mult, ALU.add))
                done(tt(out, out, t, ALU.mult))

        def exact_exp(out, x, t, r, k):
            done(ts(r, x, -87.0, 88.0, ALU.max, ALU.min))
            done(ts(t, r, 1.4426950408889634, MAGIC, ALU.mult, ALU.add))
            done(ts(t, t, -MAGIC, None, ALU.add))
            done(ts(k, t, 127.0, 8388608.0, ALU.add, ALU.mult))
            done(stt(r, t, -LN2_HI, r, ALU.mult, ALU.add))
            done(stt(r, t, -LN2_LO, r, ALU.mult, ALU.add))
            done(ts(out, r, EXP_C[0], None, ALU.mult))
            for c in EXP_C[1:]:
                done(stt(out, out, c, r, ALU.add, ALU.mult))
            done(ts(out, out, 1.0, None, ALU.add))
            done(tt(out, out, k.bitcast(F32), ALU.mult))

        def cmul(ore, oim, ar, ai, br, bi, t):
            done(tt(t, ar, br, ALU.mult))
            done(tt(ore, ai, bi, ALU.mult))
            done(tt(ore, t, ore, ALU.subtract))
            done(tt(t, ar, bi, ALU.mult))
            done(tt(oim, ai, br, ALU.mult))
            done(tt(oim, t, oim, ALU.add))

        done(V_.memset(ones[:], 1.0))
        done(V_.memset(cS[:], 0.0))
        dve.wait_ge(tanh_c, 1)
        done(stt(cT[:, 1], cT[:, 1], 1.0, cT[:, 0], ALU.add, ALU.mult))
        ts(cS[:, :, 0:2], cT[:, 1], 0.5, None, ALU.mult).then_inc(silu_c, 1)

        def mod_row(n, row, bias, gain):
            src = vec.take(dve)
            done(cp(row, src))
            dve.sem_inc(free_d, 1); vec.k += 1
            if gain is None:
                done(tt(row[0:2], row[0:2], bias, ALU.add))
            else:
                done(stt(row[0:2], row[0:2], 1.0, bias, ALU.add, ALU.add))
                done(tt(row, row, gain[:, 512 * (n % 2):512 * (n % 2) + 512], ALU.mult))
            dve.sem_inc(mod_ready, 1)

        def modulate(_):
            dve.wait_ge(sq_ready, 1)
            done(ts(small[:, 8:8 + NT], small[:, 0:NT], 1.0 / D, EPS, ALU.mult, ALU.add))
            rsqrt(small[:, 16:16 + NT], small[:, 8:8 + NT], small[:, 24:24 + NT])
            dve.wait_ge(rows_in, 48)
            for n in range(4):
                if n >= 2:
                    dve.wait_ge(full_a, 2 * (n - 1))
                mod_row(n, modrow[:, n % 2, :], bias_row[:, n, :], gain_row if n >= 2 else None)
            dve.wait_ge(bc_ready, 1)
            first = vec.k
            for t in range(NT):
                s = 0 if t < NS else 1
                if t >= 2:
                    dve.wait_ge(full_d, first + 2 * (t - 1))
                xn = XN[:, t % 2, :]
                done(stt(xn, X[:, t, :], small[:, 16 + t:17 + t], BC[:, 1, s, :], ALU.mult, ALU.mult))
                tt(xn, xn, BC[:, 0, s, :], ALU.add).then_inc(xn_ready, 1)
                for half in range(2):
                    src = vec.take(dve)
                    vec.give(cp(HT[:, 4 * half:4 * half + 4, P * t:P * t + P], src.rearrange("p (a b) -> p a b", a=4)))
            dve.wait_ge(free_d, vec.k)

        def params(hf):
            dve.wait_ge(par_in, 16 * 15 * (hf + 1))
            dve.wait_ge(bn_in, 32 * (hf + 1))
            for d in range(2):
                done(cp(NAT[:, 4 + d, :].rearrange("g (h p) -> g h p", h=2),
                        LD[:, d, :].unsqueeze(2).broadcast_to([GPH, 2, PS])))
            dve.sem_inc(nat_ready, 1)
            src = vec.take(dve)
            done(cp(PAR.rearrange("p a b -> p (a b)"), src[:, 0:10 * GPH]))
            dve.sem_inc(free_d, 1); vec.k += 1
            for j in range(2):
                src = vec.take(dve)
                vec.give(cp(CT[:, j], src[:, 0:16 * GPH].rearrange("p (a b) -> p a b", a=GPH)))
            dve.wait_ge(free_d, vec.k)
            par = lambda n: PAR[:, n:n + 2, :]
            are, aim, ldt = par(0), par(2), par(4)
            step_, re, im, mag, t1, t2 = SC_[0], SC_[1], SC_[2], SC_[6], SC_[7], SC_[8]
            exact_exp(step_, ldt, t1, t2, SCI)
            done(tt(re, are, step_, ALU.mult))
            done(tt(im, aim, step_, ALU.mult))
            exact_exp(mag, re, t1, t2, SCI)
            ang = SC_[3]
            done(ts(t1, im, float(1 / (2 * np.pi)), MAGIC, ALU.mult, ALU.add))
            done(ts(t1, t1, -MAGIC, None, ALU.add))
            done(stt(ang, t1, -TWO_PI_A, im, ALU.mult, ALU.add))
            done(stt(ang, t1, -TWO_PI_B, ang, ALU.mult, ALU.add))
            done(stt(ang, t1, -TWO_PI_C, ang, ALU.mult, ALU.add))
            ts(ang, ang, 3.1415925, -3.1415925, ALU.min, ALU.max).then_inc(ang_ready, 1)
            dve.wait_ge(sin_ready, hf + 1)
            sin, cos, half_sin = SC_[4], SC_[9], SC_[5]
            done(tt(cos, half_sin, half_sin, ALU.mult))
            done(ts(cos, cos, -2.0, 1.0, ALU.mult, ALU.add))
            done(V_.memset(PW[:, 0, :, 0, :], 1.0))
            done(V_.memset(PW[:, 1, :, 0, :], 0.0))
            done(tt(PW[:, 0, :, 1, :], mag, cos, ALU.mult))
            done(tt(PW[:, 1, :, 1, :], mag, sin, ALU.mult))
            for m in (1, 2, 4):
                b = [PW[:, j, :, m, :].unsqueeze(2).broadcast_to([P, 2, m, GPH]) for j in range(2)]
                t = PWT[:, 0:2 * m * GPH].rearrange("p (a b c) -> p a b c", a=2, b=m)
                cmul(PW[:, 0, :, m + 1:2 * m + 1, :], PW[:, 1, :, m + 1:2 * m + 1, :],
                     PW[:, 0, :, 1:m + 1, :], PW[:, 1, :, 1:m + 1, :], b[0], b[1], t)
            nre, den, qre, qim = SC_[10], SC_[11], SC_[12], SC_[13]
            done(ts(nre, PW[:, 0, :, 1, :], -1.0, None, ALU.add))
            done(tt(den, are, are, ALU.mult))
            done(tt(t1, aim, aim, ALU.mult))
            done(tt(den, den, t1, ALU.add))
            done(V_.reciprocal(den, den))
            nim = PW[:, 1, :, 1, :]
            done(tt(qre, nre, are, ALU.mult))
            done(tt(t1, nim, aim, ALU.mult))
            done(tt(qre, qre, t1, ALU.add))
            done(tt(qre, qre, den, ALU.mult))
            done(tt(qim, nim, are, ALU.mult))
            done(tt(t1, nre, aim, ALU.mult))
            done(tt(qim, qim, t1, ALU.subtract))
            done(tt(qim, qim, den, ALU.mult))
            for d in range(2):
                bc = lambda x: x[:, d, :].unsqueeze(2).broadcast_to([P, GPH, GI])
                cmul(BB[:, d, 0], BB[:, d, 1], bc(qre), bc(qim), BN[:, 0], BN[:, 1], BBT)
            ure, uim, vre, vim, m8 = SC_[10], SC_[11], SC_[12], SC_[13], SC_[14]
            cmul(ure, uim, cos, sin, cos, sin, t1)
            cmul(vre, vim, ure, uim, ure, uim, t1)
            cmul(SC_[15], SC_[16], vre, vim, vre, vim, t1)
            done(tt(m8, mag, mag, ALU.mult))
            done(tt(m8, m8, m8, ALU.mult))
            done(tt(m8, m8, m8, ALU.mult))

        def turn_F(hf):
            for d in range(2):
                pw = [PW[:, j, d, 0:Q, :].rearrange("p k g -> p g k") for j in range(2)]
                if d == 0:
                    pw = [x[:, :, ::-1] for x in pw]
                pw = [x.unsqueeze(3).broadcast_to([P, GPH, Q, GI]) for x in pw]
                bb = [BB[:, d, j].unsqueeze(2).broadcast_to([P, GPH, Q, GI]) for j in range(2)]
                if d == 1:
                    dve.wait_ge(f_done, 2 * hf + 1)
                cmul(FP[0], FP[1], pw[0], pw[1], bb[0], bb[1], FPT)
                dve.sem_inc(f_ready, 1)

        def lag_kernels(hf):
            dve.wait_ge(f_done, 2 * hf + 2)
            for d in range(2):
                pw = [PW[:, j, d].rearrange("p k g -> p g k").unsqueeze(3).broadcast_to([P, GPH, 9, GI]) for j in range(2)]
                ct = [CT[:, j].unsqueeze(2).broadcast_to([P, GPH, 9, GI]) for j in range(2)]
                done(tt(CTMP, ct[1], pw[1], ALU.mult))
                done(tt(CPW[:, d, 0], ct[0], pw[0], ALU.mult))
                done(tt(CPW[:, d, 0], CPW[:, d, 0], CTMP, ALU.subtract))
                done(tt(CTMP, ct[0], pw[1], ALU.mult))
                done(tt(CPW[:, d, 1], ct[1], pw[0], ALU.mult))
                fl = lambda x: x.rearrange("p a b c -> p (a b c)")
                done(stt(fl(CPW[:, d, 1]), fl(CPW[:, d, 1]), -1.0, fl(CTMP), ALU.mult, ALU.subtract))
            dve.sem_inc(cpw_ready, 1)
            for d in range(2):
                for q in range(4):
                    src = vec.take(dve)[0:GI].rearrange("i (g k o) -> i g k o", g=4, k=Q)
                    gs = slice(8 * (q // 2) + q % 2, 8 * (q // 2) + 8, 2)
                    if d == 0:
                        vec.give(cp(KP[:, gs, 7:15, :], src))
                    else:
                        if q == 0:
                            dve.wait_ge(free_d, vec.k)
                        done(cp(KP[:, gs, 0:7, :], src[:, :, 7:0:-1, :]))
                        vec.give(tt(KP[:, gs, 7, :], KP[:, gs, 7, :], src[:, :, 0, :], ALU.add))
            dve.wait_ge(free_d, vec.k)
            done(tt(DG, DT_.unsqueeze(2).broadcast_to([GI, GH_, GI]),
                    ident[0:GI, 0:GI].unsqueeze(1).broadcast_to([GI, GH_, GI]), ALU.mult))
            tt(KP[:, :, 7, :], KP[:, :, 7, :], DG, ALU.add).then_inc(kp_ready, 1)

        def turn_U(hf):
            dve.wait_ge(sraw_in, 16 * (hf + 1))
            cp(S[0:NC, :].rearrange("c (g s i) -> c s g i", g=GH_, s=Q), SRAW).then_inc(s_chunks, 1)
            dve.wait_ge(s_chunks, hf + 1)

        def chunk_inputs(hf):
            done(V_.memset(V[:, :, :, :, CS + 1].rearrange("p a b c -> p (a b) c"), 0.0))
            for d in range(2):
                for c in range(2):
                    done(cp(V[:, d, c, :, 0], PAR[:, 6 + 2 * c + d, :]))
            for d in range(2):
                for c in range(2):
                    for q in range(2):
                        n = min(6, GPH - 6 * q)
                        src = vec.take(dve)[:, 0:NC * n].rearrange("p (a b) -> p a b", a=n)
                        lat, con = src[:, :, 0:CS], src[:, :, CS:NC]
                        if d:
                            lat, con = lat[:, :, ::-1], con[:, :, ::-1]
                        done(cp(V[:, d, c, 6 * q:6 * q + n, 1:CS + 1], lat))
                        vec.give(cp(V[:, d, c, 6 * q:6 * q + n, CS + 2:SC], con))
            dve.wait_ge(free_d, vec.k)
            v3 = lambda x: x.rearrange("p (a b) -> p a b", b=SC)
            parts = ((slice(0, CS + 1), slice(0, CS + 1)), (slice(CS + 1, SC), slice(0, CP_ + 1)))
            for d in range(2):
                rot = [RT[:, j] for j in range(2)]
                for j in range(2):
                    done(V_.memset(rot[j][:, :, 0], 1.0 - j))
                    done(cp(rot[j][:, :, 1], SC_[15 + j][:, d, :]))
                for m in (1, 2, 4, 8, 16, 32):
                    b = [x[:, :, m:m + 1].broadcast_to([P, GPH, m]) for x in rot]
                    cmul(rot[0][:, :, m + 1:2 * m + 1], rot[1][:, :, m + 1:2 * m + 1],
                         rot[0][:, :, 1:m + 1], rot[1][:, :, 1:m + 1], b[0], b[1],
                         RTT[:, 0:m * GPH].rearrange("p (a b) -> p a b", b=m))
                done(cp(A8, SC_[14][:, d, :].unsqueeze(2).broadcast_to([P, GPH, SC])))
                done(V_.memset(A8[:, :, 0], 0.0))
                done(V_.memset(A8[:, :, CS + 1], 0.0))
                vr, vi = V[:, d, 0], V[:, d, 1]
                for cols, k in parts:
                    for dst, r_, x in ((0, 0, vr), (1, 1, vi), (2, 0, vi), (3, 1, vr)):
                        done(tt(v3(TMP4[dst])[:, :, cols], rot[r_][:, :, k], x[:, :, cols], ALU.mult))
                fl = lambda x: x.rearrange("p a b -> p (a b)")
                done(tt(fl(vr), TMP4[0], TMP4[1], ALU.add))
                done(tt(fl(vi), TMP4[2], TMP4[3], ALU.subtract))
                for j, x in enumerate((vr, vi)):
                    done(V_.tensor_tensor_scan(Z[j], fl(A8), fl(x), 0.0, ALU.mult, ALU.add))
                for cols, k in parts:
                    for dst, r_, x in ((0, 0, 0), (1, 1, 1), (2, 0, 1), (3, 1, 0)):
                        done(tt(v3(TMP4[dst])[:, :, cols], rot[r_][:, :, k], v3(Z[x])[:, :, cols], ALU.mult))
                for j, (x, y, op) in enumerate(((0, 1, ALU.subtract), (2, 3, ALU.add))):
                    xin = fl(V[:, d, j])[:, 0:GPH * NC].rearrange("p (a b) -> p a b", b=NC)
                    for out, cols in ((xin[:, :, 0:CS], slice(0, CS)), (xin[:, :, CS:NC], slice(CS + 1, CS + 1 + CP_))):
                        if d:
                            out = out[:, :, ::-1]
                        done(tt(out, v3(TMP4[x])[:, :, cols], v3(TMP4[y])[:, :, cols], op))
                    done(tt(SF[:, j, d, :], v3(TMP4[x])[:, :, SC - 1], v3(TMP4[y])[:, :, SC - 1], op))
            dve.sem_inc(xi_ready, 1)

        def chunk_outputs(hf):
            src = vec.take(dve)
            vec.give(cp(SFO.rearrange("p a b -> p (a b)"), src[0:GPH, :]))
            dve.wait_ge(free_d, vec.k)
            dve.sem_inc(sf_ready, 1)

        none = lambda hf: None
        steps = dict(params=params, modulate=modulate, su=none, F=turn_F, K=lag_kernels, U=turn_U, V=chunk_inputs, Y=chunk_outputs,
                     out=none)
        for step in ORDER:
            if not isinstance(step, int):
                steps[step[0]](step[1])
        phase_end(dve, 0)
        if STOP <= 0:
            return

        for t in range(NT):
            src = vec.take(dve)
            vec.give(cp(RKT[:, :, P * t:P * t + P], src.rearrange("p (a b) -> p a b", a=4)))
        dve.wait_ge(ret_in, 16 * 8)
        dve.wait_ge(ret_exp, 1)
        for d in range(2):
            done(tt(QX[:, 0, d], QX[:, 0, d], MASK[:, d, :].unsqueeze(1).broadcast_to([P, RH, P]), ALU.mult))
        done(tt(DEC, QX[:, 0, 0], QX[:, 0, 1], ALU.add))
        r3 = lambda x: x.rearrange("p (h e) -> p h e", h=RH)
        for i in range(len(KV_ORDER) + 1):
            if i < len(KV_ORDER):
                d, t = KV_ORDER[i]
                if i >= 2:
                    dve.wait_ge(full_d, vec.k + 1 - 0)
                tt(r3(VZ[:, i % 2, :]), r3(RV[:, t, :]), ZETA[:, d, :].unsqueeze(2).broadcast_to([P, RH, P]),
                   ALU.mult).then_inc(vz_ready, 1)
            if i >= 1:
                d, t = KV_ORDER[i - 1]
                src = vec.take(dve)
                if t == NS:
                    done(cp(KVO[:, d, :], src))
                    dve.sem_inc(kvo_ready, 1)
                else:
                    nxt = t + 1 if d == 0 else t - 1
                    for h in range(RH):
                        hs = slice(P * h, P * h + P)
                        done(stt(ST[:, d, nxt, hs], ST[:, d, t, hs], CD[:, d, h:h + 1], src[:, hs], ALU.mult, ALU.add))
                dve.sem_inc(free_d, 1); vec.k += 1
                dve.sem_inc(kv_done, 1)
        for t in range(NT):
            if t < NS:
                for d in range(2):
                    done(tt(QX[:, t % 2, d], RQT[:, :, P * t:P * t + P], XI[:, d], ALU.mult))
            src = vec.take(dve)
            done(tt(r3(SS[:, t % 2, :]), r3(src), DEC, ALU.mult))
            dve.sem_inc(free_d, 1); vec.k += 1
            dve.sem_inc(sd_ready, 1)
            src = vec.take(dve)
            done(cp(OALL[:, t, :], src))
            dve.sem_inc(free_d, 1); vec.k += 1
            done(tt(KVT, OALL[:, t, :], OALL[:, t, :], ALU.mult))
            done(V_.tensor_reduce(RSS[:, 0, RH * t:RH * t + RH], r3(KVT), AX.X, ALU.add))
        done(ts(RSS[:, 0, :], RSS[:, 0, :], 1.0 / P, EPS, ALU.mult, ALU.add))
        rsqrt(RSS[:, 1, :], RSS[:, 0, :], RSS[:, 2, :])
        for t in range(NT):
            o = OALL[:, t, :]
            done(tt(r3(o), r3(o), RSS[:, 1, RH * t:RH * t + RH].unsqueeze(2).broadcast_to([P, RH, P]), ALU.mult))
            done(tt(o, o, RNG, ALU.mult))
            dve.wait_ge(ro_gate, t + 1)
            done(stt(VZ[:, t % 2, :], VZ[:, t % 2, :], 1.0, RG[:, t, :], ALU.add, ALU.mult))
            tt(o, o, VZ[:, t % 2, :], ALU.mult).then_inc(ro_ready, 1)
        dve.wait_ge(ro_ready, NT)
        phase_end(dve, 1)
        if STOP <= 1:
            return

        NH = AH + KVH
        dve.wait_ge(att_in, 16 * 5)
        done(cp(QG[:, 0:AH, :], QGL[:, 0:1, :].broadcast_to([P, AH, HD])))
        done(cp(QG[:, AH:NH, :], QGL[:, 1:2, :].broadcast_to([P, KVH, HD])))
        h3 = lambda x: x.rearrange("p (h e) -> p h e", e=HD)
        for t in range(NT):
            done(tt(QT1, AQK[:, t, :], AQK[:, t, :], ALU.mult))
            done(V_.tensor_reduce(QSS[:, 0, NH * t:NH * t + NH], h3(QT1), AX.X, ALU.add))
        done(ts(QSS[:, 0, :], QSS[:, 0, :], 1.0 / HD, EPS, ALU.mult, ALU.add))
        rsqrt(QSS[:, 1, :], QSS[:, 0, :], QSS[:, 2, :])
        for t in range(NT):
            x, rs = AQK[:, t, :], QSS[:, 1, NH * t:NH * t + NH]
            swap = lambda v: v.rearrange("p (h b) -> p h b", h=2)
            done(tt(QT1[:, 0:512].rearrange("p (b h e) -> p h b e", b=4, h=2), x[:, 0:512].rearrange("p (h b e) -> p h b e", h=2, b=4),
                    swap(rs[:, 0:AH]).unsqueeze(3).broadcast_to([P, 2, 4, HD]), ALU.mult))
            done(tt(h3(QT1[:, 512:640]), h3(x[:, 512:640]), rs[:, AH:NH].unsqueeze(2).broadcast_to([P, KVH, HD]), ALU.mult))
            if t == NS:
                done(tt(h3(x), h3(QT1), QG, ALU.mult))
                break
            done(tt(h3(QT1), h3(QT1), QG, ALU.mult))
            pairs = lambda v: v.rearrange("p (h e two) -> p h e two", two=2, e=HD // 2)
            cos, sn = (ROPE[:, j, t, :] for j in range(2))
            done(tt(h3(x), h3(QT1), cos.unsqueeze(1).broadcast_to([P, NH, HD]), ALU.mult))
            for j in range(2):
                s_ = sn.rearrange("p (e two) -> p e two", two=2)[:, :, j].unsqueeze(1).broadcast_to([P, NH, HD // 2])
                done(tt(pairs(QT2)[:, :, :, j], pairs(QT1)[:, :, :, 1 - j], s_, ALU.mult))
            done(tt(x, x, QT2, ALU.add))
        dve.sem_inc(qk_ready, 1)
        dve.sem_inc(kv_out, 1)
        src = vec.take(dve)
        vec.give(cp(KTT[:, 0:512], src))
        src = vec.take(dve)
        done(cp(KTT[:, 512:640], src[:, 0:P]))
        vec.give(cp(KTP, src[:, P:2 * P]))
        dve.wait_ge(free_d, vec.k)
        flat = banks[:].rearrange("p b c -> p (b c)")
        NU = 8 * NT

        def top(i):
            t, half = i // 8, i % 2
            n = KEYS if t < NS else P
            dve.wait_ge(s_full, i + 1)
            if i >= 4:
                dve.wait_ge(p_ready, i - 3)
            V_.tensor_reduce(AMAX[:, i % 4:i % 4 + 1], flat[:, 1024 * half:1024 * half + n], AX.X, ALU.max,
                             negate=True).then_inc(s_max, 1)

        def copy_turned(i):
            n = KEYS if i // 8 < NS else P
            dve.wait_ge(pt_full, i + 1)
            if i >= 2:
                dve.wait_ge(o_full, i - 1)
            cp(PT[:, i % 2, 0:n], flat[:, 2048:2048 + n]).then_inc(pt_ready, 1)

        def rows_out(t):
            dve.wait_ge(o_full, 8 * t + 8)
            done(V_.reciprocal(ASUM[:, t, :], ASUM[:, t, :]))
            if t >= 2:
                dve.wait_ge(aot_full, t - 1)
            tt(h3(AO[:, t % 2, :]), h3(banks[:, 6, :]), ASUM[:, t, :].unsqueeze(2).broadcast_to([P, AH, HD]),
               ALU.mult).then_inc(ao_ready, 1)

        def columns_out(t):
            dve.wait_ge(aot_full, t + 1)
            cp(ATT[:, :, P * t:P * t + P], banks[:, 4, :].rearrange("p (a b) -> p a b", a=4)).then_inc(aot_ready, 1)

        top(0)
        for i in range(NU):
            if i + 1 < NU:
                top(i + 1)
            copy_turned(i)
            if i % 8 == 0 and i:
                rows_out(i // 8 - 1)
            if i % 8 == 2 and i > 8:
                columns_out(i // 8 - 1)
        rows_out(NT - 1)
        columns_out(NT - 1)
        dve.wait_ge(aot_ready, NT)
        phase_end(dve, 2)
        if STOP <= 2:
            return

        for n in range(2):
            ns = slice(512 * n, 512 * n + 512)
            for branch in range(3):
                for t in range(NT):
                    dst, tg = MER[:, t, ns], TG[3 * n + branch][:, t, :]
                    src = vec.take(dve)
                    if branch == 0:
                        vec.give(stt(dst, tg, 1.0, src, ALU.add, ALU.mult))
                        continue
                    mt = MT2[:, t % 2, :]
                    if branch == 1:
                        done(stt(mt, tg, 1.0, src, ALU.add, ALU.mult))
                        dve.sem_inc(free_d, 1); vec.k += 1
                    else:
                        i = NT * n + t
                        done(ts(tg, tg, 0.5, 0.5, ALU.mult, ALU.add))
                        dve.wait_ge(tb_ready, i + 1)
                        done(stt(mt, MT1[:, i % 2, :], 1.0, src, ALU.add, ALU.mult))
                        dve.sem_inc(free_d, 1); vec.k += 1
                        dve.sem_inc(tb_used, 1)
                        done(tt(mt, mt, tg, ALU.mult))
                    if branch == 1 and t == 0:
                        dve.wait_ge(free_d, vec.k)
                    done(tt(dst, dst, mt, ALU.add))
                    if n == 1 and branch == 2:
                        dve.sem_inc(mer_ready, 1)
        for t in range(NT):
            src = vec.take(dve)
            vec.give(ts(MERT[:, 0:4, P * t:P * t + P], src.rearrange("p (a b) -> p a b", a=4), 0.5, None, ALU.mult))
        dve.wait_ge(free_d, vec.k)
        phase_end(dve, 3)
        if STOP <= 3:
            return

        dve.wait_ge(x2_in, 16 * (NT + 3))
        fa, rows, half = FULL_A_BEFORE_LAST, 0, 0
        for step in LAST_ORDER:
            if step is not None:
                if rows >= 2:
                    dve.wait_ge(full_a, fa + 2 * (rows - 1))
                mod_row(step, modrow2[:, step % 2, :], bias2[:, step - 4, :], gain2 if step in (8, 9) else None)
                rows += 1
                continue
            ns = slice(512 * half, 512 * half + 512)
            half += 1
            dve.wait_ge(bc_ready, 1 + half)
            for t in range(NT):
                s = 0 if t < NS else 1
                src = vec.take(dve)
                done(tt(SQ2[:, 0:512], src, BC2[:, 0, s, ns], ALU.mult))
                dve.sem_inc(free_d, 1); vec.k += 1
                done(tt(X2[:, t, ns], X2[:, t, ns], SQ2[:, 0:512], ALU.add))
        dve.wait_ge(bc_ready, 1 + 8)
        phase_end(dve, 4)
        if STOP <= 4:
            return

        done(V_.memset(ZERO, 0))
        dve.sem_inc(zero_ready, 1)
        dve.wait_ge(sq_ready, 2)
        done(ts(small[:, 8:8 + NT], small[:, 0:NT], 1.0 / D, EPS, ALU.mult, ALU.add))
        rsqrt(small[:, 16:16 + NT], small[:, 8:8 + NT], small[:, 24:24 + NT])
        dve.wait_ge(route_in, 64)
        for t in range(NT):
            s = 0 if t < NS else 1
            if t >= 2:
                dve.wait_ge(h2_out, 16 * (t - 1))
            h = ROWS2[:, t % 2, :]
            done(stt(h, X2[:, t, :], small[:, 16 + t:17 + t], BC2[:, 2, s, :], ALU.mult, ALU.mult))
            done(tt(h, h, BC2[:, 1, s, :], ALU.add))
            dve.sem_inc(h2_ready, 1)
            src = vec.take(dve)
            done(cp(COLS2[:, t % 2, 0:4, :], src.rearrange("p (a b) -> p a b", a=4)))
            dve.sem_inc(free_d, 1); vec.k += 1
            src = vec.take(dve)
            done(tt(LOGIT[:, t, :], src[:, 0:NE], BR, ALU.add))
            dve.sem_inc(free_d, 1); vec.k += 1
        c = lambda j: ROUTE[:, j, :]
        over = lambda x, n: x.unsqueeze(2).broadcast_to([P, NT, n])
        red = lambda out, x, op: done(V_.tensor_reduce(out, x, AX.X, op))
        red(c(0), LOGIT, ALU.max)
        done(tt(LOGIT, LOGIT, over(c(0), NE), ALU.subtract))
        dve.sem_inc(exp_ready, 1)
        dve.wait_ge(exp_ready, 2)
        red(c(0), PROB, ALU.add)
        done(V_.reciprocal(c(0), c(0)))
        done(tt(PROB, PROB, over(c(0), NE), ALU.mult))
        p4 = PROB.rearrange("p t (g e) -> p t g e", e=EG)
        for j, (x, y, op) in enumerate(((0, 1, ALU.max), (0, 1, ALU.min), (2, 3, ALU.max), (2, 3, ALU.min))):
            done(tt(GH[j], p4[:, :, :, x], p4[:, :, :, y], op))
        done(tt(GH[4], GH[0], GH[2], ALU.max))
        done(tt(GH[5], GH[0], GH[2], ALU.min))
        done(tt(GH[6], GH[1], GH[3], ALU.max))
        done(tt(GH[5], GH[5], GH[6], ALU.max))
        done(tt(GH[4], GH[4], GH[5], ALU.add))

        def first_largest(onehot, index, value, x, n, tmp):
            it = IOTA[:, 0:n].unsqueeze(1).broadcast_to([P, NT, n])
            red(value, x, ALU.max)
            done(tt(tmp, x, over(value, n), ALU.is_equal))
            done(ts(tmp, tmp, -99.0, 99.0, ALU.mult, ALU.add))
            done(tt(tmp, tmp, it, ALU.add))
            red(index, tmp, ALU.min)
            done(tt(onehot, it, over(index, n), ALU.is_equal))

        first_largest(GH[7], c(0), c(1), GH[4], NG, GH[0])
        g16 = GH[7].unsqueeze(3).broadcast_to([P, NT, NG, EG])
        t4 = lambda x: x.rearrange("p t (g e) -> p t g e", e=EG)
        done(tt(t4(PROB), t4(PROB), g16, ALU.mult))
        done(tt(t4(PROB), t4(PROB), g16, ALU.add))
        done(ts(PROB, PROB, -1.0, None, ALU.add))
        E1, E2, V1, V2, R1, R2, W1, W2 = (c(j) for j in range(2, 10))
        first_largest(M1, E1, V1, PROB, NE, EQ)
        done(stt(PROB.rearrange("p t e -> p (t e)"), M1.rearrange("p t e -> p (t e)"), -3.0, PROB.rearrange("p t e -> p (t e)"), ALU.mult, ALU.add))
        first_largest(M2, E2, V2, PROB, NE, EQ)
        done(tt(MB, M1, M2, ALU.add))
        dve.sem_inc(masks_ready, 1)
        done(tt(c(0), V1, V2, ALU.add))
        done(V_.reciprocal(c(0), c(0)))
        for w_, v in ((W1, V1), (W2, V2)):
            done(tt(w_, v, c(0), ALU.mult))
            done(ts(w_, w_, 0.5, None, ALU.mult))
        src = vec.take(dve)
        done(cp(RANK, src[:, 0:NT * NE].rearrange("p (t e) -> p t e", t=NT)))
        red(c(0)[:, 0:1], src[:, NT * NE:NT * NE + NE], ALU.max)
        done(cp(TOP_COUNT, c(0)[:, 0:1]))
        dve.sem_inc(free_d, 1); vec.k += 1
        for k, (m_, rk, e_) in enumerate(((M1, R1, E1), (M2, R2, E2))):
            done(tt(EQ, m_, RANK, ALU.mult))
            red(rk, EQ, ALU.add)
            done(stt(CIDX[:, :, k], e_, float(T), rk, ALU.mult, ALU.add))
        dve.sem_inc(pos_ready, 1)
        phase_end(dve, 5)
        if STOP <= 5:
            return

        def dve_end(n, m, e, b):
            dve.wait_ge(dn0, n + 1)
            at_least(dve, out_wr[b], 16 * m)
            cp(OUT[:, b, 0:512], banks[:, 5, :]).then_inc(out_d, 1)

        def dve_begin(n, m, e, b, before):
            dve.wait_ge(g_t, n + 1)
            at_least(dve, up_full, n - 1)
            cp(COLS2[:, b, 0:4, :], banks[:, 0, :].rearrange("p (a b) -> p a b", a=4)).then_inc(gt_d, 1)
            if before:
                before()
            dve.wait_ge(th_ready, n + 1)
            at_least(dve, ht_full, n - 1)
            stt(HID[:, b, :], TH, 1.0, banks[:, 2, :], ALU.add, ALU.mult).then_inc(hid_step, 1)
            dve.wait_ge(hid_step, n + 1)
            dve.wait_ge(up_full, n + 1)
            tt(HID[:, b, :], HID[:, b, :], banks[:, 3, :], ALU.mult).then_inc(hid_ready, 1)

        def dve_pass(r):
            if not isinstance(r, int):
                dve.wait_ge(combined, NT * r)
            expert_pipeline(dve, r, dve_begin, dve_end)
            k = [0]

            def step(ins):
                k[0] += 1
                ins.then_inc(comb_step, 1)
                dve.wait_ge(comb_step, COMB_STEPS * r + k[0])

            lo = ROUTE[:, 10, :]
            for j, (rk, e_, w_) in enumerate(((R1, E1, W1), (R2, E2, W2))):
                if isinstance(r, int):
                    step(ts(lo, rk, 0.0, None, ALU.add))
                else:
                    step(ts(rk, rk, -float(CAP), None, ALU.add))
                    step(ts(lo, rk, 0.0, None, ALU.add))
                step(ts(ROUTE[:, 11, :], lo, 0.0, None, ALU.is_ge))
                step(ts(ROUTE[:, 12, :], lo, CAP - 0.5, None, ALU.is_lt))
                step(tt(ROUTE[:, 11, :], ROUTE[:, 11, :], ROUTE[:, 12, :], ALU.mult))
                step(tt(ROUTE[:, 11, :], ROUTE[:, 11, :], w_, ALU.mult))
                step(cp(WP[:, j, :], ROUTE[:, 11, :]))
                step(ts(lo, lo, 0.0, CAP - 1.0, ALU.max, ALU.min))
                step(stt(CIDX[:, :, j], e_, float(CAP), lo, ALU.mult, ALU.add))
                if isinstance(r, int):
                    step(cp(ROUTE[:, 12, :], lo))
            dve.sem_inc(cidx_ready, 1)
            for t in range(NT):
                s = 0 if t < NS else 1
                dve.wait_ge(y_in[t % 2], 32 * ((3, 2)[t % 2] * r + t // 2 + 1))
                y = [YR[:, t % 2, j, :] for j in range(2)]
                step(ts(y[0], y[0], WP[:, 0, t:t + 1], None, ALU.mult))
                step(stt(y[0], y[1], WP[:, 1, t:t + 1], y[0], ALU.mult, ALU.add))
                step(tt(y[0], y[0], BC2[:, 3, s, :], ALU.mult))
                step(tt(X2[:, t, :], X2[:, t, :], y[0], ALU.add))
                dve.sem_inc(combined, 1)
            assert k[0] == COMB_STEPS

        all_passes(dve, dve_pass)
        phase_end(dve, 6)
        if STOP <= 6:
            return
        dve.wait_ge(fin_sq, 1)
        dve.wait_ge(fin_in, 16)
        done(ts(small[:, 8:8 + NT], small[:, 0:NT], 1.0 / D, EPS, ALU.mult, ALU.add))
        rsqrt(small[:, 16:16 + NT], small[:, 8:8 + NT], small[:, 24:24 + NT])
        for t in range(NT):
            stt(X2[:, t, :], X2[:, t, :], small[:, 16 + t:17 + t], FG, ALU.mult, ALU.mult).then_inc(fin_ready, 1)

    @block.gpsimd
    def _(pool):
        n_out = 0
        pair = lambda x: x.rearrange("(g h) p -> g (h p)", h=2)
        for hf in range(2):
            gps = slice(GPH * hf, GPH * hf + GPH)
            if hf:
                pool.wait_ge(s5_done, 1)
            for d, (re, im, ld) in enumerate((("a_re_f", "a_im_f", "log_dt_f"), ("a_re_b", "a_im_b", "log_dt_b"))):
                pool.dma_start(NAT[:, d, :], pair(a[re][0])[gps]).then_inc(par_in, 16)
                pool.dma_start(NAT[:, 2 + d, :], pair(a[im][0])[gps]).then_inc(par_in, 16)
                pool.dma_start(LD[:, d, :], a[ld][0].rearrange("(g h) -> g h", h=2)[gps]).then_inc(par_in, 16)
                pool.dma_start(NAT[:, 6 + d, :], pair(a["state_ssm_re"][0, 0, d])[gps]).then_inc(par_in, 16)
                pool.dma_start(NAT[:, 8 + d, :], pair(a["state_ssm_im"][0, 0, d])[gps]).then_inc(par_in, 16)
            for j, (b, c) in enumerate((("ssm_b_re", "ssm_c_re"), ("ssm_b_im", "ssm_c_im"))):
                for h in range(2):
                    q = pool.dma_start(BN[64 * h:64 * h + 64, j], a[b][0].rearrange("(g h) p i -> h p g i", h=2)[h][:, gps])
                    if h == 0:
                        q.then_inc(bn_in, 16)
                    else:
                        q.then_inc(par_in, 16)
                pool.dma_start(CNAT[:, j], a[c][0].rearrange("g o p -> o g p")[:, GH_ * hf:GH_ * hf + GH_]).then_inc(par_in, 16)
            pool.dma_start(DT_, a["ssm_d"].rearrange("o (g i) -> i (o g)", i=GI)[:, GH_ * hf:GH_ * hf + GH_],
                           allow_slow_non_contiguous=True).then_inc(par_in, 16)
            if hf == 0:
                for t in range(NT):
                    pool.wait_ge(scr, t + 1)
                    pool.dma_start(scratch_su[P * t:P * (t + 1), :], SU[:, t, :]).then_inc(su_out, 16)
            pool.wait_ge(su_out, 16 * NT)
            pool.wait_ge(kp_ready, hf + 1)
            for s in range(Q):
                pool.dma_start(TOE[16 * s:16 * s + 16, :, :],
                               KP[:, :, 7 - s:15 - s, :].rearrange("i g t o -> i g (t o)")).then_inc(toe_in, 16)
            pool.wait_ge(toe_in, 16 * Q * (hf + 1))
            pool.dma_start(SRAW.rearrange("c s g i -> c s (g i)"),
                           scratch_su.rearrange("(c s) f -> c s f", s=Q)[:, :, 256 * hf:256 * hf + 256]).then_inc(sraw_in, 16)
            pool.wait_ge(sf_ready, hf + 1)
            for j, name in enumerate(("new_re", "new_im")):
                for d in range(2):
                    pool.dma_start(pair(a[name][0, 0, d])[gps], SFO[:, 2 * j + d, :]).then_inc(state_out, 16)
            pool.wait_ge(state_out, 64 * (hf + 1))
        phase_end(pool, 0)
        if STOP <= 0:
            return
        for d, name in enumerate(("ret_lg_f", "ret_lg_b")):
            pool.dma_start(LG[:, d, :], a[name].broadcast_to([P, RH])).then_inc(ret_in, 16)
            pool.dma_start(ST[:, d, 3 * d, :].rearrange("p (h e) -> p h e", h=RH),
                           a["state_ret"][0, 0, d].rearrange("h p e -> p h e")).then_inc(ret_in, 16)
        pool.dma_start(RNG, a["ret_norm_g"].broadcast_to([P, RW])).then_inc(ret_in, 16)
        pool.dma_start(DIST, a["k_dist"]).then_inc(ret_in, 16)
        pool.dma_start(MASK, a["k_mask"]).then_inc(ret_in, 16)
        pool.dma_start(ZPOS, a["k_zpos"]).then_inc(ret_in, 16)
        for d in range(2):
            pool.wait_ge(kvo_ready, d + 1)
            pool.dma_start(a["new_ret"][0, 0, d].rearrange("h p e -> p h e"),
                           KVO[:, d, :].rearrange("p (h e) -> p h e", h=RH)).then_inc(state_out, 16)
        pool.wait_ge(state_out, 128 + 32)
        phase_end(pool, 1)
        if STOP <= 1:
            return
        pool.dma_start(CK, a["cache_attn_k"][0, 0].rearrange("t h d -> t (h d)")).then_inc(att_in, 16)
        pool.dma_start(CV, a["cache_attn_v"][0, 0].rearrange("t h d -> t (h d)")).then_inc(att_in, 16)
        pool.dma_start(ROPE, a["k_rope"]).then_inc(att_in, 16)
        pool.dma_start(QGL[:, 0, :], a["att_q_norm_g"].broadcast_to([P, HD])).then_inc(att_in, 16)
        pool.dma_start(QGL[:, 1, :], a["att_k_norm_g"].broadcast_to([P, HD])).then_inc(att_in, 16)
        pool.wait_ge(kv_out, 1)
        pool.dma_start(a["new_k"][0, 0].rearrange("t h d -> t (h d)"), AQK[:, NS, AH * HD:]).then_inc(state_out, 16)
        pool.dma_start(a["new_v"][0, 0].rearrange("t h d -> t (h d)"), AV[:, NS, :]).then_inc(state_out, 16)
        pool.wait_ge(state_out, 128 + 64)
        for n in range(2, 5):
            phase_end(pool, n)
            if STOP <= n:
                return
        nc.gpsimd.memset(PACE[:, 0:1], 0.0).then_inc(pool_step, 1)
        pool.wait_ge(pool_step, 1)
        pool.wait_ge(zero_out, 16)
        pool.wait_ge(pos_ready, 1)
        pool.wait_ge(route_in, 64)
        for t in range(NT):
            for k in range(2):
                pool.indirect_dma_start(lists, bass.IndirectOffsetOnAxis(ap=CIDX[:, t, k:k + 1].bitcast(U32), axis=0),
                                        TOK[:, t:t + 1], None).then_inc(pos_out, 16)
        pool.wait_ge(pos_out, 16 * 2 * NT)
        phase_end(pool, 5)
        if STOP <= 5:
            return

        pace = [0]

        def pool_wait(s_, n):
            at_least(pool, s_, n)
            if not isinstance(n, int):
                pace[0] = pace[0] % 26 + 1
                nc.gpsimd.tensor_tensor(PACE[:, pace[0]:pace[0] + 1], PACE[:, 0:1], PACE[:, 0:1], ALU.add).then_inc(pool_step, 1)

        def pool_pass(r):
            pool_wait(idx_in, 32 * r + 32)
            for e in range(NE):
                pool_wait(g_t, 16 * r + e - 1)
                pool.indirect_dma_start(ROWS2[:, e % 2, :], None, scratch_h2,
                                        bass.IndirectOffsetOnAxis(ap=IDX[:, e:e + 1].bitcast(U32), axis=0)).then_inc(g_in[e % 2], 16)
            for b in range(2):
                pool_wait(out_wr[b], 16 * 8 * r + 16 * 8)
            pool_wait(cidx_ready, r + 1)
            for t in range(NT):
                if t >= 2:
                    pool_wait(combined, NT * r + t - 1)
                for k in range(2):
                    pool.indirect_dma_start(YR[:, t % 2, k, :], None, scratch_out,
                                            bass.IndirectOffsetOnAxis(ap=CIDX[:, t, k:k + 1].bitcast(U32), axis=0)).then_inc(y_in[t % 2], 16)
            pool_wait(combined, NT * r + NT)
            if not isinstance(r, int):
                pool.wait_ge(pool_step, pace[0] * r + 1)

        all_passes(pool, pool_pass)
        phase_end(pool, 6)

    ctx.close()




def constants():
    k = {}
    k["k_ident"] = np.eye(P, dtype=np.float32)
    k["k_upper"] = np.triu(np.ones((P, P), np.float32), 1)
    s = np.zeros((P, 2, P), np.float32)
    for j in range(4):
        s[32 * j, 0] = s[32 * j + 1, 1] = 1
    k["k_sel"] = s
    k["k_iota"] = np.tile(np.arange(NE, dtype=np.float32), (P, 1))
    k["k_tok"] = np.ascontiguousarray(np.arange(T, dtype=np.int32).reshape(NT, P).T)
    pos = np.arange(P, dtype=np.float32)
    s_, t_ = pos[:, None], pos[None, :]
    k["k_dist"] = np.stack([np.maximum(t_ - s_, 0), np.maximum(s_ - t_, 0), t_ + 1 + 0 * s_, P - t_ + 0 * s_], 1).astype(np.float32)
    k["k_mask"] = np.stack([t_ >= s_, s_ >= t_], 1).astype(np.float32)
    k["k_zpos"] = np.stack([P - 1 - pos, pos], 1).astype(np.float32)
    tok = np.arange(SAMPLE)
    inv = np.float32(10000.0) ** (-np.arange(HD // 4, dtype=np.float32) / np.float32(HD // 4))
    ang = np.concatenate([(tok // 64).astype(np.float32)[:, None] * inv, (tok % 64).astype(np.float32)[:, None] * inv], 1)
    c, s = np.repeat(np.cos(ang), 2, 1), np.repeat(np.sin(ang), 2, 1)
    s[:, 0::2] *= -1
    k["k_rope"] = np.ascontiguousarray(np.stack([c, s]).reshape(2, NS, P, HD).transpose(2, 0, 1, 3)).astype(np.float32)
    return k


_INS = ["x_prompt", "x_sample", "c", "cache_attn_k", "cache_attn_v", "state_ret", "state_ssm_re", "state_ssm_im", "c_ctx",
        "w_ada", "b_ada", "norm1_g", "norm2_g", "w_in", "ret_lg_f", "ret_lg_b", "ret_norm_g", "w_ret_out",
        "att_q_norm_g", "att_k_norm_g", "w_att_out", "a_re_f", "a_im_f", "a_re_b", "a_im_b", "log_dt_f", "log_dt_b",
        "ssm_b_re", "ssm_b_im", "ssm_c_re", "ssm_c_im", "ssm_d", "w_glu", "w_out", "w_router", "b_router",
        "w_gate", "w_up", "w_down", "final_norm_g"]
_OUTS = {"y_prompt": (1, PROMPT, D), "y_sample": (1, SAMPLE, D), "new_k": (1, 1, PROMPT, KVH, HD),
         "new_v": (1, 1, PROMPT, KVH, HD), "new_ret": (1, 1, 2, RH, P, P), "new_re": (1, 1, 2, G, PS), "new_im": (1, 1, 2, G, PS)}


def kernel(**inputs):
    import concourse.bacc as bacc
    from concourse.bass_utils import run_bass_kernel_spmd

    nc = bacc.Bacc("TRN2", target_bir_lowering=False, num_devices=1)
    arrays = {name: np.ascontiguousarray(inputs[name]) for name in _INS}
    arrays.update(constants())
    aps = {name: nc.dram_tensor(name, x.shape, mybir.dt.from_np(x.dtype), kind="ExternalInput").ap() for name, x in arrays.items()}
    for name, shape in _OUTS.items():
        aps[name] = nc.dram_tensor(name, shape, F32, kind="ExternalOutput").ap()
    build(nc, aps)
    got = run_bass_kernel_spmd(nc, [arrays], core_ids=[0]).results[0]
    return tuple(got[name] for name in _OUTS)
```

```python
import numpy as np
import concourse.bass as bass
from concourse import mybir
from contextlib import ExitStack

F32 = mybir.dt.float32
I32 = mybir.dt.int32
U32 = mybir.dt.uint32
ALU = mybir.AluOpType
ACT = mybir.ActivationFunctionType
AX = mybir.AxisListType

P = 128
D = 1024
KD = D // P
SAMPLE, PROMPT = 512, 128
T = SAMPLE + PROMPT
NT = T // P
NS = SAMPLE // P
RH, RW = 4, 512
AH, KVH, HD = 8, 2, 64
QK_W = (AH + KVH) * HD
KEYS = SAMPLE + PROMPT
G, PS, GI = 32, 64, 16
GH_, GPH = G // 2, G // 4
GP = G // 2
Q = 8
CS, CP_ = SAMPLE // Q, PROMPT // Q
NC = CS + CP_
SC = CS + 1 + CP_ + 1
NE, NG, EG = 16, 4, 4
FF = 512
CAP = 128
PASSES = T // CAP
EPS = 1e-6
COL_RQ, COL_RK, COL_RV, COL_RG, COL_AQ, COL_KV, COL_SU, COL_G = 0, 512, 1024, 1536, 2048, 2560, 2816, 3328
MAGIC = 12582912.0
LN2_HI, LN2_LO = 0.693359375, -2.12194440e-4
TWO_PI_A, TWO_PI_B = 6.28125, 0.0019350051879882812
TWO_PI_C = float(2 * np.pi - 6.28125 - 0.0019350051879882812)
EXP_C = [1 / 5040., 1 / 720., 1 / 120., 1 / 24., 1 / 6., 0.5, 1.0]


def build(nc, a, STOP=99):
    ctx = ExitStack()
    sem = lambda name: ctx.enter_context(nc.semaphore(name))

    REG_SIZE = 38740

    def sb(name, shape, dt=F32):
        return ctx.enter_context(nc.sbuf_tensor(name, shape, dt))

    ident = sb("ident", [P, P])
    upper = sb("upper", [P, P])
    ones = sb("ones", [P, P])
    sel = sb("sel", [P, 2, P])
    small = sb("small", [P, 256])
    cS = sb("cS", [P, KD, 32])
    wring = sb("wring", [P, 2, KD, 512])
    HT = sb("HT", [P, KD, T])
    REG = sb("REG", [P, REG_SIZE])

    class Region:
        def __init__(self, at=0):
            self.at = at

        def take(self, *shape, parts=P, dt=F32):
            n = int(np.prod(shape))
            assert self.at + n <= REG_SIZE, self.at + n
            v = REG[0:parts, self.at:self.at + n]
            self.at += n
            if dt is not F32:
                v = v.bitcast(dt)
            if len(shape) > 1:
                names = "abcdef"[:len(shape)]
                v = v.rearrange(f"p ({' '.join(names)}) -> p {' '.join(names)}",
                                **{n_: s for n_, s in zip(names, shape)})
            return v

    YT = Region().take(4, T)
    r = Region(4 * T)
    RQT = r.take(RH, T)
    RKT = r.take(RH, T)
    RK = r.take(NT, RW)
    RV = r.take(NT, RW)
    RG_AT = r.at
    RG = r.take(NT, RW)
    AQK_AT = r.at
    AQK = r.take(NT, QK_W)
    AV = r.take(NT, KVH * HD)
    OWN = r.at

    r = Region()
    X = r.take(NT, D)
    W_START = r.take(KD, 512)
    MODC = r.take(2, KD, 2)
    XN = r.take(2, D)
    SQ = r.take(D)
    cT = r.take(2, KD, 2)
    modrow = r.take(2, 512)
    bias_row = r.take(4, 512, parts=2)
    gain_row = r.take(D)
    assert r.at <= OWN

    r = Region(OWN)
    FM = r.take(2, 2, GPH, P)
    CPW = r.take(2, 2, GPH, 9, GI)
    TOE_AT = r.at
    TOE = r.take(GH_, P)
    U = r.take(GH_, NC)
    SY_AT = r.at
    S = r.take(Q * GH_ * GI)
    V_AT = r.at
    V = r.take(2, 2, GPH, SC)
    A8_AT = r.at
    A8 = r.take(GPH, SC)
    RT_AT = r.at
    RT = r.take(2, GPH, CS + 1)
    PAR = r.take(10, GPH)
    SC_ = [r.take(2, GPH) for _ in range(17)]
    SCI = r.take(2, GPH, dt=I32)
    SF = r.take(2, 2, GPH)
    r = Region(OWN)
    TMP4 = [r.take(GPH * SC) for _ in range(4)]
    Z = [r.take(GPH * SC) for _ in range(2)]
    assert r.at <= OWN + 4 * GPH * P
    r = Region(V_AT)
    FP = [r.take(GPH, Q, GI) for _ in range(2)]
    FPT = r.take(GPH, Q, GI)
    assert r.at <= RT_AT
    CTMP = Region(V_AT).take(GPH, 9, GI)
    KP = Region(V_AT).take(GH_, 2 * Q - 1, GI, parts=GI)
    SU = Region(TOE_AT).take(NT, 512)
    SRAW = Region(AQK_AT).take(Q, GH_, GI, parts=NC)
    SFO = Region(RT_AT).take(4, P, parts=GPH)
    RTT = Region(A8_AT).take(GPH * 32)
    NATS, CNATS, LDS, BNS = [], [], [], []
    for r, rc in ((Region(OWN), Region(TOE_AT)), (Region(AQK_AT + Q * GH_ * GI), Region(RG_AT))):
        NATS.append(r.take(10, P, parts=GPH))
        CNATS.append(rc.take(2, GH_, PS, parts=GI))
        LDS.append(r.take(2, 2, parts=GPH))
        BNS.append(r.take(2, GPH, GI))
    DTS = [None, r.take(GH_, parts=GI)]
    assert r.at <= OWN
    r = Region(SY_AT)
    CT = r.take(2, GPH, GI)
    BB = r.take(2, 2, GPH, GI)
    PW = r.take(2, 2, 9, GPH)
    BBT = r.take(GPH, GI)
    PWT = r.take(2 * 4 * GPH)
    DTS[0] = r.take(GH_, parts=GI)
    DG = r.take(GH_, GI, parts=GI)
    assert r.at <= V_AT

    r = Region(OWN)
    ROT = r.take(4, T)
    ATT_AT = r.at
    ATT = r.take(4, T)
    E4 = r.at
    ST = r.take(2, NS, RW)
    DEC = r.take(RH, P)
    XI = r.take(2, RH, P)
    ZETA = r.take(2, RH)
    CD = r.take(2, RH)
    LG = r.take(2, RH)
    DIST = r.take(4, P)
    MASK = r.take(2, P)
    ZPOS = r.take(2)
    RNG = r.take(RW)
    KVT = r.take(P)
    SS = r.take(2, RW)
    QX = r.take(2, 2, RH, P)
    RSS = r.take(3, NT * RH)
    TG5_AT = REG_SIZE - NT * 512
    assert r.at <= TG5_AT
    r = Region(ATT_AT)
    KVO = r.take(2, RW)
    VZ = r.take(3, RW)
    assert r.at <= E4
    OALL = RK
    r = Region(E4)
    QTT = r.take(4, T)
    KTT = r.take(KEYS)
    KTP = r.take(P)
    CK = r.take(KVH * HD)
    CV = r.take(KVH * HD)
    PR = r.take(2, KEYS)
    PT = r.take(2, 5 * P)
    AO = r.take(2, RW)
    ROPE = r.take(2, NS, HD)
    QGL = r.take(2, HD)
    QG = r.take(AH + KVH, HD)
    QT1 = r.take(QK_W)
    QT2 = r.take(QK_W)
    QSS = r.take(3, NT * (AH + KVH))
    ASUM = r.take(NT, AH)
    AMAX = r.take(4)
    assert r.at <= TG5_AT
    TG5 = Region(TG5_AT).take(NT, 512)
    TG = [REG[:, 4 * T + 2560 * j:4 * T + 2560 * (j + 1)].rearrange("p (t c) -> p t c", t=NT) for j in range(5)] + [TG5]

    r = Region(E4)
    MER = r.take(NT, D)
    MERT_AT = r.at
    MERT = r.take(KD, T)
    assert MERT_AT + KD * T <= TG5_AT
    r = Region(AQK_AT)
    MT1 = r.take(2, 512)
    MT2 = r.take(2, 512)
    r = Region(4 * T)
    X2 = r.take(NT, D)
    BC2 = r.take(4, 2, D)
    SLOT_AT = r.at
    modrow2 = r.take(2, 512)
    bias2 = r.take(8, 512, parts=2)
    gain2 = r.take(D)
    SQ2 = r.take(D)
    assert r.at <= MERT_AT
    r = Region(SLOT_AT)
    slots = [wring[:, j] for j in range(2)] + [r.take(KD, 512) for j in range(4)]
    WG = [slots[0], slots[3]]
    WU = [slots[1], slots[4]]
    WD = [x.rearrange("p k c -> p (k c)").rearrange("p (k c) -> p k c", k=4) for x in (slots[2], slots[5])]
    HTF = HT[:].rearrange("p k t -> p (k t)")
    ROWS2 = HTF[:, 0:2048].rearrange("p (b c) -> p b c", b=2)
    COLS2 = HTF[:, 2048:4096].rearrange("p (b k t) -> p b k t", b=2, k=KD)
    TH = HTF[:, 4096:4608]
    r0 = Region(0)
    HID = r0.take(2, 512)
    HIDT = r0.take(2, 512)
    MISC_AT = r.at
    NROWS = Region(MISC_AT).take(NT, D)
    OUT = r.take(2, D)
    r.take(3, D)
    WR = r.take(KD, NE)
    BR = r.take(NE)
    IOTA = r.take(NE)
    TOK = r.take(NT, dt=I32)
    WP = r.take(2, NT)
    PACE = r.take(27)
    ROUTE = r.take(14, NT)
    CIDX = r.take(NT, 2, dt=I32)
    IDX = r.take(NE, dt=I32)
    TOP_COUNT = r.take(1, dt=I32)
    r = Region(0)
    LOGIT, PROB, TMPR, EQ, M1, M2, MB, RANK = [r.take(NT, NE) for _ in range(8)]
    GH = [r.take(NT, NG) for _ in range(8)]
    ZERO = r.take(NE * T // P, dt=I32)
    SQ3 = r.take(D)
    assert r.at <= 4 * T
    YR = Region(SLOT_AT).take(NT, 2, D)
    COMB_STEPS = 2 * 9 + 3 * NT
    FG = COLS2[:, 0].rearrange("p k t -> p (k t)")

    banks = ctx.enter_context(nc.psum_tensor("banks", [P, 8, 512], F32))

    phase = sem("phase_joined")
    consts_in = sem("consts_in")
    c_in = sem("c_in")
    x_in = [sem(f"x_tile{t}_in") for t in range(NT)]
    turned_in, modulated = sem("input_columns_ready"), sem("input_modulated")
    rows_in = sem("rows_in")
    w_in = [sem(f"w_slot{j}_loaded") for j in range(8)]
    w_used = sem("w_blocks_used")
    full_d, free_d = sem("psum_full_for_vector"), sem("psum_emptied_by_vector")
    full_a, free_a = sem("psum_full_for_scalar"), sem("psum_emptied_by_scalar")
    full_p, free_p = sem("projection_full"), sem("projection_emptied")
    full_g, free_g = sem("gate_block_full"), sem("gate_block_emptied")
    f_ready, f_done = sem("s5_input_matrices_ready"), sem("s5_input_matrices_turned")
    cpw_ready, kp_ready, s_chunks = sem("s5_output_powers_ready"), sem("s5_lag_kernels_ready"), sem("s5_chunks_ready")
    ang_ready, sin_ready = sem("s5_angles_ready"), sem("s5_sines_ready")
    sraw_in, xi_ready, sf_ready = sem("s5_chunks_in"), sem("s5_states_ready"), sem("s5_final_states_ready")
    su_out, state_out = sem("s5_channels_stored"), sem("states_stored")
    s5_done = sem("s5_half_done")
    bc_ready = sem("modulation_spread")
    dve_step, act_step, pool_step = sem("dve_step"), sem("act_step"), sem("pool_step")
    tanh_c, silu_c = sem("tanh_c_ready"), sem("silu_c_ready")
    sq_ready = sem("squares_summed")
    mod_ready = sem("mod_row_ready")
    xn_ready = sem("xn_tile_ready")
    par_in = sem("s5_parameters_in")
    nat_ready = sem("s5_natural_ready")
    scr = sem("scratch_written")
    toe_in = sem("toeplitz_copied")
    out_done = sem("outputs_written")
    ret_in = sem("retention_inputs_in")
    ret_exp = sem("decays_ready")
    vz_ready, kv_done = sem("decayed_values_ready"), sem("new_states_ready")
    kvo_ready = sem("context_states_ready")
    sd_ready = sem("decayed_scores_ready")
    ro_gate, ro_ready = sem("retention_gate_tanh"), sem("retention_rows_ready")
    gate_step, gated, rss_ready = sem("retention_gate_step"), sem("retention_gates_ready"), sem("retention_squares_summed")
    att_in = sem("attention_inputs_in")
    qk_ready = sem("queries_keys_ready")
    kv_out = sem("context_keys_ready")
    s_full, s_max, p_ready = sem("scores_full"), sem("maximum_ready"), sem("probabilities_ready")
    pt_full, pt_ready = sem("probabilities_transposed"), sem("transposed_probabilities_ready")
    o_full, ao_ready, aot_full, aot_ready = sem("attention_out_full"), sem("attention_rows_ready"), sem("attention_rows_transposed"), sem("attention_columns_ready")
    mer_ready = sem("merged_ready")
    tb_ready, tb_used = sem("glu_tanh_ready"), sem("glu_tanh_used")
    route_in, h2_ready, h2_out = sem("router_inputs_in"), sem("normed_row_ready"), sem("normed_row_stored")
    exp_ready, masks_ready, pos_ready, pos_out, zero_ready, zero_out = (sem(n) for n in (
        "router_exponentials", "choice_masks_ready", "positions_ready", "tokens_listed", "zero_ready", "lists_zeroed"))
    idx_in = sem("token_lists_in")
    g_in = [sem("rows_gathered0"), sem("rows_gathered1")]
    wg_in = [sem("gate_weights_in0"), sem("gate_weights_in1")]
    wu_in = [sem("up_weights_in0"), sem("up_weights_in1")]
    wd_in = [sem("down_weights_in0"), sem("down_weights_in1")]
    g_t, gt_d, gt_a = sem("rows_transposed"), sem("columns_by_vector"), sem("columns_by_scalar")
    gate_full, up_full, th_ready, hid_ready = sem("gate_full"), sem("up_full"), sem("gate_tanh"), sem("hidden_ready")
    ht_full, ht_ready, dn0, dn1 = sem("hidden_transposed"), sem("hidden_columns_ready"), sem("down_half0_full"), sem("down_half1_full")
    out_d, out_a = sem("expert_out_by_vector"), sem("expert_out_by_scalar")
    out_wr = [sem("expert_rows_stored0"), sem("expert_rows_stored1")]
    hid_step, comb_step = sem("hidden_step"), sem("combine_step")
    cidx_ready, y_in, combined = sem("row_places_ready"), [sem(f"expert_rows_in{t}") for t in range(NT)], sem("tiles_combined")
    scaled_y = sem("first_rows_weighted")
    fin_in, fin_sq, fin_ready = sem("final_gain_in"), sem("final_squares"), sem("final_rows_ready")
    x2_in, x2_ready = sem("residual_in"), sem("residual_ready")

    def engine_tools(eng, step):
        count = [0]

        def done(ins):
            count[0] += 1
            ins.then_inc(step, 1)
            eng.wait_ge(step, count[0])

        def going(ins):
            count[0] += 1
            ins.then_inc(step, 1)
        return done, going, lambda: count[0]

    def phase_end(eng, n):
        eng.sem_inc(phase, 1)
        eng.wait_ge(phase, 5 * (n + 1))

    def at_least(eng, s, n):
        if not isinstance(n, int) or n > 0:
            eng.wait_ge(s, n)

    def expert_pipeline(eng, r, begin, end):
        def turn(e):
            last = None if isinstance(e, int) and e == 0 else lambda: end(16 * r + e - 1, 8 * r + i - 1, e - 1, 1)
            begin(16 * r + e, 8 * r + i, e, 0, last)
            begin(16 * r + e + 1, 8 * r + i, e + 1, 1, lambda: end(16 * r + e, 8 * r + i, e, 0))

        for i in range(2):
            turn(2 * i)
        with eng.Fori(2, NE // 2) as i:
            turn(2 * i)
        end(16 * r + 15, 8 * r + 7, 15, 1)

    def all_passes(eng, one_pass):
        one_pass(0)
        most = eng.value_load(TOP_COUNT[0:1, 0:1], min_val=0, max_val=T)
        with eng.If(most > CAP):
            with eng.Fori(1, PASSES) as r:
                one_pass(r)

    class Bank:

        def __init__(self, first, depth, full, free):
            self.first, self.depth, self.full, self.free, self.k = first, depth, full, free, 0

        def bank(self):
            return banks[:, self.first + self.k % self.depth, :]

        def open(self, pe):
            if self.k >= self.depth:
                pe.wait_ge(self.free, self.k - self.depth + 1)
            return self.bank()

        def close(self, last):
            last.then_inc(self.full, 1)
            self.k += 1

        def take(self, eng):
            eng.wait_ge(self.full, self.k + 1)
            return self.bank()

        def give(self, last):
            last.then_inc(self.free, 1)
            self.k += 1

        def all_emptied(self, pe):
            if self.k:
                pe.wait_ge(self.free, self.k)

    w_ada, w_proj = a["w_ada"][0], a["w_in"][0]
    blocks = [(w_ada, D, 512 * n, 512) for n in range(4)]
    blocks += [(w_proj, D, c, 512) for c in (COL_SU, COL_RQ, COL_RK, COL_RV, COL_RG, COL_AQ)] + [(w_proj, D, COL_KV, 256)]
    GATE_ORDER = (5, 0, 1, 2, 3, 4)
    blocks += [(w_proj, D, COL_G + D * (j % 3) + 512 * (j // 3), 512) for j in GATE_ORDER]
    FIRST_MERGE_BLOCK = len(blocks)
    FIRST_GATE_BLOCK = FIRST_MERGE_BLOCK - 6
    for n in range(2):
        blocks += [(a["w_ret_out"][0], 512, 512 * n, 512), (a["w_att_out"][0], 512, 512 * n, 512)]
        blocks += [(a["w_glu"][0], 512, 512 * n, 512), (a["w_glu"][0], 512, D + 512 * n, 512)]
    ada = lambda n: (w_ada, D, 512 * n, 512)
    w_out = a["w_out"][0]
    FIRST_LAST_BLOCK = len(blocks)
    slot_of = [0, 1, 3, 0] + [(n + 1) % 2 for n in range(4, FIRST_MERGE_BLOCK)] + [4, 5, 6, 7] * 2 + [(2, 0, 1)[j % 3] for j in range(10)]
    place = lambda m: {4: {0}, 5: {0}, 6: {1}, 7: {1}}.get(slot_of[m], {slot_of[m]})
    meet = lambda m, n: slot_of[m] == slot_of[n] or (place(m) == place(n) and (slot_of[m] < 4 or slot_of[n] < 4))
    slot_before = [max([m for m in range(n) if meet(m, n)], default=None) for n in range(len(slot_of))]
    slot_loads = [slot_of[:n + 1].count(slot_of[n]) for n in range(len(slot_of))]
    W_SLOTS = [wring[:, 0], wring[:, 1], HTF[:, 0:KD * 512].rearrange("p (k c) -> p k c", k=KD), W_START]
    W_SLOTS += [wring[:, j, 4 * h:4 * h + 4] for j in range(2) for h in range(2)]
    blocks += [ada(4), ada(5), (w_out, D, 0, 512), ada(6), ada(7), (w_out, D, 512, 512), ada(8), ada(9), ada(10), ada(11)]

    scratch_h2 = nc.dram_tensor("scratch_h2", (T, D), F32).ap()
    scratch_out = nc.dram_tensor("scratch_out", (NE * CAP, D), F32).ap()
    lists = nc.dram_tensor("token_lists", (NE * T, 1), I32).ap()
    scratch_su = nc.dram_tensor("scratch_su", (T, 512), F32).ap()

    LAST_ORDER = (4, 5, None, 6, 7, None, 8, 9, 10, 11)
    ORDER = (("modulate", 0), ("params", 0), ("su", 0), ("F", 0), 3, ("K", 0), 2, ("U", 0), 1, ("V", 0), 7, ("Y", 0), ("out", 0), ("params", 1), 5,
             ("F", 1), 3, ("K", 1), 1, ("U", 1), 1, ("V", 1), 10, ("Y", 1), ("out", 1))
    PARS = 17
    PROJ_TILES = 8 + 5 * NT
    assert sum(x for x in ORDER if isinstance(x, int)) == PROJ_TILES

    TILES_AFTER_ROW = ((), (0, 1), (2, 3, 4), ())
    GATES_IN_KV, GATES_IN_SCORES = (0, 0, 3), (0, 2)
    KV_ORDER = ((0, 0), (1, 3), (0, 1), (1, 2), (0, 2), (1, 1), (0, 4), (1, 4))
    FULL_A_BEFORE_RET = 4 + 2 * (8 + 3 + 4 + 4)
    FULL_A_BEFORE_LAST = FULL_A_BEFORE_RET + 2 * NT + NT + 2 * NT + NT

    block = ctx.enter_context(nc.Block())

    @block.sync
    def _(sp):
        sp.dma_start(cT[:, 0, :, 0], a["c"].rearrange("o (k p) -> p (o k)", p=P), allow_slow_non_contiguous=True).then_inc(c_in, 16)
        sp.dma_start(cT[:, 0, :, 1], a["c_ctx"].rearrange("(k p) -> p k", p=P), allow_slow_non_contiguous=True).then_inc(c_in, 16)
        n_loaded = [0]

        def load_block():
            n = n_loaded[0]
            n_loaded[0] += 1
            w, rows, c0, cols = blocks[n]
            if slot_before[n] is not None:
                sp.wait_ge(w_used, slot_before[n] + 1)
            sp.dma_start(W_SLOTS[slot_of[n]][:, 0:rows // P, 0:cols],
                         w[0:rows, c0:c0 + cols].rearrange("(k p) c -> p k c", p=P)).then_inc(w_in[slot_of[n]], 16)

        def load_x(t):
            src = a["x_sample"][0, P * t:P * (t + 1), :] if t < NS else a["x_prompt"][0]
            sp.dma_start(X[:, t, :], src).then_inc(x_in[t], 16)

        load_x(0)
        load_block()
        for t, src in ((ident, "k_ident"), (sel, "k_sel"), (upper, "k_upper")):
            sp.dma_start(t[:], a[src]).then_inc(consts_in, 16)
        for s in range(2):
            sp.dma_start(bias_row[s:s + 1], a["b_ada"].rearrange("o (n c) -> o n c", n=12)[:, 0:4, :]).then_inc(rows_in, 16)
        sp.dma_start(gain_row, a["norm1_g"].broadcast_to([P, D])).then_inc(rows_in, 16)
        for t in range(1, NT):
            load_x(t)
        load_block()
        load_block()
        for stage, used in enumerate((FIRST_GATE_BLOCK, FIRST_GATE_BLOCK + 1, FIRST_MERGE_BLOCK, FIRST_LAST_BLOCK)):
            while n_loaded[0] < used + (2, 2, 4, 3)[stage]:
                load_block()
            phase_end(sp, stage)
        for s in range(2):
            sp.dma_start(bias2[s:s + 1], a["b_ada"].rearrange("o (n c) -> o n c", n=12)[:, 4:12, :]).then_inc(rows_in, 16)
        sp.dma_start(gain2, a["norm2_g"].broadcast_to([P, D])).then_inc(rows_in, 16)
        for t in range(NT):
            src = a["x_sample"][0, P * t:P * (t + 1), :] if t < NS else a["x_prompt"][0]
            sp.dma_start(X2[:, t, :], src).then_inc(x2_in, 16)
        while n_loaded[0] < len(blocks):
            load_block()
        phase_end(sp, 4)
        if STOP <= 4:
            return
        n_out = 0
        sp.dma_start(WR, a["w_router"].rearrange("(k p) e -> p k e", p=P)).then_inc(route_in, 16)
        sp.dma_start(BR, a["b_router"].rearrange("(o e) -> o e", o=1).broadcast_to([P, NE])).then_inc(route_in, 16)
        sp.dma_start(IOTA, a["k_iota"]).then_inc(route_in, 16)
        sp.dma_start(TOK, a["k_tok"]).then_inc(route_in, 16)
        def weights_in(n, m, e, b):
            at_least(sp, up_full, n - 1)
            sp.dma_start(WG[b], a["w_gate"][0][e].rearrange("(k p) c -> p k c", p=P)).then_inc(wg_in[b], 16)
            sp.dma_start(WU[b], a["w_up"][0][e].rearrange("(k p) c -> p k c", p=P)).then_inc(wu_in[b], 16)
            at_least(sp, dn1, n - 1)
            sp.dma_start(WD[b], a["w_down"][0][e].rearrange("(k p) c -> p k c", p=P)).then_inc(wd_in[b], 16)

        sp.wait_ge(h2_ready, NT)
        for e in range(2):
            weights_in(e, 0, e, e)
        phase_end(sp, 5)
        if STOP <= 5:
            return

        def sp_pass(r):
            if not isinstance(r, int):
                sp.wait_ge(fin_sq, NT * r)
            for k in range(2):
                sp.dma_start(IDX[:, 8 * k:8 * k + 8], lists.rearrange("(e r) o -> r (e o)", r=T)[bass.ds(CAP * r, CAP), 8 * k:8 * k + 8],
                             allow_slow_non_contiguous=True).then_inc(idx_in, 16)
            if not isinstance(r, int):
                for e in range(2):
                    weights_in(16 * r + e, 8 * r, e, e)
            with sp.Fori(1, NE // 2) as i:
                for b in range(2):
                    weights_in(16 * r + 2 * i + b, 8 * r + i, 2 * i + b, b)

        all_passes(sp, sp_pass)
        phase_end(sp, 6)
        if STOP <= 6:
            return
        sp.dma_start(FG, a["final_norm_g"].rearrange("(o e) -> o e", o=1).broadcast_to([P, D])).then_inc(fin_in, 16)
        for t in range(NT):
            sp.wait_ge(fin_ready, t + 1)
            dst = a["y_sample"][0, P * t:P * (t + 1), :] if t < NS else a["y_prompt"][0]
            sp.dma_start(dst, X2[:, t, :]).then_inc(out_done, 16)
        n_out += NT
        sp.wait_ge(out_done, 16 * n_out)

    @block.tensor
    def _(pe):
        vec, sca = Bank(0, 4, full_d, free_d), Bank(4, 2, full_a, free_a)
        pro, gat = Bank(6, 2, full_p, free_p), Bank(7, 1, full_g, free_g)
        wcount = [0]
        mm = nc.tensor.matmul

        def all_emptied():
            vec.all_emptied(pe)
            sca.all_emptied(pe)

        def weights():
            n = wcount[0]
            wcount[0] += 1
            pe.wait_ge(w_in[slot_of[n]], 16 * slot_loads[n])
            return W_SLOTS[slot_of[n]]

        def weights_used(bank):
            pe.wait_ge(bank.full, bank.k)
            pe.sem_inc(w_used, 1)

        def transposes(chan, blocks_):
            out = chan.open(pe)
            for j, src in enumerate(blocks_):
                last = nc.tensor.transpose(out[:, P * j:P * j + P], src, ident[:])
            chan.close(last)

        def ada_row(n):
            w = weights()
            out = vec.open(pe)
            for k in range(KD):
                j = k % 4
                last = mm(out[32 * j:32 * j + 32, :], cS[:, k, :], w[:, k, :], start=k < 4, stop=k >= 4)
            vec.close(last)
            weights_used(vec)

        def ada_columns(n):
            pe.wait_ge(mod_ready, n + 1)
            out = sca.open(pe)
            for j in range(4):
                last = mm(out[:, 2 * j:2 * j + 2], modrow[:, n % 2, P * j:P * j + P], sel[:, :, 0], start=True, stop=True)
            sca.close(last)

        def project(out, w, t, cols=512):
            for k in range(KD):
                last = mm(out[:, 0:cols], HT[:, k, P * t:P * t + P], w[:, k, 0:cols], start=k == 0, stop=k == KD - 1)
            return last

        proj = [0, None]

        def tiles(count):
            for _ in range(count):
                i = proj[0]
                proj[0] += 1
                if i == 0 or i >= 8 and (i - 8) % NT == 0:
                    proj[1] = weights()
                out = pro.open(pe)
                if i < 8:
                    h, context = i // 2, i % 2
                    cols = slice(SAMPLE, T) if context else slice(0, SAMPLE)
                    for k in range(KD):
                        last = mm(out[:, 0:PROMPT if context else SAMPLE], proj[1][:, k, P * h:P * h + P], HT[:, k, cols],
                                  start=k == 0, stop=k == KD - 1)
                else:
                    last = project(out, proj[1], (i - 8) % NT, 512 if i < 8 + 4 * NT else 256)
                pro.close(last)
                if i == 7 or i > 8 and (i - 8) % NT == NT - 1:
                    weights_used(pro)

        def modulate(_):
            pe.wait_ge(silu_c, 1)
            for n in range(4):
                ada_row(n)
                for t in TILES_AFTER_ROW[n]:
                    pe.wait_ge(xn_ready, t + 1)
                    for half in range(2):
                        transposes(vec, [XN[:, t % 2, P * k:P * k + P] for k in range(4 * half, 4 * half + 4)])
                ada_columns(n)
            pe.wait_ge(modulated, 2)

        def params(hf):
            pe.wait_ge(par_in, 16 * PARS * (hf + 1))
            pe.wait_ge(nat_ready, hf + 1)
            out = vec.open(pe)
            for j in range(10):
                last = nc.tensor.transpose(out[:, GPH * j:GPH * j + GPH], NATS[hf][:, j, :], ident[0:GPH, 0:GPH])
            vec.close(last)
            for j in range(2):
                out = vec.open(pe)
                for p in range(GPH):
                    last = nc.tensor.transpose(out[:, 16 * p:16 * p + 16],
                                               CNATS[hf][:, j, 2 * p:2 * p + 2, :].rearrange("o g p -> o (g p)"), ident[0:16, 0:16])
                vec.close(last)

        def turn_F(hf):
            for d in range(2):
                pe.wait_ge(f_ready, 2 * hf + d + 1)
                for j in range(2):
                    for q in range(2):
                        transposes(sca, [FP[j][:, 4 * q + p].rearrange("p s i -> p (s i)") for p in range(4)])

        def lag_kernels(hf):
            pe.wait_ge(cpw_ready, hf + 1)
            for d in range(2):
                for q in range(4):
                    out = vec.open(pe)
                    for j in range(4):
                        h, p = q % 2, 4 * (q // 2) + j
                        hs = slice(64 * h, 64 * h + 64)
                        for c in range(2):
                            last = mm(out[0:GI, P * j:P * j + P], BB[hs, d, c, p, :],
                                      CPW[hs, d, c, p, 0:Q, :].rearrange("p k o -> p (k o)"), start=c == 0, stop=c == 1)
                    vec.close(last)

        def su_rows(_):
            w = weights()
            for t in range(NT):
                pro.close(project(pro.open(pe), w, t))
            weights_used(pro)

        def turn_U(hf):
            pe.wait_ge(s_chunks, hf + 1)
            for q in range(3):
                gs = range(6 * q, min(6 * q + 6, GH_))
                out = sca.open(pe)
                for j, g in enumerate(gs):
                    last = nc.tensor.transpose(out[:, NC * j:NC * j + NC], S[0:NC, P * g:P * g + P], ident[0:NC, 0:NC])
                sca.close(last)
            sca.all_emptied(pe)

        def chunk_inputs(hf):
            for d in range(2):
                for c in range(2):
                    for q in range(2):
                        ps = range(6 * q, min(6 * q + 6, GPH))
                        out = vec.open(pe)
                        for j, p in enumerate(ps):
                            for h in range(2):
                                last = mm(out[64 * h:64 * h + 64, NC * j:NC * j + NC], FM[:, d, c, p, 64 * h:64 * h + 64],
                                          U[:, 2 * p + h, :], start=True, stop=True)
                        vec.close(last)

        def chunk_outputs(hf):
            pe.wait_ge(toe_in, 16 * Q * (hf + 1))
            pe.wait_ge(xi_ready, hf + 1)
            for q in range(4):
                out = sca.open(pe)
                for j in range(4):
                    h, p = q % 2, 4 * (q // 2) + j
                    g = 2 * p + h
                    hs = slice(64 * h, 64 * h + 64)
                    o = out[0:NC, P * j:P * j + P]
                    mm(o, U[:, g, :], TOE[:, g, :], start=True, stop=False)
                    for d in range(2):
                        for c in range(2):
                            xin = V[hs, d, c, :, :].rearrange("p a b -> p (a b)")[:, NC * p:NC * p + NC]
                            pw = CPW[hs, d, c, p, 1:Q + 1, :]
                            if d:
                                pw = pw[:, ::-1, :]
                            last = mm(o, xin, pw, start=False, stop=d + c == 2)
                sca.close(last)
            out = vec.open(pe)
            for j in range(4):
                last = mm(out[0:GPH, P * j:P * j + P], SF[:, j // 2, j % 2, :], ident[:], start=True, stop=True)
            vec.close(last)

        def turn_outputs_s5(hf):
            sca.all_emptied(pe)
            Y = S[0:NC, :].rearrange("c (t f) -> c t f", t=Q)
            for kb in range(2):
                for th in range(2):
                    out = sca.open(pe)
                    for j in range(4):
                        last = nc.tensor.transpose(out[:, NC * j:NC * j + NC], Y[:, 4 * th + j, P * kb:P * kb + P], ident[0:NC, 0:NC])
                    sca.close(last)

        pe.wait_ge(consts_in, 48)
        steps = dict(params=params, modulate=modulate, su=su_rows, F=turn_F, K=lag_kernels, U=turn_U, V=chunk_inputs, Y=chunk_outputs,
                     out=turn_outputs_s5)
        for step in ORDER:
            if isinstance(step, int):
                tiles(step)
            else:
                steps[step[0]](step[1])
        phase_end(pe, 0)
        if STOP <= 0:
            return

        gate = [0, None]

        def gate_half(chan, half):
            i = gate[0]
            if half == 0:
                if i % NT == 0:
                    gate[1] = weights()
                chan.open(pe)
            for k in range(4 * half, 4 * half + 4):
                last = mm(chan.bank(), HT[:, k, P * (i % NT):P * (i % NT) + P], gate[1][:, k, :], start=k == 0, stop=k == KD - 1)
            if half == 1:
                chan.close(last)
                gate[0] += 1
                if i % NT == NT - 1:
                    weights_used(chan)

        def gate_tile():
            gate_half(pro, 0)
            gate_half(pro, 1)

        for t in range(NT):
            transposes(vec, [RK[:, t, P * h:P * h + P] for h in range(RH)])
        for i, (d, t) in enumerate(KV_ORDER):
            for _ in range(GATES_IN_KV.count(i)):
                gate_tile()
            pe.wait_ge(vz_ready, i + 1)
            out = vec.open(pe)
            for h in range(RH):
                hs = slice(P * h, P * h + P)
                last = mm(out[:, hs], RK[:, t, hs], VZ[:, i % 3, hs], start=True, stop=True)
            vec.close(last)
        pe.wait_ge(kv_done, len(KV_ORDER))
        for t in range(NT):
            ts_ = slice(P * t, P * t + P)
            out = vec.open(pe)
            for h in range(RH):
                last = mm(out[:, P * h:P * h + P], RKT[:, h, ts_], RQT[:, h, ts_], start=True, stop=True)
            vec.close(last)
            if t in GATES_IN_SCORES:
                gate_tile()
            pe.wait_ge(sd_ready, t + 1)
            out = sca.open(pe)
            for h in range(RH):
                hs = slice(P * h, P * h + P)
                last = mm(out[:, hs], SS[:, t % 2, hs], RV[:, t, hs], start=True, stop=t == NS)
                if t < NS:
                    for d in range(2):
                        last = mm(out[:, hs], QX[:, t % 2, d, h, :], ST[:, d, t, hs], start=False, stop=d == 1)
            sca.close(last)
        for t in range(NT):
            pe.wait_ge(ro_ready, t + 1)
            transposes(sca, [OALL[:, t, P * h:P * h + P] for h in range(RH)])
        phase_end(pe, 1)
        if STOP <= 1:
            return

        for _ in range(NT):
            gate_tile()
        pe.wait_ge(free_p, pro.k)
        pe.wait_ge(qk_ready, 1)
        for t in range(NT):
            transposes(sca, [AQK[:, t, P * b:P * b + P] for b in range(4)])
        transposes(vec, [AQK[:, t, 512:640] for t in range(NS)])
        transposes(vec, [CK, AQK[:, NS, 512:640]])
        all_emptied()
        flat = banks[:].rearrange("p b c -> p (b c)")
        units = [(t, b, half) for t in range(NT) for b in range(4) for half in range(2)]

        def keys_of(t):
            return KEYS if t < NS else P

        def scores(i):
            t, b, half = units[i]
            if i >= 2:
                pe.wait_ge(p_ready, i - 1)
            hs = slice(64 * half, 64 * half + 64)
            q = QTT[hs, b, P * t:P * t + P]
            at = 1024 * half
            if t < NS:
                mm(flat[:, at:at + 512], q, KTT[hs, 0:512], start=True, stop=True)
                last = mm(flat[:, at + 512:at + 640], q, KTT[hs, 512:640], start=True, stop=True)
            else:
                last = mm(flat[:, at:at + P], q, KTP[hs, :], start=True, stop=True)
            last.then_inc(s_full, 1)

        def turn_probabilities(i):
            t = units[i][0]
            pe.wait_ge(p_ready, i + 1)
            if i >= 1:
                pe.wait_ge(pt_ready, i)
            if turned[0]:
                pe.wait_ge(aot_ready, turned[0])
            for c in range(keys_of(t) // P):
                last = nc.tensor.transpose(flat[:, 2048 + P * c:2048 + P * c + P], PR[:, i % 2, P * c:P * c + P], ident[:])
            last.then_inc(pt_full, 1)

        def values(i):
            t, b, half = units[i]
            pe.wait_ge(pt_ready, i + 1)
            if b == half == 0 and t >= 1:
                pe.wait_ge(ao_ready, t)
            head = b + 4 * half
            n = keys_of(t) // P
            for c in range(n):
                if t < NS:
                    v = AV[:, c, :] if c < NS else CV
                else:
                    v = AV[:, NS, :]
                last = mm(banks[:, 6, 64 * head:64 * head + 64], PT[:, i % 2, P * c:P * c + P],
                          v[:, 64 * half:64 * half + 64], start=c == 0, stop=c == n - 1)
            last.then_inc(o_full, 1)

        def turn_outputs(t):
            pe.wait_ge(ao_ready, t + 1)
            pe.wait_ge(pt_ready, 8 * t + (8 if t == NT - 1 else 11))
            turned[0] = t + 1
            for b in range(4):
                last = nc.tensor.transpose(banks[:, 4, P * b:P * b + P], AO[:, t % 2, P * b:P * b + P], ident[:])
            last.then_inc(aot_full, 1)

        turned = [0]
        scores(0)
        for i in range(len(units)):
            if i + 1 < len(units):
                scores(i + 1)
            gate_half(gat, i % 2)
            turn_probabilities(i)
            if i >= 1:
                values(i - 1)
            if i % 8 == 2 and i > 8:
                turn_outputs(i // 8 - 1)
        values(len(units) - 1)
        turn_outputs(NT - 1)
        phase_end(pe, 2)
        if STOP <= 2:
            return

        for n in range(2):
            for branch, x in enumerate((ROT, ATT, YT)):
                chans = (vec,) if branch < 2 else (vec, sca)
                ws = [weights() for _ in chans]
                for t in range(NT):
                    for chan, w in list(zip(chans, ws))[::-1]:
                        out = chan.open(pe)
                        for k in range(4):
                            last = mm(out, x[:, k, P * t:P * t + P], w[:, k, :], start=k == 0, stop=k == 3)
                        chan.close(last)
                for _ in chans:
                    weights_used(vec)
        for t in range(NT):
            pe.wait_ge(mer_ready, t + 1)
            for half in range(2):
                transposes((vec, sca)[half], [MER[:, t, P * k:P * k + P] for k in range(4 * half, 4 * half + 4)])
        phase_end(pe, 3)
        if STOP <= 3:
            return

        def project_out():
            w = weights()
            for t in range(NT):
                out = vec.open(pe)
                for k in range(KD):
                    last = mm(out, MERT[:, k, P * t:P * t + P], w[:, k, :], start=k == 0, stop=k == KD - 1)
                vec.close(last)
            weights_used(vec)

        behind = []

        def spread_one():
            n = behind.pop(0)
            pe.wait_ge(mod_ready, n + 1)
            for s in range(2):
                sca.close(mm(sca.open(pe), sel[:, s, :], modrow2[:, n % 2, :], start=True, stop=True))

        for step in LAST_ORDER:
            if step is None:
                while behind:
                    spread_one()
                project_out()
                continue
            ada_row(step)
            behind.append(step)
            if len(behind) > 1:
                spread_one()
        spread_one()
        phase_end(pe, 4)
        if STOP <= 4:
            return

        pe.wait_ge(route_in, 64)
        turned = [(0, 0)] * NT

        def turn_rows(t):
            pe.wait_ge(h2_ready, t + 1)
            for half in (1, 0):
                transposes((vec, sca)[half], [NROWS[:, t, P * k:P * k + P] for k in range(4 * half, 4 * half + 4)])
            turned[t] = vec.k, sca.k

        turn_rows(0)
        for t in range(NT):
            if t + 1 < NT:
                turn_rows(t + 1)
            pe.wait_ge(free_d, turned[t][0])
            pe.wait_ge(free_a, turned[t][1])
            out = vec.open(pe)
            for k in range(KD):
                last = mm(out[:, 0:NE], COLS2[:, t % 2, k, :], WR[:, k, :], start=k == 0, stop=k == KD - 1)
            vec.close(last)
        pe.wait_ge(masks_ready, 1)
        out = vec.open(pe)
        mb = MB.rearrange("p t e -> p (t e)")
        mm(out[:, 0:NE * NT], upper[:], mb, start=True, stop=True)
        last = mm(out[:, NE * NT:2 * NE * NT], ones[:], mb, start=True, stop=True)
        vec.close(last)
        phase_end(pe, 5)
        if STOP <= 5:
            return

        def down(n, m, e, b):
            pe.wait_ge(hid_ready, n + 1)
            at_least(pe, ht_ready, n)
            for k in range(4):
                last = nc.tensor.transpose(banks[:, 4, P * k:P * k + P], HID[:, b, P * k:P * k + P], ident[:])
            last.then_inc(ht_full, 1)
            pe.wait_ge(ht_ready, n + 1)
            pe.wait_ge(wd_in[b], 16 * m + 16)
            for half, (full, emptied) in enumerate(((dn0, out_d), (dn1, out_a))):
                at_least(pe, emptied, n)
                for k in range(4):
                    last = mm(banks[:, 5 + half, :], HIDT[:, b, P * k:P * k + P], WD[b][:, k, 512 * half:512 * half + 512],
                              start=k == 0, stop=k == 3)
                last.then_inc(full, 1)

        def gate_up(n, m, e, b, before):
            pe.wait_ge(g_in[b], 16 * m + 16)
            at_least(pe, gt_d, n)
            at_least(pe, gt_a, n)
            for k in range(KD):
                last = nc.tensor.transpose(banks[:, k // 4, P * (k % 4):P * (k % 4) + P], ROWS2[:, b, P * k:P * k + P], ident[:])
            last.then_inc(g_t, 1)
            if before:
                before()
            pe.wait_ge(gt_d, n + 1)
            pe.wait_ge(gt_a, n + 1)
            at_least(pe, hid_ready, n)
            for bank, w, w_in_, full in ((2, WG, wg_in, gate_full), (3, WU, wu_in, up_full)):
                pe.wait_ge(w_in_[b], 16 * m + 16)
                for k in range(KD):
                    last = mm(banks[:, bank, :], COLS2[:, b, k, :], w[b][:, k, :], start=k == 0, stop=k == KD - 1)
                last.then_inc(full, 1)

        all_passes(pe, lambda r: expert_pipeline(pe, r, gate_up, down))
        phase_end(pe, 6)

    @block.scalar
    def _(act):
        sca = Bank(4, 2, full_a, free_a)
        pro, gat = Bank(6, 2, full_p, free_p), Bank(7, 1, full_g, free_g)
        act_done, act_going, act_steps_so_far = engine_tools(act, act_step)
        A = nc.scalar.activation
        four = lambda x: x.rearrange("p (a b) -> p a b", a=4)

        def copy_out(dst):
            src = sca.take(act)
            sca.give(A(dst, src, ACT.Copy))

        act.wait_ge(c_in, 32)
        A(cT[:, 1], cT[:, 0], ACT.Tanh, scale=0.5).then_inc(tanh_c, 1)

        def params(hf):
            act.wait_ge(ang_ready, hf + 1)
            act_done(A(SC_[4], SC_[3], ACT.Sin))
            A(SC_[5], SC_[3], ACT.Sin, scale=0.5).then_inc(sin_ready, 1)

        def modulate(_):
            for t in range(NT):
                act.wait_ge(x_in[t], 16)
                act_done(A(SQ, X[:, t, :], ACT.Square, accum_out=small[:, t:t + 1]))
            act.sem_inc(sq_ready, 1)
            for n in range(4):
                src = sca.take(act)
                sca.give(A(MODC[:, n // 2, 4 * (n % 2):4 * (n % 2) + 4, :], src[:, 0:8].rearrange("p (k s) -> p k s", s=2), ACT.Copy))
            act.wait_ge(free_a, sca.k)
            act.sem_inc(bc_ready, 1)
            act.wait_ge(turned_in, 1)
            for s, cols in enumerate((slice(0, SAMPLE), slice(SAMPLE, T))):
                for k in range(5, KD):
                    act_going(A(HT[:, k, cols], HT[:, k, cols], ACT.Identity, scale=MODC[:, 1, k, s:s + 1], bias=MODC[:, 0, k, s:s + 1]))
            act.wait_ge(act_step, act_steps_so_far())
            act.sem_inc(modulated, 1)

        def turn_F(hf):
            for d in range(2):
                for j in range(2):
                    for q in range(2):
                        src = sca.take(act)
                        sca.give(A(FM[:, d, j, 4 * q:4 * q + 4, :], four(src), ACT.Copy))
                act.wait_ge(free_a, sca.k)
                act.sem_inc(f_done, 1)

        def su_rows(_):
            for t in range(NT):
                src = pro.take(act)
                pro.give(A(SU[:, t, :], src, ACT.Copy))
                act.wait_ge(free_p, pro.k)
                act.sem_inc(scr, 1)

        def turn_U(hf):
            for q in range(3):
                n = min(6, GH_ - 6 * q)
                src = sca.take(act)
                sca.give(A(U[:, 6 * q:6 * q + n, :], src[:, 0:NC * n].rearrange("p (a b) -> p a b", a=n), ACT.Copy))

        def chunk_outputs(hf):
            Y = S[0:NC, :].rearrange("c (t g o) -> c g t o", t=Q, g=GH_)
            for q in range(4):
                src = sca.take(act)
                sca.give(A(Y[:, 8 * (q // 2) + q % 2:8 * (q // 2) + 8:2], src[0:NC].rearrange("c (g t o) -> c g t o", g=4, t=Q),
                           ACT.Gelu_apprx_tanh))

        def turn_outputs_s5(hf):
            for kb in range(2):
                for th in range(2):
                    src = sca.take(act)
                    dst = YT[:, 2 * hf + kb, :].rearrange("p (c t) -> p t c", t=Q)[:, 4 * th:4 * th + 4, :]
                    sca.give(A(dst, src[:, 0:4 * NC].rearrange("p (t c) -> p t c", t=4), ACT.Copy))
            act.wait_ge(free_a, sca.k)
            act.sem_inc(s5_done, 1)

        proj = [0]

        def tiles(count):
            for _ in range(count):
                i = proj[0]
                proj[0] += 1
                src = pro.take(act)
                if i < 8:
                    h, context = i // 2, i % 2
                    cols = slice(SAMPLE, T) if context else slice(0, SAMPLE)
                    pro.give(A(RQT[:, h, cols], src[:, 0:PROMPT if context else SAMPLE], ACT.Copy, scale=float(P) ** -0.5))
                    continue
                b, t = (i - 8) // NT, (i - 8) % NT
                if b < 4:
                    pro.give(A((RK, RV, RG, AQK[:, :, 0:512])[b][:, t, :], src, ACT.Copy))
                else:
                    act_done(A(AQK[:, t, 512:640], src[:, 0:128], ACT.Copy))
                    pro.give(A(AV[:, t, :], src[:, 128:256], ACT.Copy))

        none = lambda hf: None
        steps = dict(params=params, modulate=modulate, su=su_rows, F=turn_F, K=none, U=turn_U, V=none, Y=chunk_outputs,
                     out=turn_outputs_s5)
        for step in ORDER:
            if isinstance(step, int):
                tiles(step)
            else:
                steps[step[0]](step[1])
        act.wait_ge(free_p, pro.k)
        phase_end(act, 0)
        if STOP <= 0:
            return

        act.wait_ge(ret_in, 16 * 8)
        for d in range(2):
            for h in range(RH):
                lg = LG[:, d, h:h + 1]
                A(QX[:, 0, d, h, :], DIST[:, d, :], ACT.Exp, scale=lg)
                A(XI[:, d, h, :], DIST[:, 2 + d, :], ACT.Exp, scale=lg)
                A(ZETA[:, d, h:h + 1], ZPOS[:, d:d + 1], ACT.Exp, scale=lg)
        act_done(A(CD, LG, ACT.Exp, scale=float(P)))
        act.sem_inc(ret_exp, 1)
        tanhs = [0]

        def gate_out(chan):
            i = tanhs[0]
            tanhs[0] += 1
            src = chan.take(act)
            chan.give(A(TG[GATE_ORDER[i // NT]][:, i % NT, :], src, ACT.Tanh, scale=0.5))

        for i, (d, t) in enumerate(KV_ORDER):
            if i >= 3:
                act.wait_ge(kv_done, i - 2)
            for h in range(RH):
                hs = slice(P * h, P * h + P)
                last = A(VZ[:, i % 3, hs], RV[:, t, hs], ACT.Copy, scale=ZETA[:, d, h:h + 1])
            last.then_inc(vz_ready, 1)
            for _ in range(GATES_IN_KV.count(i - 2)):
                gate_out(pro)
        act.wait_ge(kv_done, len(KV_ORDER))

        def gate_tanh(t):
            if t >= 3:
                act.wait_ge(gated, t - 2)
            A(VZ[:, t % 3, :], RG[:, t, :], ACT.Tanh, scale=0.5).then_inc(ro_gate, 1)

        for t in range(NT):
            gate_tanh(t)
            if t in GATES_IN_SCORES:
                gate_out(pro)
            src = sca.take(act)
            for h in range(RH):
                act_done(A(KVT, src[:, P * h:P * h + P], ACT.Square, accum_out=RSS[:, 0, RH * t + h:RH * t + h + 1]))
            sca.give(A(OALL[:, t, :], src, ACT.Copy))
        act.wait_ge(free_a, sca.k)
        act.sem_inc(rss_ready, 1)
        for t in range(NT - 1):
            src = sca.take(act)
            sca.give(A(ROT[:, :, P * t:P * t + P], src.rearrange("p (a b) -> p a b", a=4), ACT.Copy, scale=0.5))
        src = sca.take(act)
        sca.give(A(ROT[:, :, P * (NT - 1):P * NT], src.rearrange("p (a b) -> p a b", a=4), ACT.Copy, scale=0.5))
        act.wait_ge(free_a, sca.k)
        act.wait_ge(free_p, pro.k)
        phase_end(act, 1)
        if STOP <= 1:
            return

        for _ in range(NT):
            gate_out(pro)
        for t in range(NT):
            src = sca.take(act)
            sca.give(A(QTT[:, :, P * t:P * t + P], src.rearrange("p (a b) -> p a b", a=4), ACT.Copy, scale=float(HD) ** -0.5))
        flat = banks[:].rearrange("p b c -> p (b c)")
        for i in range(8 * NT):
            t, b, half = i // 8, i % 8 // 2, i % 2
            n = KEYS if t < NS else P
            act.wait_ge(s_max, i + 1)
            if i >= 2:
                act.wait_ge(pt_full, i - 1)
            head = b + 4 * half
            A(PR[:, i % 2, 0:n], flat[:, 1024 * half:1024 * half + n], ACT.Exp, bias=AMAX[:, i % 4:i % 4 + 1],
              accum_out=ASUM[:, t, head:head + 1]).then_inc(p_ready, 1)
            if i % 2:
                gate_out(gat)
        act.wait_ge(free_g, gat.k)
        phase_end(act, 2)
        if STOP <= 2:
            return

        for i in range(2 * NT):
            src = sca.take(act)
            if i >= 2:
                act.wait_ge(tb_used, i - 1)
            act_done(A(MT1[:, i % 2, :], src, ACT.Tanh, scale=0.5))
            act.sem_inc(free_a, 1); sca.k += 1
            act.sem_inc(tb_ready, 1)
        for t in range(NT):
            src = sca.take(act)
            sca.give(A(MERT[:, 4:8, P * t:P * t + P], src.rearrange("p (a b) -> p a b", a=4), ACT.Copy, scale=0.5))
        act.wait_ge(free_a, sca.k)
        phase_end(act, 3)
        if STOP <= 3:
            return

        for n in range(8):
            if n == 4:
                for t in range(NT):
                    act.wait_ge(x2_ready, t + 1)
                    act_done(A(SQ3, X2[:, t, :], ACT.Square, accum_out=small[:, t:t + 1]))
                act.sem_inc(sq_ready, 1)
            for s in range(2):
                copy_out(BC2[:, n // 2, s, 512 * (n % 2):512 * (n % 2) + 512])
            act.wait_ge(free_a, sca.k)
            act.sem_inc(bc_ready, 1)
        phase_end(act, 4)
        if STOP <= 4:
            return

        for t in range(NT):
            src = sca.take(act)
            sca.give(A(COLS2[:, t % 2, 4:8, :], src.rearrange("p (a b) -> p a b", a=4), ACT.Copy))
        act.wait_ge(exp_ready, 1)
        act_done(A(PROB, LOGIT, ACT.Exp))
        act.sem_inc(exp_ready, 1)
        phase_end(act, 5)
        if STOP <= 5:
            return

        def act_end(n, m, e, b):
            act.wait_ge(ht_full, n + 1)
            at_least(act, dn1, n - 1)
            A(HIDT[:, b, :], banks[:, 4, :], ACT.Copy).then_inc(ht_ready, 1)
            act.wait_ge(dn1, n + 1)
            at_least(act, out_wr[b], 16 * m)
            A(OUT[:, b, 512:1024], banks[:, 6, :], ACT.Copy).then_inc(out_a, 1)
            act.wait_ge(out_a, n + 1)
            act.wait_ge(out_d, n + 1)
            act.dma_start(scratch_out.rearrange("(e p) c -> e p c", p=CAP)[e], OUT[:, b, :]).then_inc(out_wr[b], 16)

        def act_begin(n, m, e, b, before):
            act.wait_ge(g_t, n + 1)
            at_least(act, up_full, n - 1)
            A(COLS2[:, b, 4:8, :], banks[:, 1, :].rearrange("p (a b) -> p a b", a=4), ACT.Copy).then_inc(gt_a, 1)
            if before:
                before()
            act.wait_ge(gate_full, n + 1)
            at_least(act, hid_ready, n)
            A(TH, banks[:, 2, :], ACT.Tanh, scale=0.5).then_inc(th_ready, 1)

        def act_pass(r):
            expert_pipeline(act, r, act_begin, act_end)
            act.wait_ge(cidx_ready, r + 1)
            for t in range(NT):
                act.wait_ge(y_in[t], 32 * r + 32)
                A(YR[:, t, 0, :], YR[:, t, 0, :], ACT.Copy, scale=WP[:, 0, t:t + 1]).then_inc(scaled_y, 1)
                if t >= 1:
                    squares(r, t - 1)
            squares(r, NT - 1)

        def squares(r, t):
            act.wait_ge(combined, NT * r + t + 1)
            A(YR[:, t, 0, :], X2[:, t, :], ACT.Square, accum_out=small[:, t:t + 1]).then_inc(fin_sq, 1)
            act.wait_ge(fin_sq, NT * r + t + 1)

        all_passes(act, act_pass)
        phase_end(act, 6)

    @block.vector
    def _(dve):
        vec = Bank(0, 4, full_d, free_d)
        done, going, steps_so_far = engine_tools(dve, dve_step)
        V_ = nc.vector
        tt, ts, stt, cp = V_.tensor_tensor, V_.tensor_scalar, V_.scalar_tensor_tensor, V_.tensor_copy

        def rsqrt(out, x, t):
            done(ts(out.bitcast(I32), x.bitcast(I32), -0.5, float(0x5f3759df), ALU.mult, ALU.add))
            for _ in range(3):
                done(tt(t, out, out, ALU.mult))
                done(tt(t, t, x, ALU.mult))
                done(ts(t, t, -0.5, 1.5, ALU.mult, ALU.add))
                done(tt(out, out, t, ALU.mult))

        def exact_exp(out, x, t, r, k):
            done(ts(r, x, -87.0, 88.0, ALU.max, ALU.min))
            done(ts(t, r, 1.4426950408889634, MAGIC, ALU.mult, ALU.add))
            done(ts(t, t, -MAGIC, None, ALU.add))
            done(ts(k, t, 127.0, 8388608.0, ALU.add, ALU.mult))
            done(stt(r, t, -LN2_HI, r, ALU.mult, ALU.add))
            done(stt(r, t, -LN2_LO, r, ALU.mult, ALU.add))
            done(ts(out, r, EXP_C[0], None, ALU.mult))
            for c in EXP_C[1:]:
                done(stt(out, out, c, r, ALU.add, ALU.mult))
            done(ts(out, out, 1.0, None, ALU.add))
            done(tt(out, out, k.bitcast(F32), ALU.mult))

        def cmul(ore, oim, ar, ai, br, bi, t):
            going(tt(t, ar, br, ALU.mult))
            done(tt(ore, ai, bi, ALU.mult))
            done(tt(ore, t, ore, ALU.subtract))
            going(tt(t, ar, bi, ALU.mult))
            done(tt(oim, ai, br, ALU.mult))
            done(tt(oim, t, oim, ALU.add))

        done(V_.memset(ones[:], 1.0))
        done(V_.memset(cS[:], 0.0))
        dve.wait_ge(tanh_c, 1)
        done(stt(cT[:, 1], cT[:, 1], 1.0, cT[:, 0], ALU.add, ALU.mult))
        ts(cS[:, :, 0:2], cT[:, 1], 0.5, None, ALU.mult).then_inc(silu_c, 1)

        def mod_row(n, row, bias, gain):
            src = vec.take(dve)
            done(cp(row, src))
            dve.sem_inc(free_d, 1); vec.k += 1
            if gain is None:
                done(tt(row[0:2], row[0:2], bias, ALU.add))
            else:
                done(stt(row[0:2], row[0:2], 1.0, bias, ALU.add, ALU.add))
                done(tt(row, row, gain[:, 512 * (n % 2):512 * (n % 2) + 512], ALU.mult))
            dve.sem_inc(mod_ready, 1)

        def modulate(_):
            def scaled(t):
                ts(XN[:, t % 2, :], X[:, t, :], small[:, 16 + t:17 + t], None, ALU.mult).then_inc(xn_ready, 1)

            dve.wait_ge(rows_in, 48)
            for n in range(4):
                if n >= 2:
                    dve.wait_ge(full_a, n - 1)
                mod_row(n, modrow[:, n % 2, :], bias_row[:, n, :], gain_row if n >= 2 else None)
                if n == 0:
                    dve.wait_ge(sq_ready, 1)
                    done(ts(small[:, 8:8 + NT], small[:, 0:NT], 1.0 / D, EPS, ALU.mult, ALU.add))
                    rsqrt(small[:, 16:16 + NT], small[:, 8:8 + NT], small[:, 24:24 + NT])
                    scaled(0)
                for t in TILES_AFTER_ROW[n]:
                    if t + 1 < NT:
                        scaled(t + 1)
                    for half in range(2):
                        src = vec.take(dve)
                        vec.give(cp(HT[:, 4 * half:4 * half + 4, P * t:P * t + P], src.rearrange("p (a b) -> p a b", a=4)))
            dve.wait_ge(free_d, vec.k)
            dve.sem_inc(turned_in, 1)
            dve.wait_ge(bc_ready, 1)
            for s, cols in enumerate((slice(0, SAMPLE), slice(SAMPLE, T))):
                for k in range(5):
                    going(ts(HT[:, k, cols], HT[:, k, cols], MODC[:, 1, k, s:s + 1], MODC[:, 0, k, s:s + 1], ALU.mult, ALU.add))
            dve.wait_ge(dve_step, steps_so_far())
            dve.sem_inc(modulated, 1)

        def params(hf):
            dve.wait_ge(par_in, 16 * PARS * (hf + 1))
            for d in range(2):
                done(cp(NATS[hf][:, 4 + d, :].rearrange("g (h p) -> g h p", h=2),
                        LDS[hf][:, d, :].unsqueeze(2).broadcast_to([GPH, 2, PS])))
            dve.sem_inc(nat_ready, 1)
            src = vec.take(dve)
            done(cp(PAR.rearrange("p a b -> p (a b)"), src[:, 0:10 * GPH]))
            dve.sem_inc(free_d, 1); vec.k += 1
            for j in range(2):
                src = vec.take(dve)
                vec.give(cp(CT[:, j], src[:, 0:16 * GPH].rearrange("p (a b) -> p a b", a=GPH)))
            dve.wait_ge(free_d, vec.k)
            par = lambda n: PAR[:, n:n + 2, :]
            are, aim, ldt = par(0), par(2), par(4)
            step_, re, im, mag, t1, t2 = SC_[0], SC_[1], SC_[2], SC_[6], SC_[7], SC_[8]
            exact_exp(step_, ldt, t1, t2, SCI)
            done(tt(re, are, step_, ALU.mult))
            done(tt(im, aim, step_, ALU.mult))
            exact_exp(mag, re, t1, t2, SCI)
            ang = SC_[3]
            done(ts(t1, im, float(1 / (2 * np.pi)), MAGIC, ALU.mult, ALU.add))
            done(ts(t1, t1, -MAGIC, None, ALU.add))
            done(stt(ang, t1, -TWO_PI_A, im, ALU.mult, ALU.add))
            done(stt(ang, t1, -TWO_PI_B, ang, ALU.mult, ALU.add))
            done(stt(ang, t1, -TWO_PI_C, ang, ALU.mult, ALU.add))
            ts(ang, ang, 3.1415925, -3.1415925, ALU.min, ALU.max).then_inc(ang_ready, 1)
            dve.wait_ge(sin_ready, hf + 1)
            sin, cos, half_sin = SC_[4], SC_[9], SC_[5]
            done(tt(cos, half_sin, half_sin, ALU.mult))
            done(ts(cos, cos, -2.0, 1.0, ALU.mult, ALU.add))
            done(V_.memset(PW[:, 0, :, 0, :], 1.0))
            done(V_.memset(PW[:, 1, :, 0, :], 0.0))
            done(tt(PW[:, 0, :, 1, :], mag, cos, ALU.mult))
            done(tt(PW[:, 1, :, 1, :], mag, sin, ALU.mult))
            for m in (1, 2, 4):
                b = [PW[:, j, :, m, :].unsqueeze(2).broadcast_to([P, 2, m, GPH]) for j in range(2)]
                t = PWT[:, 0:2 * m * GPH].rearrange("p (a b c) -> p a b c", a=2, b=m)
                cmul(PW[:, 0, :, m + 1:2 * m + 1, :], PW[:, 1, :, m + 1:2 * m + 1, :],
                     PW[:, 0, :, 1:m + 1, :], PW[:, 1, :, 1:m + 1, :], b[0], b[1], t)
            nre, den, qre, qim = SC_[10], SC_[11], SC_[12], SC_[13]
            done(ts(nre, PW[:, 0, :, 1, :], -1.0, None, ALU.add))
            done(tt(den, are, are, ALU.mult))
            done(tt(t1, aim, aim, ALU.mult))
            done(tt(den, den, t1, ALU.add))
            done(V_.reciprocal(den, den))
            nim = PW[:, 1, :, 1, :]
            done(tt(qre, nre, are, ALU.mult))
            done(tt(t1, nim, aim, ALU.mult))
            done(tt(qre, qre, t1, ALU.add))
            done(tt(qre, qre, den, ALU.mult))
            done(tt(qim, nim, are, ALU.mult))
            done(tt(t1, nre, aim, ALU.mult))
            done(tt(qim, qim, t1, ALU.subtract))
            done(tt(qim, qim, den, ALU.mult))
            for d in range(2):
                bc = lambda x: x[:, d, :].unsqueeze(2).broadcast_to([P, GPH, GI])
                cmul(BB[:, d, 0], BB[:, d, 1], bc(qre), bc(qim), BNS[hf][:, 0], BNS[hf][:, 1], BBT)
            ure, uim, vre, vim, m8 = SC_[10], SC_[11], SC_[12], SC_[13], SC_[14]
            cmul(ure, uim, cos, sin, cos, sin, t1)
            cmul(vre, vim, ure, uim, ure, uim, t1)
            cmul(SC_[15], SC_[16], vre, vim, vre, vim, t1)
            done(tt(m8, mag, mag, ALU.mult))
            done(tt(m8, m8, m8, ALU.mult))
            done(tt(m8, m8, m8, ALU.mult))

        def turn_F(hf):
            for d in range(2):
                pw = [PW[:, j, d, 0:Q, :].rearrange("p k g -> p g k") for j in range(2)]
                if d == 0:
                    pw = [x[:, :, ::-1] for x in pw]
                pw = [x.unsqueeze(3).broadcast_to([P, GPH, Q, GI]) for x in pw]
                bb = [BB[:, d, j].unsqueeze(2).broadcast_to([P, GPH, Q, GI]) for j in range(2)]
                if d == 1:
                    dve.wait_ge(f_done, 2 * hf + 1)
                cmul(FP[0], FP[1], pw[0], pw[1], bb[0], bb[1], FPT)
                dve.sem_inc(f_ready, 1)

        def lag_kernels(hf):
            dve.wait_ge(f_done, 2 * hf + 2)
            if hf:
                dve.wait_ge(state_out, 64)
            for d in range(2):
                pw = [PW[:, j, d].rearrange("p k g -> p g k").unsqueeze(3).broadcast_to([P, GPH, 9, GI]) for j in range(2)]
                ct = [CT[:, j].unsqueeze(2).broadcast_to([P, GPH, 9, GI]) for j in range(2)]
                done(tt(CTMP, ct[1], pw[1], ALU.mult))
                done(tt(CPW[:, d, 0], ct[0], pw[0], ALU.mult))
                done(tt(CPW[:, d, 0], CPW[:, d, 0], CTMP, ALU.subtract))
                done(tt(CTMP, ct[0], pw[1], ALU.mult))
                done(tt(CPW[:, d, 1], ct[1], pw[0], ALU.mult))
                fl = lambda x: x.rearrange("p a b c -> p (a b c)")
                done(stt(fl(CPW[:, d, 1]), fl(CPW[:, d, 1]), -1.0, fl(CTMP), ALU.mult, ALU.subtract))
            dve.sem_inc(cpw_ready, 1)
            for d in range(2):
                for q in range(4):
                    src = vec.take(dve)[0:GI].rearrange("i (g k o) -> i g k o", g=4, k=Q)
                    gs = slice(8 * (q // 2) + q % 2, 8 * (q // 2) + 8, 2)
                    if d == 0:
                        vec.give(cp(KP[:, gs, 7:15, :], src))
                    else:
                        if q == 0:
                            dve.wait_ge(free_d, vec.k)
                        done(cp(KP[:, gs, 0:7, :], src[:, :, 7:0:-1, :]))
                        vec.give(tt(KP[:, gs, 7, :], KP[:, gs, 7, :], src[:, :, 0, :], ALU.add))
            dve.wait_ge(free_d, vec.k)
            done(tt(DG, DTS[hf].unsqueeze(2).broadcast_to([GI, GH_, GI]),
                    ident[0:GI, 0:GI].unsqueeze(1).broadcast_to([GI, GH_, GI]), ALU.mult))
            tt(KP[:, :, 7, :], KP[:, :, 7, :], DG, ALU.add).then_inc(kp_ready, 1)

        def turn_U(hf):
            dve.wait_ge(sraw_in, 16 * (hf + 1))
            dve.wait_ge(kp_ready, hf + 1)
            cp(S[0:NC, :].rearrange("c (g s i) -> c s g i", g=GH_, s=Q), SRAW).then_inc(s_chunks, 1)
            dve.wait_ge(s_chunks, hf + 1)

        def chunk_inputs(hf):
            dve.wait_ge(toe_in, 16 * Q * (hf + 1))
            done(V_.memset(V[:, :, :, :, CS + 1].rearrange("p a b c -> p (a b) c"), 0.0))
            for d in range(2):
                for c in range(2):
                    done(cp(V[:, d, c, :, 0], PAR[:, 6 + 2 * c + d, :]))
            for d in range(2):
                for c in range(2):
                    for q in range(2):
                        n = min(6, GPH - 6 * q)
                        src = vec.take(dve)[:, 0:NC * n].rearrange("p (a b) -> p a b", a=n)
                        lat, con = src[:, :, 0:CS], src[:, :, CS:NC]
                        if d:
                            lat, con = lat[:, :, ::-1], con[:, :, ::-1]
                        done(cp(V[:, d, c, 6 * q:6 * q + n, 1:CS + 1], lat))
                        vec.give(cp(V[:, d, c, 6 * q:6 * q + n, CS + 2:SC], con))
            dve.wait_ge(free_d, vec.k)
            v3 = lambda x: x.rearrange("p (a b) -> p a b", b=SC)
            parts = ((slice(0, CS + 1), slice(0, CS + 1)), (slice(CS + 1, SC), slice(0, CP_ + 1)))
            for d in range(2):
                rot = [RT[:, j] for j in range(2)]
                for j in range(2):
                    going(V_.memset(rot[j][:, :, 0], 1.0 - j))
                    done(cp(rot[j][:, :, 1], SC_[15 + j][:, d, :]))
                for m in (1, 2, 4, 8, 16, 32):
                    b = [x[:, :, m:m + 1].broadcast_to([P, GPH, m]) for x in rot]
                    cmul(rot[0][:, :, m + 1:2 * m + 1], rot[1][:, :, m + 1:2 * m + 1],
                         rot[0][:, :, 1:m + 1], rot[1][:, :, 1:m + 1], b[0], b[1],
                         RTT[:, 0:m * GPH].rearrange("p (a b) -> p a b", b=m))
                done(cp(A8, SC_[14][:, d, :].unsqueeze(2).broadcast_to([P, GPH, SC])))
                going(V_.memset(A8[:, :, 0], 0.0))
                done(V_.memset(A8[:, :, CS + 1], 0.0))
                vr, vi = V[:, d, 0], V[:, d, 1]
                for cols, k in parts:
                    for dst, r_, x in ((0, 0, vr), (1, 1, vi), (2, 0, vi), (3, 1, vr)):
                        going(tt(v3(TMP4[dst])[:, :, cols], rot[r_][:, :, k], x[:, :, cols], ALU.mult))
                dve.wait_ge(dve_step, steps_so_far())
                fl = lambda x: x.rearrange("p a b -> p (a b)")
                going(tt(fl(vr), TMP4[0], TMP4[1], ALU.add))
                done(tt(fl(vi), TMP4[2], TMP4[3], ALU.subtract))
                for j, x in enumerate((vr, vi)):
                    going(V_.tensor_tensor_scan(Z[j], fl(A8), fl(x), 0.0, ALU.mult, ALU.add))
                dve.wait_ge(dve_step, steps_so_far())
                for cols, k in parts:
                    for dst, r_, x in ((0, 0, 0), (1, 1, 1), (2, 0, 1), (3, 1, 0)):
                        going(tt(v3(TMP4[dst])[:, :, cols], rot[r_][:, :, k], v3(Z[x])[:, :, cols], ALU.mult))
                dve.wait_ge(dve_step, steps_so_far())
                for j, (x, y, op) in enumerate(((0, 1, ALU.subtract), (2, 3, ALU.add))):
                    xin = fl(V[:, d, j])[:, 0:GPH * NC].rearrange("p (a b) -> p a b", b=NC)
                    for out, cols in ((xin[:, :, 0:CS], slice(0, CS)), (xin[:, :, CS:NC], slice(CS + 1, CS + 1 + CP_))):
                        if d:
                            out = out[:, :, ::-1]
                        going(tt(out, v3(TMP4[x])[:, :, cols], v3(TMP4[y])[:, :, cols], op))
                    done(tt(SF[:, j, d, :], v3(TMP4[x])[:, :, SC - 1], v3(TMP4[y])[:, :, SC - 1], op))
            dve.sem_inc(xi_ready, 1)

        def chunk_outputs(hf):
            src = vec.take(dve)
            vec.give(cp(SFO.rearrange("p a b -> p (a b)"), src[0:GPH, :]))
            dve.wait_ge(free_d, vec.k)
            dve.sem_inc(sf_ready, 1)

        none = lambda hf: None
        steps = dict(params=params, modulate=modulate, su=none, F=turn_F, K=lag_kernels, U=turn_U, V=chunk_inputs, Y=chunk_outputs,
                     out=none)
        for step in ORDER:
            if not isinstance(step, int):
                steps[step[0]](step[1])
        phase_end(dve, 0)
        if STOP <= 0:
            return

        for t in range(NT):
            src = vec.take(dve)
            vec.give(cp(RKT[:, :, P * t:P * t + P], src.rearrange("p (a b) -> p a b", a=4)))
        dve.wait_ge(ret_in, 16 * 8)
        dve.wait_ge(ret_exp, 1)
        for d in range(2):
            done(tt(QX[:, 0, d], QX[:, 0, d], MASK[:, d, :].unsqueeze(1).broadcast_to([P, RH, P]), ALU.mult))
        done(tt(DEC, QX[:, 0, 0], QX[:, 0, 1], ALU.add))
        r3 = lambda x: x.rearrange("p (h e) -> p h e", h=RH)
        for d, t in KV_ORDER:
            src = vec.take(dve)
            if t == NS:
                done(cp(KVO[:, d, :], src))
                dve.sem_inc(kvo_ready, 1)
            else:
                nxt = t + 1 if d == 0 else t - 1
                for h in range(RH):
                    hs = slice(P * h, P * h + P)
                    done(stt(ST[:, d, nxt, hs], ST[:, d, t, hs], CD[:, d, h:h + 1], src[:, hs], ALU.mult, ALU.add))
            dve.sem_inc(free_d, 1); vec.k += 1
            dve.sem_inc(kv_done, 1)
        for t in range(NT):
            if t >= 2:
                dve.wait_ge(full_a, FULL_A_BEFORE_RET + t - 1)
            if t < NS:
                for d in range(2):
                    done(tt(QX[:, t % 2, d], RQT[:, :, P * t:P * t + P], XI[:, d], ALU.mult))
            src = vec.take(dve)
            done(tt(r3(SS[:, t % 2, :]), r3(src), DEC, ALU.mult))
            dve.sem_inc(free_d, 1); vec.k += 1
            dve.sem_inc(sd_ready, 1)
        dve.wait_ge(rss_ready, 1)
        done(ts(RSS[:, 0, :], RSS[:, 0, :], 1.0 / P, EPS, ALU.mult, ALU.add))
        rsqrt(RSS[:, 1, :], RSS[:, 0, :], RSS[:, 2, :])
        for t in range(NT):
            o = OALL[:, t, :]
            done(tt(r3(o), r3(o), RSS[:, 1, RH * t:RH * t + RH].unsqueeze(2).broadcast_to([P, RH, P]), ALU.mult))
            dve.wait_ge(gated, t + 1)
            tt(o, o, RG[:, t, :], ALU.mult).then_inc(ro_ready, 1)
        dve.wait_ge(ro_ready, NT)
        phase_end(dve, 1)
        if STOP <= 1:
            return

        NH = AH + KVH
        h3 = lambda x: x.rearrange("p (h e) -> p h e", e=HD)
        for t in range(NT):
            done(tt(QT1, AQK[:, t, :], AQK[:, t, :], ALU.mult))
            done(V_.tensor_reduce(QSS[:, 0, NH * t:NH * t + NH], h3(QT1), AX.X, ALU.add))
        done(ts(QSS[:, 0, :], QSS[:, 0, :], 1.0 / HD, EPS, ALU.mult, ALU.add))
        rsqrt(QSS[:, 1, :], QSS[:, 0, :], QSS[:, 2, :])
        dve.wait_ge(att_in, 16 * 5)
        done(cp(QG[:, 0:AH, :], QGL[:, 0:1, :].broadcast_to([P, AH, HD])))
        done(cp(QG[:, AH:NH, :], QGL[:, 1:2, :].broadcast_to([P, KVH, HD])))
        for t in range(NT):
            x, rs = AQK[:, t, :], QSS[:, 1, NH * t:NH * t + NH]
            swap = lambda v: v.rearrange("p (h b) -> p h b", h=2)
            done(tt(QT1[:, 0:512].rearrange("p (b h e) -> p h b e", b=4, h=2), x[:, 0:512].rearrange("p (h b e) -> p h b e", h=2, b=4),
                    swap(rs[:, 0:AH]).unsqueeze(3).broadcast_to([P, 2, 4, HD]), ALU.mult))
            done(tt(h3(QT1[:, 512:640]), h3(x[:, 512:640]), rs[:, AH:NH].unsqueeze(2).broadcast_to([P, KVH, HD]), ALU.mult))
            if t == NS:
                done(tt(h3(x), h3(QT1), QG, ALU.mult))
                break
            done(tt(h3(QT1), h3(QT1), QG, ALU.mult))
            pairs = lambda v: v.rearrange("p (h e two) -> p h e two", two=2, e=HD // 2)
            cos, sn = (ROPE[:, j, t, :] for j in range(2))
            done(tt(h3(x), h3(QT1), cos.unsqueeze(1).broadcast_to([P, NH, HD]), ALU.mult))
            for j in range(2):
                s_ = sn.rearrange("p (e two) -> p e two", two=2)[:, :, j].unsqueeze(1).broadcast_to([P, NH, HD // 2])
                done(tt(pairs(QT2)[:, :, :, j], pairs(QT1)[:, :, :, 1 - j], s_, ALU.mult))
            done(tt(x, x, QT2, ALU.add))
        dve.sem_inc(qk_ready, 1)
        dve.sem_inc(kv_out, 1)
        src = vec.take(dve)
        vec.give(cp(KTT[:, 0:512], src))
        src = vec.take(dve)
        done(cp(KTT[:, 512:640], src[:, 0:P]))
        vec.give(cp(KTP, src[:, P:2 * P]))
        dve.wait_ge(free_d, vec.k)
        flat = banks[:].rearrange("p b c -> p (b c)")
        NU = 8 * NT

        def top(i):
            t, half = i // 8, i % 2
            n = KEYS if t < NS else P
            dve.wait_ge(s_full, i + 1)
            if i >= 4:
                dve.wait_ge(p_ready, i - 3)
            V_.tensor_reduce(AMAX[:, i % 4:i % 4 + 1], flat[:, 1024 * half:1024 * half + n], AX.X, ALU.max,
                             negate=True).then_inc(s_max, 1)

        def copy_turned(i):
            n = KEYS if i // 8 < NS else P
            dve.wait_ge(pt_full, i + 1)
            if i >= 2:
                dve.wait_ge(o_full, i - 1)
            cp(PT[:, i % 2, 0:n], flat[:, 2048:2048 + n]).then_inc(pt_ready, 1)

        def rows_out(t):
            dve.wait_ge(o_full, 8 * t + 8)
            done(V_.reciprocal(ASUM[:, t, :], ASUM[:, t, :]))
            if t >= 2:
                dve.wait_ge(aot_full, t - 1)
            tt(h3(AO[:, t % 2, :]), h3(banks[:, 6, :]), ASUM[:, t, :].unsqueeze(2).broadcast_to([P, AH, HD]),
               ALU.mult).then_inc(ao_ready, 1)

        def columns_out(t):
            dve.wait_ge(aot_full, t + 1)
            cp(ATT[:, :, P * t:P * t + P], banks[:, 4, :].rearrange("p (a b) -> p a b", a=4)).then_inc(aot_ready, 1)

        top(0)
        for i in range(NU):
            if i + 1 < NU:
                top(i + 1)
            copy_turned(i)
            if i % 8 == 0 and i:
                rows_out(i // 8 - 1)
            if i % 8 == 2 and i > 8:
                columns_out(i // 8 - 1)
        rows_out(NT - 1)
        columns_out(NT - 1)
        dve.wait_ge(aot_ready, NT)
        phase_end(dve, 2)
        if STOP <= 2:
            return

        for n in range(2):
            ns = slice(512 * n, 512 * n + 512)
            for branch in range(3):
                for t in range(NT):
                    dst, tg = MER[:, t, ns], TG[3 * n + branch][:, t, :]
                    src = vec.take(dve)
                    if branch == 0:
                        vec.give(stt(dst, tg, 1.0, src, ALU.add, ALU.mult))
                        continue
                    mt = MT2[:, t % 2, :]
                    if branch == 1:
                        done(stt(mt, tg, 1.0, src, ALU.add, ALU.mult))
                        dve.sem_inc(free_d, 1); vec.k += 1
                    else:
                        i = NT * n + t
                        done(ts(tg, tg, 0.5, 0.5, ALU.mult, ALU.add))
                        dve.wait_ge(tb_ready, i + 1)
                        done(stt(mt, MT1[:, i % 2, :], 1.0, src, ALU.add, ALU.mult))
                        dve.sem_inc(free_d, 1); vec.k += 1
                        dve.sem_inc(tb_used, 1)
                        done(tt(mt, mt, tg, ALU.mult))
                    if branch == 1 and t == 0:
                        dve.wait_ge(free_d, vec.k)
                    done(tt(dst, dst, mt, ALU.add))
                    if n == 1 and branch == 2:
                        dve.sem_inc(mer_ready, 1)
        for t in range(NT):
            src = vec.take(dve)
            vec.give(ts(MERT[:, 0:4, P * t:P * t + P], src.rearrange("p (a b) -> p a b", a=4), 0.5, None, ALU.mult))
        dve.wait_ge(free_d, vec.k)
        phase_end(dve, 3)
        if STOP <= 3:
            return

        dve.wait_ge(rows_in, 96)
        fa, rows, half = FULL_A_BEFORE_LAST, 0, 0
        for step in LAST_ORDER:
            if step is not None:
                if rows >= 2:
                    dve.wait_ge(full_a, fa + 2 * (rows - 1))
                mod_row(step, modrow2[:, step % 2, :], bias2[:, step - 4, :], gain2 if step in (8, 9) else None)
                rows += 1
                continue
            ns = slice(512 * half, 512 * half + 512)
            half += 1
            dve.wait_ge(bc_ready, 1 + half)
            dve.wait_ge(x2_in, 16 * NT)
            for t in range(NT):
                s = 0 if t < NS else 1
                src = vec.take(dve)
                done(tt(SQ2[:, 0:512], src, BC2[:, 0, s, ns], ALU.mult))
                dve.sem_inc(free_d, 1); vec.k += 1
                done(tt(X2[:, t, ns], X2[:, t, ns], SQ2[:, 0:512], ALU.add))
                if half == 2:
                    dve.sem_inc(x2_ready, 1)
        dve.wait_ge(sq_ready, 2)
        done(ts(small[:, 8:8 + NT], small[:, 0:NT], 1.0 / D, EPS, ALU.mult, ALU.add))
        rsqrt(small[:, 16:16 + NT], small[:, 8:8 + NT], small[:, 24:24 + NT])
        dve.wait_ge(bc_ready, 1 + 8)
        phase_end(dve, 4)
        if STOP <= 4:
            return

        done(V_.memset(ZERO, 0))
        dve.sem_inc(zero_ready, 1)

        def normed(t):
            s = 0 if t < NS else 1
            h = NROWS[:, t, :]
            done(stt(h, X2[:, t, :], small[:, 16 + t:17 + t], BC2[:, 2, s, :], ALU.mult, ALU.mult))
            tt(h, h, BC2[:, 1, s, :], ALU.add).then_inc(h2_ready, 1)

        def columns_in(t):
            src = vec.take(dve)
            vec.give(cp(COLS2[:, t % 2, 0:4, :], src.rearrange("p (a b) -> p a b", a=4)))

        def logits(t):
            src = vec.take(dve)
            vec.give(tt(LOGIT[:, t, :], src[:, 0:NE], BR, ALU.add))

        normed(0)
        normed(1)
        columns_in(0)
        dve.wait_ge(route_in, 64)
        for t in range(1, NT):
            if t + 1 < NT:
                normed(t + 1)
            columns_in(t)
            logits(t - 1)
        logits(NT - 1)
        dve.wait_ge(free_d, vec.k)
        c = lambda j: ROUTE[:, j, :]
        over = lambda x, n: x.unsqueeze(2).broadcast_to([P, NT, n])
        red = lambda out, x, op: done(V_.tensor_reduce(out, x, AX.X, op))
        red(c(0), LOGIT, ALU.max)
        done(tt(LOGIT, LOGIT, over(c(0), NE), ALU.subtract))
        dve.sem_inc(exp_ready, 1)
        dve.wait_ge(exp_ready, 2)
        red(c(0), PROB, ALU.add)
        done(V_.reciprocal(c(0), c(0)))
        done(tt(PROB, PROB, over(c(0), NE), ALU.mult))
        p4 = PROB.rearrange("p t (g e) -> p t g e", e=EG)
        for j, (x, y, op) in enumerate(((0, 1, ALU.max), (0, 1, ALU.min), (2, 3, ALU.max), (2, 3, ALU.min))):
            done(tt(GH[j], p4[:, :, :, x], p4[:, :, :, y], op))
        done(tt(GH[4], GH[0], GH[2], ALU.max))
        done(tt(GH[5], GH[0], GH[2], ALU.min))
        done(tt(GH[6], GH[1], GH[3], ALU.max))
        done(tt(GH[5], GH[5], GH[6], ALU.max))
        done(tt(GH[4], GH[4], GH[5], ALU.add))

        def first_largest(onehot, index, value, x, n, tmp):
            it = IOTA[:, 0:n].unsqueeze(1).broadcast_to([P, NT, n])
            red(value, x, ALU.max)
            done(tt(tmp, x, over(value, n), ALU.is_equal))
            done(ts(tmp, tmp, -99.0, 99.0, ALU.mult, ALU.add))
            done(tt(tmp, tmp, it, ALU.add))
            red(index, tmp, ALU.min)
            done(tt(onehot, it, over(index, n), ALU.is_equal))

        first_largest(GH[7], c(0), c(1), GH[4], NG, GH[0])
        g16 = GH[7].unsqueeze(3).broadcast_to([P, NT, NG, EG])
        t4 = lambda x: x.rearrange("p t (g e) -> p t g e", e=EG)
        done(tt(t4(PROB), t4(PROB), g16, ALU.mult))
        done(tt(t4(PROB), t4(PROB), g16, ALU.add))
        done(ts(PROB, PROB, -1.0, None, ALU.add))
        E1, E2, V1, V2, R1, R2, W1, W2 = (c(j) for j in range(2, 10))
        first_largest(M1, E1, V1, PROB, NE, EQ)
        done(stt(PROB.rearrange("p t e -> p (t e)"), M1.rearrange("p t e -> p (t e)"), -3.0, PROB.rearrange("p t e -> p (t e)"), ALU.mult, ALU.add))
        first_largest(M2, E2, V2, PROB, NE, EQ)
        done(tt(MB, M1, M2, ALU.add))
        dve.sem_inc(masks_ready, 1)
        done(tt(c(0), V1, V2, ALU.add))
        done(V_.reciprocal(c(0), c(0)))
        for w_, v in ((W1, V1), (W2, V2)):
            done(tt(w_, v, c(0), ALU.mult))
            done(ts(w_, w_, 0.5, None, ALU.mult))
        src = vec.take(dve)
        done(cp(PROB, src[:, NT * NE:2 * NT * NE].rearrange("p (t e) -> p t e", t=NT)))
        for t in range(1, NT):
            done(tt(PROB[:, t, :], PROB[:, t, :], PROB[:, t - 1, :], ALU.add))
        done(cp(RANK, src[:, 0:NT * NE].rearrange("p (t e) -> p t e", t=NT)))
        done(tt(RANK[:, 1:NT, :], RANK[:, 1:NT, :], PROB[:, 0:NT - 1, :], ALU.add))
        red(c(0)[:, 0:1], PROB[:, NT - 1, :], ALU.max)
        done(cp(TOP_COUNT, c(0)[:, 0:1]))
        dve.sem_inc(free_d, 1); vec.k += 1
        for k, (m_, rk, e_) in enumerate(((M1, R1, E1), (M2, R2, E2))):
            done(tt(EQ, m_, RANK, ALU.mult))
            red(rk, EQ, ALU.add)
            done(stt(CIDX[:, :, k], e_, float(T), rk, ALU.mult, ALU.add))
        dve.sem_inc(pos_ready, 1)
        phase_end(dve, 5)
        if STOP <= 5:
            return

        def dve_end(n, m, e, b):
            dve.wait_ge(dn0, n + 1)
            at_least(dve, out_wr[b], 16 * m)
            cp(OUT[:, b, 0:512], banks[:, 5, :]).then_inc(out_d, 1)

        def dve_begin(n, m, e, b, before):
            dve.wait_ge(g_t, n + 1)
            at_least(dve, up_full, n - 1)
            cp(COLS2[:, b, 0:4, :], banks[:, 0, :].rearrange("p (a b) -> p a b", a=4)).then_inc(gt_d, 1)
            if before:
                before()
            dve.wait_ge(th_ready, n + 1)
            at_least(dve, ht_full, n - 1)
            stt(HID[:, b, :], TH, 1.0, banks[:, 2, :], ALU.add, ALU.mult).then_inc(hid_step, 1)
            dve.wait_ge(hid_step, n + 1)
            dve.wait_ge(up_full, n + 1)
            tt(HID[:, b, :], HID[:, b, :], banks[:, 3, :], ALU.mult).then_inc(hid_ready, 1)

        def dve_pass(r):
            if not isinstance(r, int):
                dve.wait_ge(combined, NT * r)
            expert_pipeline(dve, r, dve_begin, dve_end)
            k = [0]

            def step(ins):
                k[0] += 1
                ins.then_inc(comb_step, 1)
                dve.wait_ge(comb_step, COMB_STEPS * r + k[0])

            lo = ROUTE[:, 10, :]
            for j, (rk, e_, w_) in enumerate(((R1, E1, W1), (R2, E2, W2))):
                if isinstance(r, int):
                    step(ts(lo, rk, 0.0, None, ALU.add))
                else:
                    step(ts(rk, rk, -float(CAP), None, ALU.add))
                    step(ts(lo, rk, 0.0, None, ALU.add))
                step(ts(ROUTE[:, 11, :], lo, 0.0, None, ALU.is_ge))
                step(ts(ROUTE[:, 12, :], lo, CAP - 0.5, None, ALU.is_lt))
                step(tt(ROUTE[:, 11, :], ROUTE[:, 11, :], ROUTE[:, 12, :], ALU.mult))
                step(tt(ROUTE[:, 11, :], ROUTE[:, 11, :], w_, ALU.mult))
                step(cp(WP[:, j, :], ROUTE[:, 11, :]))
                step(ts(lo, lo, 0.0, CAP - 1.0, ALU.max, ALU.min))
                step(stt(CIDX[:, :, j], e_, float(CAP), lo, ALU.mult, ALU.add))
                if isinstance(r, int):
                    step(cp(ROUTE[:, 12, :], lo))
            dve.sem_inc(cidx_ready, 1)
            for t in range(NT):
                s = 0 if t < NS else 1
                dve.wait_ge(scaled_y, NT * r + t + 1)
                y = [YR[:, t, j, :] for j in range(2)]
                step(stt(y[0], y[1], WP[:, 1, t:t + 1], y[0], ALU.mult, ALU.add))
                step(tt(y[0], y[0], BC2[:, 3, s, :], ALU.mult))
                step(tt(X2[:, t, :], X2[:, t, :], y[0], ALU.add))
                dve.sem_inc(combined, 1)
            assert k[0] == COMB_STEPS

        all_passes(dve, dve_pass)
        phase_end(dve, 6)
        if STOP <= 6:
            return
        dve.wait_ge(fin_in, 16)
        done(ts(small[:, 8:8 + NT], small[:, 0:NT], 1.0 / D, EPS, ALU.mult, ALU.add))
        rsqrt(small[:, 16:16 + NT], small[:, 8:8 + NT], small[:, 24:24 + NT])
        for t in range(NT):
            stt(X2[:, t, :], X2[:, t, :], small[:, 16 + t:17 + t], FG, ALU.mult, ALU.mult).then_inc(fin_ready, 1)

    @block.gpsimd
    def _(pool):
        n_out = 0
        pair = lambda x: x.rearrange("(g h) p -> g (h p)", h=2)
        def parameters_in(hf):
            gps = slice(GPH * hf, GPH * hf + GPH)
            NAT, CNAT, LD, BN = NATS[hf], CNATS[hf], LDS[hf], BNS[hf]
            for d, (re, im, ld) in enumerate((("a_re_f", "a_im_f", "log_dt_f"), ("a_re_b", "a_im_b", "log_dt_b"))):
                pool.dma_start(NAT[:, d, :], pair(a[re][0])[gps]).then_inc(par_in, 16)
                pool.dma_start(NAT[:, 2 + d, :], pair(a[im][0])[gps]).then_inc(par_in, 16)
                pool.dma_start(LD[:, d, :], a[ld][0].rearrange("(g h) -> g h", h=2)[gps]).then_inc(par_in, 16)
                pool.dma_start(NAT[:, 6 + d, :], pair(a["state_ssm_re"][0, 0, d])[gps]).then_inc(par_in, 16)
                pool.dma_start(NAT[:, 8 + d, :], pair(a["state_ssm_im"][0, 0, d])[gps]).then_inc(par_in, 16)
            for j, (b, c) in enumerate((("ssm_b_re", "ssm_c_re"), ("ssm_b_im", "ssm_c_im"))):
                for h in range(2):
                    pool.dma_start(BN[64 * h:64 * h + 64, j],
                                   a[b][0].rearrange("(g h) p i -> h p g i", h=2)[h][:, gps]).then_inc(par_in, 16)
                pool.dma_start(CNAT[:, j], a[c][0].rearrange("g o p -> o g p")[:, GH_ * hf:GH_ * hf + GH_]).then_inc(par_in, 16)
            pool.dma_start(DTS[hf], a["ssm_d"].rearrange("o (g i) -> i (o g)", i=GI)[:, GH_ * hf:GH_ * hf + GH_],
                           allow_slow_non_contiguous=True).then_inc(par_in, 16)

        parameters_in(0)
        pool.wait_ge(par_in, 16 * PARS)
        for hf in range(2):
            gps = slice(GPH * hf, GPH * hf + GPH)
            if hf == 0:
                for t in range(NT):
                    pool.wait_ge(scr, t + 1)
                    pool.dma_start(scratch_su[P * t:P * (t + 1), :], SU[:, t, :]).then_inc(su_out, 16)
                pool.wait_ge(su_out, 16 * NT)
            else:
                pool.wait_ge(s_chunks, 1)
            pool.dma_start(SRAW.rearrange("c s g i -> c s (g i)"),
                           scratch_su.rearrange("(c s) f -> c s f", s=Q)[:, :, 256 * hf:256 * hf + 256]).then_inc(sraw_in, 16)
            if hf == 0:
                parameters_in(1)
            pool.wait_ge(kp_ready, hf + 1)
            pool.wait_ge(kp_ready, hf + 1)
            for s in range(Q):
                pool.dma_start(TOE[16 * s:16 * s + 16, :, :],
                               KP[:, :, 7 - s:15 - s, :].rearrange("i g t o -> i g (t o)")).then_inc(toe_in, 16)
            pool.wait_ge(toe_in, 16 * Q * (hf + 1))
            pool.wait_ge(sf_ready, hf + 1)
            for j, name in enumerate(("new_re", "new_im")):
                for d in range(2):
                    pool.dma_start(pair(a[name][0, 0, d])[gps], SFO[:, 2 * j + d, :]).then_inc(state_out, 16)
            pool.wait_ge(state_out, 64 * (hf + 1))
        phase_end(pool, 0)
        if STOP <= 0:
            return
        for d, name in enumerate(("ret_lg_f", "ret_lg_b")):
            pool.dma_start(LG[:, d, :], a[name].broadcast_to([P, RH])).then_inc(ret_in, 16)
            pool.dma_start(ST[:, d, 3 * d, :].rearrange("p (h e) -> p h e", h=RH),
                           a["state_ret"][0, 0, d].rearrange("h p e -> p h e")).then_inc(ret_in, 16)
        pool.dma_start(RNG, a["ret_norm_g"].broadcast_to([P, RW])).then_inc(ret_in, 16)
        pool.dma_start(DIST, a["k_dist"]).then_inc(ret_in, 16)
        pool.dma_start(MASK, a["k_mask"]).then_inc(ret_in, 16)
        pool.dma_start(ZPOS, a["k_zpos"]).then_inc(ret_in, 16)
        for d in range(2):
            pool.wait_ge(kvo_ready, d + 1)
            pool.dma_start(a["new_ret"][0, 0, d].rearrange("h p e -> p h e"),
                           KVO[:, d, :].rearrange("p (h e) -> p h e", h=RH)).then_inc(state_out, 16)
        pool.wait_ge(ret_in, 16 * 8)
        for t in range(NT):
            pool.wait_ge(ro_gate, t + 1)
            tanh, gate = VZ[:, t % 3, :], RG[:, t, :]
            nc.gpsimd.tensor_tensor(tanh, tanh, gate, ALU.mult).then_inc(gate_step, 1)
            pool.wait_ge(gate_step, 2 * t + 1)
            nc.gpsimd.tensor_tensor(gate, gate, tanh, ALU.add).then_inc(gate_step, 1)
            pool.wait_ge(gate_step, 2 * t + 2)
            nc.gpsimd.tensor_tensor(gate, gate, RNG, ALU.mult).then_inc(gated, 1)
        pool.wait_ge(state_out, 128 + 32)
        phase_end(pool, 1)
        if STOP <= 1:
            return
        pool.dma_start(CK, a["cache_attn_k"][0, 0].rearrange("t h d -> t (h d)")).then_inc(att_in, 16)
        pool.dma_start(CV, a["cache_attn_v"][0, 0].rearrange("t h d -> t (h d)")).then_inc(att_in, 16)
        pool.dma_start(ROPE, a["k_rope"]).then_inc(att_in, 16)
        pool.dma_start(QGL[:, 0, :], a["att_q_norm_g"].broadcast_to([P, HD])).then_inc(att_in, 16)
        pool.dma_start(QGL[:, 1, :], a["att_k_norm_g"].broadcast_to([P, HD])).then_inc(att_in, 16)
        pool.wait_ge(kv_out, 1)
        pool.dma_start(a["new_k"][0, 0].rearrange("t h d -> t (h d)"), AQK[:, NS, AH * HD:]).then_inc(state_out, 16)
        pool.dma_start(a["new_v"][0, 0].rearrange("t h d -> t (h d)"), AV[:, NS, :]).then_inc(state_out, 16)
        pool.wait_ge(state_out, 128 + 64)
        for n in range(2, 5):
            phase_end(pool, n)
            if STOP <= n:
                return
        nc.gpsimd.memset(PACE[:, 0:1], 0.0).then_inc(pool_step, 1)
        pool.wait_ge(pool_step, 1)
        pool.wait_ge(zero_ready, 1)
        pool.dma_start(lists.rearrange("(p c) o -> p (c o)", p=P), ZERO).then_inc(zero_out, 16)
        for t in range(NT):
            pool.wait_ge(h2_ready, t + 1)
            pool.dma_start(scratch_h2[P * t:P * t + P, :], NROWS[:, t, :]).then_inc(h2_out, 16)
        pool.wait_ge(h2_out, 16 * NT)
        pool.wait_ge(zero_out, 16)
        pool.wait_ge(pos_ready, 1)
        pool.wait_ge(route_in, 64)
        for t in range(NT):
            for k in range(2):
                pool.indirect_dma_start(lists, bass.IndirectOffsetOnAxis(ap=CIDX[:, t, k:k + 1].bitcast(U32), axis=0),
                                        TOK[:, t:t + 1], None).then_inc(pos_out, 16)
        pool.wait_ge(pos_out, 16 * 2 * NT)
        phase_end(pool, 5)
        if STOP <= 5:
            return

        pace = [0]

        def pool_wait(s_, n):
            at_least(pool, s_, n)
            if not isinstance(n, int):
                pace[0] = pace[0] % 26 + 1
                nc.gpsimd.tensor_tensor(PACE[:, pace[0]:pace[0] + 1], PACE[:, 0:1], PACE[:, 0:1], ALU.add).then_inc(pool_step, 1)

        def pool_pass(r):
            pool_wait(idx_in, 32 * r + 32)
            for e in range(NE):
                pool_wait(g_t, 16 * r + e - 1)
                pool.indirect_dma_start(ROWS2[:, e % 2, :], None, scratch_h2,
                                        bass.IndirectOffsetOnAxis(ap=IDX[:, e:e + 1].bitcast(U32), axis=0)).then_inc(g_in[e % 2], 16)
            for b in range(2):
                pool_wait(out_wr[b], 16 * 8 * r + 16 * 8)
            pool_wait(cidx_ready, r + 1)
            for t in range(NT):
                for k in range(2):
                    pool.indirect_dma_start(YR[:, t, k, :], None, scratch_out,
                                            bass.IndirectOffsetOnAxis(ap=CIDX[:, t, k:k + 1].bitcast(U32), axis=0)).then_inc(y_in[t], 16)
            pool_wait(combined, NT * r + NT)
            if not isinstance(r, int):
                pool.wait_ge(pool_step, pace[0] * r + 1)

        all_passes(pool, pool_pass)
        phase_end(pool, 6)

    ctx.close()




def constants():
    k = {}
    k["k_ident"] = np.eye(P, dtype=np.float32)
    k["k_upper"] = np.triu(np.ones((P, P), np.float32), 1)
    s = np.zeros((P, 2, P), np.float32)
    for j in range(4):
        s[32 * j, 0] = s[32 * j + 1, 1] = 1
    k["k_sel"] = s
    k["k_iota"] = np.tile(np.arange(NE, dtype=np.float32), (P, 1))
    k["k_tok"] = np.ascontiguousarray(np.arange(T, dtype=np.int32).reshape(NT, P).T)
    pos = np.arange(P, dtype=np.float32)
    s_, t_ = pos[:, None], pos[None, :]
    k["k_dist"] = np.stack([np.maximum(t_ - s_, 0), np.maximum(s_ - t_, 0), t_ + 1 + 0 * s_, P - t_ + 0 * s_], 1).astype(np.float32)
    k["k_mask"] = np.stack([t_ >= s_, s_ >= t_], 1).astype(np.float32)
    k["k_zpos"] = np.stack([P - 1 - pos, pos], 1).astype(np.float32)
    tok = np.arange(SAMPLE)
    inv = np.float32(10000.0) ** (-np.arange(HD // 4, dtype=np.float32) / np.float32(HD // 4))
    ang = np.concatenate([(tok // 64).astype(np.float32)[:, None] * inv, (tok % 64).astype(np.float32)[:, None] * inv], 1)
    c, s = np.repeat(np.cos(ang), 2, 1), np.repeat(np.sin(ang), 2, 1)
    s[:, 0::2] *= -1
    k["k_rope"] = np.ascontiguousarray(np.stack([c, s]).reshape(2, NS, P, HD).transpose(2, 0, 1, 3)).astype(np.float32)
    return k


_INS = ["x_prompt", "x_sample", "c", "cache_attn_k", "cache_attn_v", "state_ret", "state_ssm_re", "state_ssm_im", "c_ctx",
        "w_ada", "b_ada", "norm1_g", "norm2_g", "w_in", "ret_lg_f", "ret_lg_b", "ret_norm_g", "w_ret_out",
        "att_q_norm_g", "att_k_norm_g", "w_att_out", "a_re_f", "a_im_f", "a_re_b", "a_im_b", "log_dt_f", "log_dt_b",
        "ssm_b_re", "ssm_b_im", "ssm_c_re", "ssm_c_im", "ssm_d", "w_glu", "w_out", "w_router", "b_router",
        "w_gate", "w_up", "w_down", "final_norm_g"]
_OUTS = {"y_prompt": (1, PROMPT, D), "y_sample": (1, SAMPLE, D), "new_k": (1, 1, PROMPT, KVH, HD),
         "new_v": (1, 1, PROMPT, KVH, HD), "new_ret": (1, 1, 2, RH, P, P), "new_re": (1, 1, 2, G, PS), "new_im": (1, 1, 2, G, PS)}


def kernel(**inputs):
    import concourse.bacc as bacc
    from concourse.bass_utils import run_bass_kernel_spmd

    nc = bacc.Bacc("TRN2", target_bir_lowering=False, num_devices=1)
    arrays = {name: np.ascontiguousarray(inputs[name]) for name in _INS}
    arrays.update(constants())
    aps = {name: nc.dram_tensor(name, x.shape, mybir.dt.from_np(x.dtype), kind="ExternalInput").ap() for name, x in arrays.items()}
    for name, shape in _OUTS.items():
        aps[name] = nc.dram_tensor(name, shape, F32, kind="ExternalOutput").ap()
    build(nc, aps)
    got = run_bass_kernel_spmd(nc, [arrays], core_ids=[0]).results[0]
    return tuple(got[name] for name in _OUTS)
```
